# Optimizing a Trainium2 kernel written in Bass

```python
import jax, jax.numpy as jnp
from jax import lax
import numpy as np

D_MODEL = 1024
BATCH = 1
SEQ = 1024
DEPTH = 2

CHUNK = 64
N_LEFT_CHUNKS = 8
BAND = (N_LEFT_CHUNKS + 1) * CHUNK
REL_MAX = 4 * CHUNK
N_REL = REL_MAX + CHUNK
ATT_HEADS = 8
HEAD_DIM = 64
ATT_WIDTH = ATT_HEADS * HEAD_DIM
CONV_WIDTH = D_MODEL // 2
CONV_TAPS = 31
EVEN_IN = 2 * CONV_WIDTH + 3 * ATT_WIDTH
EVEN_MIX = CONV_WIDTH + ATT_WIDTH
GMLP_CHUNK = 128
GMLP_GROUPS = 8
GMLP_WIDTH = 2 * D_MODEL
GMLP_GROUP_DIM = GMLP_WIDTH // GMLP_GROUPS
D_FF = 2816
FFN_TAPS = 3
EPS = 1e-6
N_EVEN = (DEPTH + 1) // 2
N_ODD = DEPTH // 2

kernel_name = "hybrid_conformer_chunkattn_gmlp_convffn"

def rms_norm(x, g):
    xf = x.astype(jnp.float32)
    y = xf * lax.rsqrt(jnp.mean(xf * xf, axis=-1, keepdims=True) + EPS)
    return (y * g.astype(jnp.float32)).astype(x.dtype)

def layer_norm(x, g, b):
    xf = x.astype(jnp.float32)
    mu = jnp.mean(xf, axis=-1, keepdims=True)
    var = jnp.mean(jnp.square(xf - mu), axis=-1, keepdims=True)
    y = (xf - mu) * lax.rsqrt(var + EPS) * g.astype(jnp.float32) + b.astype(jnp.float32)
    return y.astype(x.dtype)

def causal_dwconv(x, w, b):
    taps = w.shape[0]
    y = lax.conv_general_dilated(
        x, w[:, None, :].astype(x.dtype), window_strides=(1,),
        padding=[(taps - 1, 0)], dimension_numbers=('NWC', 'WIO', 'NWC'),
        feature_group_count=x.shape[-1])
    return y + b.astype(x.dtype)

def band_rel_index():
    qpos = np.arange(CHUNK)[:, None] + N_LEFT_CHUNKS * CHUNK
    kpos = np.arange(BAND)[None, :]
    return np.clip(qpos - kpos, -(CHUNK - 1), REL_MAX) + (CHUNK - 1)

def chunked_rel_attention(q, k, v, qn_g, kn_g, rel_bias):
    B, S, _ = q.shape
    nc = S // CHUNK
    q = rms_norm(q.reshape(B, nc, CHUNK, ATT_HEADS, HEAD_DIM), qn_g)
    k = rms_norm(k.reshape(B, S, ATT_HEADS, HEAD_DIM), kn_g)
    v = v.reshape(B, S, ATT_HEADS, HEAD_DIM)
    pad = [(0, 0), (N_LEFT_CHUNKS * CHUNK, 0), (0, 0), (0, 0)]
    kp = jnp.pad(k, pad).reshape(B, nc + N_LEFT_CHUNKS, CHUNK, ATT_HEADS, HEAD_DIM)
    vp = jnp.pad(v, pad).reshape(B, nc + N_LEFT_CHUNKS, CHUNK, ATT_HEADS, HEAD_DIM)
    band = jnp.arange(nc)[:, None] + jnp.arange(N_LEFT_CHUNKS + 1)[None, :]
    kb = kp[:, band].reshape(B, nc, BAND, ATT_HEADS, HEAD_DIM)
    vb = vp[:, band].reshape(B, nc, BAND, ATT_HEADS, HEAD_DIM)
    s = jnp.einsum('bcqhd,bckhd->bchqk', q, kb).astype(jnp.float32) * (HEAD_DIM ** -0.5)
    bias = rel_bias[:, band_rel_index()].astype(jnp.float32)
    key_chunk = jnp.arange(nc)[:, None] + (jnp.arange(BAND) // CHUNK)[None, :] - N_LEFT_CHUNKS
    valid = (key_chunk >= 0)[None, :, None, None, :]
    s = jnp.where(valid, s + bias[None, None], -1e30)
    p = jax.nn.softmax(s, axis=-1).astype(v.dtype)
    o = jnp.einsum('bchqk,bckhd->bcqhd', p, vb)
    return o.reshape(B, S, ATT_WIDTH)

def conv_attn_mixer(h, w_in, conv_w, conv_b, conv_ln_g, conv_ln_b, qn_g, kn_g, rel_bias, w_out):
    z = h @ w_in
    a_lin, a_gate, q, k, v = jnp.split(
        z, [CONV_WIDTH, 2 * CONV_WIDTH, 2 * CONV_WIDTH + ATT_WIDTH,
            2 * CONV_WIDTH + 2 * ATT_WIDTH], axis=-1)
    a = a_lin * jax.nn.sigmoid(a_gate)
    a = causal_dwconv(a, conv_w, conv_b)
    a = jax.nn.silu(layer_norm(a, conv_ln_g, conv_ln_b))
    o = chunked_rel_attention(q, k, v, qn_g, kn_g, rel_bias)
    return jnp.concatenate([a, o], axis=-1) @ w_out

def gmlp_mixer(h, w_in, gate_ln_g, gate_ln_b, w_sp, b_sp, w_out):
    B, S, _ = h.shape
    z = jax.nn.gelu(h @ w_in)
    u, v = jnp.split(z, 2, axis=-1)
    v = layer_norm(v, gate_ln_g, gate_ln_b)
    nc = S // GMLP_CHUNK
    v = v.reshape(B, nc, GMLP_CHUNK, GMLP_GROUPS, GMLP_GROUP_DIM)
    causal = jnp.tril(jnp.ones((GMLP_CHUNK, GMLP_CHUNK), dtype=bool))
    w = jnp.where(causal[None], w_sp, 0.0).astype(v.dtype)
    sv = jnp.einsum('gts,bcsgd->bctgd', w, v) + b_sp.T.astype(v.dtype)[None, None, :, :, None]
    y = u * sv.reshape(B, S, GMLP_WIDTH)
    return y @ w_out

def conv_ffn(h, w_gate, w_up, dw_w, dw_b, w_down):
    g = causal_dwconv(h @ w_gate, dw_w, dw_b)
    return (jax.nn.silu(g) * (h @ w_up)) @ w_down

def setup_inputs(seed: int = 0) -> dict:
    key = jax.random.key(seed)
    ks = jax.random.split(key, 24)

    def nrm(k, shape, scale):
        return jax.random.normal(k, shape, jnp.float32) * scale

    return {
        "x": nrm(ks[0], (BATCH, SEQ, D_MODEL), 1.0),
        "mix_norm_g": 1.0 + nrm(ks[1], (DEPTH, D_MODEL), 0.05),
        "w_in_e": nrm(ks[2], (N_EVEN, D_MODEL, EVEN_IN), D_MODEL ** -0.5),
        "conv_w": nrm(ks[3], (N_EVEN, CONV_TAPS, CONV_WIDTH), CONV_TAPS ** -0.5),
        "conv_b": nrm(ks[4], (N_EVEN, CONV_WIDTH), 0.02),
        "conv_ln_g": 1.0 + nrm(ks[5], (N_EVEN, CONV_WIDTH), 0.05),
        "conv_ln_b": nrm(ks[6], (N_EVEN, CONV_WIDTH), 0.02),
        "qn_g": 1.0 + nrm(ks[7], (N_EVEN, HEAD_DIM), 0.05),
        "kn_g": 1.0 + nrm(ks[8], (N_EVEN, HEAD_DIM), 0.05),
        "rel_bias": nrm(ks[9], (N_EVEN, ATT_HEADS, N_REL), 0.5),
        "w_out_e": nrm(ks[10], (N_EVEN, EVEN_MIX, D_MODEL), EVEN_MIX ** -0.5),
        "w_in_o": nrm(ks[11], (N_ODD, D_MODEL, 2 * GMLP_WIDTH), D_MODEL ** -0.5),
        "gate_ln_g": 1.0 + nrm(ks[12], (N_ODD, GMLP_WIDTH), 0.05),
        "gate_ln_b": nrm(ks[13], (N_ODD, GMLP_WIDTH), 0.02),
        "w_sp": nrm(ks[14], (N_ODD, GMLP_GROUPS, GMLP_CHUNK, GMLP_CHUNK), GMLP_CHUNK ** -0.5),
        "b_sp": 1.0 + nrm(ks[15], (N_ODD, GMLP_GROUPS, GMLP_CHUNK), 0.1),
        "w_out_o": nrm(ks[16], (N_ODD, GMLP_WIDTH, D_MODEL), GMLP_WIDTH ** -0.5),
        "ffn_norm_g": 1.0 + nrm(ks[17], (DEPTH, D_MODEL), 0.05),
        "w_gate": nrm(ks[18], (DEPTH, D_MODEL, D_FF), D_MODEL ** -0.5),
        "w_up": nrm(ks[19], (DEPTH, D_MODEL, D_FF), D_MODEL ** -0.5),
        "ffn_dw_w": nrm(ks[20], (DEPTH, FFN_TAPS, D_FF), FFN_TAPS ** -0.5),
        "ffn_dw_b": nrm(ks[21], (DEPTH, D_FF), 0.02),
        "w_down": nrm(ks[22], (DEPTH, D_FF, D_MODEL), D_FF ** -0.5),
    }

def reference(x, mix_norm_g, w_in_e, conv_w, conv_b, conv_ln_g, conv_ln_b, qn_g, kn_g,
              rel_bias, w_out_e, w_in_o, gate_ln_g, gate_ln_b, w_sp, b_sp, w_out_o,
              ffn_norm_g, w_gate, w_up, ffn_dw_w, ffn_dw_b, w_down):
    for layer in range(DEPTH):
        h = rms_norm(x, mix_norm_g[layer])
        if layer % 2 == 0:
            e = layer // 2
            x = x + conv_attn_mixer(h, w_in_e[e], conv_w[e], conv_b[e], conv_ln_g[e],
                                    conv_ln_b[e], qn_g[e], kn_g[e], rel_bias[e], w_out_e[e])
        else:
            o = layer // 2
            x = x + gmlp_mixer(h, w_in_o[o], gate_ln_g[o], gate_ln_b[o], w_sp[o], b_sp[o],
                               w_out_o[o])
        h = rms_norm(x, ffn_norm_g[layer])
        x = x + conv_ffn(h, w_gate[layer], w_up[layer], ffn_dw_w[layer], ffn_dw_b[layer],
                         w_down[layer])
    return x


_drawn_inputs = setup_inputs


def setup_inputs(seed=0):
    import zlib

    import numpy as np

    out = dict(_drawn_inputs(seed))
    spreads = {}
    factors = {'conv_b': 2.854,
     'conv_ln_b': 5.422,
     'qn_g': 8.0,
     'kn_g': 8.0,
     'gate_ln_g': 3.492,
     'gate_ln_b': 8.0,
     'ffn_dw_b': 4.199}
    for name, (base, spread) in spreads.items():
        noise = np.random.default_rng([zlib.crc32(name.encode()), seed]).standard_normal(out[name].shape)
        drawn = base * np.exp(spread * noise) if base else spread * noise
        out[name] = __import__('jax').numpy.asarray(drawn.astype(out[name].dtype))
    for name, factor in factors.items():
        out[name] = (out[name] * factor).astype(out[name].dtype)
    return out
```

```python
from contextlib import ExitStack

import numpy as np

import concourse.bass as bass
from concourse import mybir

ALU = mybir.AluOpType
ACT = mybir.ActivationFunctionType
AX = mybir.AxisListType
F32 = mybir.dt.float32
F32R = mybir.dt.float32r

P = 128
D = 1024
S = 1024
HALF = 512
KB = D // P
TB = S // P
EPS = 1e-6

CONVW = 512
CB = CONVW // P
TAPS = 31
LEFT = TAPS - 1
CVW = 1056
NH, HD = 8, 64
NPAIR = NH // 2
BANDW = 640
NREL = 320
RELW = 768
MASKED = -1e30

FB = 2816 // P
FG = FB // 2
GB = 2048 // P
GG = GB // 2

T_QKV = 2 * CB
T_OUT = T_QKV + 12
T_FFN0 = T_OUT + 8
T_GMLP = T_FFN0 + 3 * FB
T_V = T_GMLP + 2
T_GLOOP = T_V + 16
T_FFN1 = T_GMLP + 3 * GB
NT = T_FFN1 + 3 * FB
SA, SB, SC, SD = range(4)

C_MIXG = 0
C_FFNG = C_MIXG + 2 * KB
C_CONVW = C_FFNG + 2 * KB
C_CONVB = C_CONVW + CB * TAPS
C_LNG = C_CONVB + CB
C_LNB = C_LNG + CB
C_QG = C_LNB + CB
C_KG = C_QG + 1
C_GG = C_KG + 1
C_GB = C_GG + GB
C_DW = C_GB + GB
NPAR = C_DW + 2 * FB * 4

ST_N0, ST_LN, ST_N1, ST_N2, ST_N3 = range(5)
NORM_G = [C_MIXG, C_FFNG, C_MIXG + KB, C_FFNG + KB]
NORM_ORDER = [list(range(8)), [4, 5, 0, 1, 2, 3, 6, 7], list(range(8)), list(range(8))]

SWEEP = [4, 5, 6, 7, 0, 1, 2, 3]


def program(nc, xT, wstream, params, rel, wsp, bsp, outT):
    with ExitStack() as ctx:
        base = nc.sbuf_base
        base = (base + 31) // 32 * 32

        def at(name, offset, shape, dt):
            return nc.alloc_sbuf_tensor_at(name, shape, dt, offset=base + offset)

        def sem(name):
            return ctx.enter_context(nc.semaphore(name))

        KiB = 1024
        o_x, o_hh, o_hl, o_hid, o_raw = 0, 32 * KiB, 64 * KiB, 96 * KiB, 128 * KiB
        o_wh, o_wl = 136 * KiB, 152 * KiB
        o_rb, o_ta, o_tc, o_tu, o_tg = 168 * KiB, 172 * KiB, 176 * KiB, 180 * KiB, 184 * KiB
        o_vn = o_tg + 4128
        o_small = o_vn + 16 * KiB

        x = at("x", o_x, [P, KB, S], F32)
        hh = at("hh", o_hh, [P, KB, S], F32R)
        hl = at("hl", o_hl, [P, KB, S], F32R)
        hidh = at("hidh", o_hid, [P, 4, S], F32R)
        hidl = at("hidl", o_hid + 16 * KiB, [P, 4, S], F32R)
        raw = at("raw", o_raw, [P, 2, 1024], F32)
        wh = at("wh", o_wh, [P, 4, 1024], F32R)
        wl = at("wl", o_wl, [P, 4, 1024], F32R)
        rstdB = at("rstdB", o_rb, [P, S], F32)
        tA = at("tA", o_ta, [P, S], F32)
        tC = at("tC", o_tc, [P, S], F32)
        tU = at("tU", o_tu, [P, S], F32)
        tG = at("tG", o_tg, [P, S + 2], F32)
        vnh = at("vnh", o_vn, [P, S], F32R)
        vnl = at("vnl", o_vn + 4 * KiB, [P, S], F32R)
        wsph = at("wsph", o_vn + 8 * KiB, [P, S], F32R)
        wspl = at("wspl", o_vn + 12 * KiB, [P, S], F32R)
        qk = at("qk", o_x, [P, 2, TB, CONVW], F32)
        vraw = at("vraw", o_vn, [P, TB, CONVW], F32)
        cv = at("cv", o_hid, [P, CB + 1, CVW], F32)
        ptl = at("ptl", o_hid + 21120, [P, 2, BANDW], F32R)
        diagp = at("diagp", o_hid + 26240, [P, 2, P], F32)
        ssq = at("ssq", o_hid + 27264, [P, 2 * TB * NH], F32)
        rqk = at("rqk", o_hid + 27776, [P, 2 * TB * NH], F32)
        qgs = at("qgs", o_hid + 28288, [P, 1], F32)
        negmax = at("negmax", o_hid + 28320, [P, 2], F32)
        rsum = at("rsum", o_hid + 28352, [P, 2], F32)
        rinv = at("rinv", o_hid + 28384, [P, 2], F32)
        qth = at("qth", o_hh, [P, S], F32R)
        qtl = at("qtl", o_hh + 4 * KiB, [P, S], F32R)
        kth = at("kth", o_hh + 8 * KiB, [P, S], F32R)
        ktl = at("ktl", o_hh + 12 * KiB, [P, S], F32R)
        vh = at("vh", o_hl, [P, TB, P], F32R)
        vl = at("vl", o_hl + 4 * KiB, [P, TB, P], F32R)
        bias = at("bias", o_hl + 8 * KiB, [P, 2, BANDW], F32)
        prob = at("prob", o_wh + 8 * KiB, [P, 2, BANDW], F32)
        pth = at("pth", o_wl + 8 * KiB, [P, 2, BANDW], F32R)
        sBt = at("sBt", o_vn, [P, GB, P], F32)
        swsp = at("swsp", o_vn + 8 * KiB, [P, S], F32)
        sbsp = at("sbsp", o_vn + 12 * KiB, [P, S], F32)
        etab = at("etab", o_hid, [NH, RELW], F32)
        uearly = at("uearly", o_hid + 8 * KiB, [P, 2, S], F32)
        vst = at("vst", o_hid + 24 * KiB, [P, 4, HALF], F32)
        wspr = at("wspr", o_hid, [P, S], F32)

        s_off = [o_small]

        def small(name, cols, dt=F32):
            t = at(name, s_off[0], [P, cols], dt)
            s_off[0] += (cols * 4 + 31) // 32 * 32
            return t

        par = small("par", NPAR)
        ident = small("ident", P)
        ones = small("ones", P)
        bblk = small("bblk", 2 * P)
        rcol = small("rcol", TB)
        root = small("root", TB)
        epsc = small("epsc", 1)
        mv = small("mv", 2 * TB)
        vstat = at("vstat", o_vn, [P, TB, 4, 6], F32)

        PS = [ctx.enter_context(nc.psum_tensor(f"ps{i}", [P, 2 * HALF], F32)) for i in range(4)]

        def bank(tok):
            return PS[tok // 2][:, tok % 2 * HALF:(tok % 2 + 1) * HALF]

        e_dram = nc.dram_tensor("rel_rows", [NH, P, RELW], F32, kind="Internal").ap()
        v_dram = nc.dram_tensor("v_gelu", [S, 2048], F32, kind="Internal").ap()
        b_dram = nc.dram_tensor("pos_bias", [P, GB * P], F32, kind="Internal").ap()
        w_dram = nc.dram_tensor("pos_masked", [P, S], F32, kind="Internal").ap()
        v_blocks = v_dram.rearrange("(c s) d -> s c d", s=P)

        raw_in = [sem(f"raw_in{i}") for i in range(2)]
        w_hi, w_lo = sem("w_hi"), sem("w_lo")
        w_used = sem("w_used")
        x_in = [sem(f"x_in{i}") for i in range(KB)]
        par_in, rel_in, pos_in = sem("par_in"), sem("rel_in"), sem("pos_in")
        const = sem("const")
        e_ready, e_out = sem("e_ready"), sem("e_out")
        pos_masked, pos_rows, pos_copied = sem("pos_masked"), sem("pos_rows"), sem("pos_copied")
        pos_bias, pos_out = sem("pos_bias"), sem("pos_out")
        n_hi, n_lo, n_sq, n_sum = sem("n_hi"), sem("n_lo"), sem("n_sq"), sem("n_sum")
        st_sum, st_root, st_rcol = sem("st_sum"), sem("st_root"), sem("st_rcol")
        st_diag, st_row, st_rb = sem("st_diag"), sem("st_row"), sem("st_rb")
        lin_out, gate_out, sig, glu = sem("lin_out"), sem("gate_out"), sem("sig"), sem("glu")
        cv_pad, cv_first, cv_tap, cv_done = sem("cv_pad"), sem("cv_first"), sem("cv_tap"), sem("cv_done")
        tok_done, tok_free = sem("tok_done"), sem("tok_free")
        qk_sq, qk_sum, qk_root, qk_rinv = sem("qk_sq"), sem("qk_sum"), sem("qk_root"), sem("qk_rinv")
        qg_ready = sem("qg_ready")
        qn_ready, qt_done, qt_hi, qt_lo = sem("qn_ready"), sem("qt_done"), sem("qt_hi"), sem("qt_lo")
        bias_in = [sem(f"bias_in{i}") for i in range(2)]
        bias_ok = sem("bias_ok")
        sc_seen, bias_seen = sem("sc_seen"), sem("bias_seen")
        sc_done, sc_max, exp_done = sem("sc_done"), sem("sc_max"), sem("exp_done")
        p_inv, p_diag, pt_done = sem("p_inv"), sem("p_diag"), sem("pt_done")
        pt_hi, pt_lo, pv_done = sem("pt_hi"), sem("pt_lo"), sem("pv_done")
        o_hi, o_lo = sem("o_hi"), sem("o_lo")
        ln_sum0, ln_mean, ln_cent = sem("ln_sum0"), sem("ln_mean"), sem("ln_cent")
        ln_sq, ln_sum, ln_mul = sem("ln_sq"), sem("ln_sum"), sem("ln_mul")
        ln_act, ln_hi, ln_lo = sem("ln_act"), sem("ln_hi"), sem("ln_lo")
        m_done, x_add = sem("m_done"), sem("x_add")
        g_out, g_tap2, g_tap1, g_tap0 = sem("g_out"), sem("g_tap2"), sem("g_tap1"), sem("g_tap0")
        g_silu, up_out, hid, hid_hi, hid_lo = sem("g_silu"), sem("up_out"), sem("hid"), sem("hid_hi"), sem("hid_lo")
        wsp_in, wsp_hi, wsp_lo = sem("wsp_in"), sem("wsp_hi"), sem("wsp_lo")
        v_gelu, v_stat, v_mv, v_root, v_rs = sem("v_gelu"), sem("v_stat"), sem("v_mv"), sem("v_root"), sem("v_rs")
        v_out = [sem(f"v_out{i}") for i in range(4)]
        v_in, b_in = sem("v_in"), [sem("b_in0"), sem("b_in1")]
        vn_f, vn_hi, vn_lo = sem("vn_f"), sem("vn_hi"), sem("vn_lo")
        sv_done, sv_out, u_out, u_gelu = sem("sv_done"), sem("sv_out"), sem("u_out"), sem("u_gelu")
        y_f, y_hi, y_lo = sem("y_f"), sem("y_hi"), sem("y_lo")
        out_done = sem("out_done")

        X_OUTA, X_OUT = 8, 16
        X_FFN0 = X_OUT + FG * KB
        X_GMLP = X_FFN0 + GG * KB
        X_END = X_GMLP + FG * KB

        block = ctx.enter_context(nc.Block())

        def col(c):
            return par[:, c:c + 1]

        @block.sync
        def _(sp):
            def tile(t, slot):
                sp.wait_ge(w_lo, t - 1)
                sp.dma_start(raw[:, slot, :], wstream[t]).then_inc(raw_in[slot], 16)

            sp.dma_start(par[:], params).then_inc(par_in, 16)
            for m in range(KB):
                sp.dma_start(x[:, m, :], xT[m * P:(m + 1) * P, :]).then_inc(x_in[m], 16)
                if m == 0:
                    sp.dma_start(raw[:, 0, :], wstream[0]).then_inc(raw_in[0], 16)
                if m == 2:
                    sp.dma_start(raw[:, 1, :], wstream[1]).then_inc(raw_in[1], 16)
            sp.dma_start(etab[:, 383:383 + NREL], rel).then_inc(rel_in, 16)
            sp.dma_start(swsp[:], wsp).then_inc(pos_in, 16)
            sp.dma_start(sbsp[:], bsp.partition_broadcast(P)).then_inc(pos_in, 16)
            sp.wait_ge(e_ready, 2)
            sp.dma_start(e_dram, etab[:].unsqueeze(1).broadcast_to([NH, P, RELW])).then_inc(e_out, 16)
            sp.wait_ge(pos_masked, 1)
            sp.dma_start(w_dram, swsp[:]).then_inc(pos_out, 16)
            sp.wait_ge(pos_bias, GB)
            sp.dma_start(b_dram, sBt[:].rearrange("p b t -> p (b t)")).then_inc(pos_out, 16)
            with sp.Fori(1, (T_OUT + 2) // 2) as i:
                tile(2 * i, 0)
                tile(2 * i + 1, 1)
            sp.wait_ge(e_out, 16)
            sp.wait_ge(w_used, T_OUT)
            for p in range(NPAIR):
                for hd in range(2):
                    if p:
                        sp.wait_ge(sc_max, 16 * (p - 1) + 8 * hd + 8)
                    rows = bass.AP(tensor=e_dram.tensor, offset=(2 * p + hd) * P * RELW + P - 1,
                                   ap=[[RELW - 1, P], [1, BANDW]])
                    sp.dma_start(bias[:, hd, :], rows).then_inc(bias_in[hd], 16)
            sp.wait_ge(qn_ready, 2 * NPAIR)
            for m in range(KB):
                sp.dma_start(x[:, m, :], xT[m * P:(m + 1) * P, :]).then_inc(x_in[m], 16)
            with sp.Fori((T_OUT + 2) // 2, (T_FFN0 + 4) // 2) as i:
                tile(2 * i, 0)
                tile(2 * i + 1, 1)
            with sp.Fori((T_FFN0 + 4) // 2, (T_GMLP + 2) // 2) as i:
                tile(2 * i, 0)
                tile(2 * i + 1, 1)
            sp.wait_ge(pos_out, 32)
            sp.wait_ge(x_add, X_FFN0)
            sp.dma_start(wspr[:], w_dram).then_inc(wsp_in, 16)
            with sp.Fori(T_V // 2, (T_GLOOP + 2) // 2) as i:
                tile(2 * i, 0)
                tile(2 * i + 1, 1)
            for s in v_out:
                sp.wait_ge(s, 16 * 8)

            def vblock(b, j):
                sp.wait_ge(vn_lo, b)
                sp.dma_start(tA[:].rearrange("p (c d) -> p c d", c=TB),
                             v_blocks[:, :, bass.ts(b, P)]).then_inc(v_in, 16)
                sp.wait_ge(sv_out, b - 1)
                sp.dma_start(bblk[:, j * P:(j + 1) * P], b_dram[:, bass.ts(b, P)]).then_inc(b_in[j], 16)

            sp.wait_ge(st_row, ST_N2 + 1)
            sp.dma_start(tA[:].rearrange("p (c d) -> p c d", c=TB), v_blocks[:, :, 0:P]).then_inc(v_in, 16)
            sp.dma_start(bblk[:, 0:P], b_dram[:, 0:P]).then_inc(b_in[0], 16)
            vblock(1, 1)
            with sp.Fori(0, GG - 1) as i:
                tile(4 * i + (T_GLOOP + 2), 0)
                tile(4 * i + (T_GLOOP + 3), 1)
                vblock(2 * i + 2, 0)
                tile(4 * i + (T_GLOOP + 4), 0)
                tile(4 * i + (T_GLOOP + 5), 1)
                vblock(2 * i + 3, 1)
            with sp.Fori(T_FFN1 // 2, (T_FFN1 + 4) // 2) as i:
                tile(2 * i, 0)
                tile(2 * i + 1, 1)
            with sp.Fori((T_FFN1 + 4) // 2, NT // 2) as i:
                tile(2 * i, 0)
                tile(2 * i + 1, 1)
            for m in range(KB):
                sp.wait_ge(x_add, X_END - KB + m + 1)
                sp.dma_start(outT[m * P:(m + 1) * P, :], x[:, m, :]).then_inc(out_done, 16)
            sp.wait_ge(out_done, 16 * KB)

        @block.gpsimd
        def _(pool):
            pool.memset(ones[:], 1.0).then_inc(const, 1)
            pool.memset(epsc[:], EPS).then_inc(const, 1)
            pool.memset(ident[:], 0.0).then_inc(const, 1)
            pool.wait_ge(const, 3)
            pool.affine_select(out=ident[:], in_=ident[:], compare_op=ALU.not_equal, fill=1.0, base=0,
                               pattern=[[-1, P]], channel_multiplier=1).then_inc(const, 1)
            pool.memset(tG[:, 0:2], 0.0).then_inc(const, 1)

            def norm_sums(n):
                for m in range(1, KB):
                    pool.wait_ge(n_sq, 8 * n + m + 1)
                    if m > 1:
                        pool.wait_ge(n_sum, 7 * n + m - 1)
                    pool.tensor_tensor(tA[:], tA[:], (tC, tU)[m % 2][:], ALU.add).then_inc(n_sum, 1)

            norm_sums(0)
            pool.memset(etab[:, 383 + NREL:RELW], 0.0).then_inc(e_ready, 1)
            pool.wait_ge(rel_in, 16)
            pool.tensor_copy(etab[:, 0:383], etab[:, 383:384].broadcast_to([NH, 383])).then_inc(e_ready, 1)
            pool.wait_ge(pos_in, 32)
            w3 = swsp[:].rearrange("s (g t) -> s g t", g=GG)
            pool.affine_select(out=w3, in_=w3, compare_op=ALU.is_ge, fill=0.0, base=0,
                               pattern=[[0, GG], [1, P]], channel_multiplier=-1).then_inc(pos_masked, 1)
            pool.wait_ge(e_out, 16)
            pool.memset(cv[:, 0:CB, 0:LEFT], 0.0).then_inc(cv_pad, 1)
            pool.wait_ge(qk_rinv, 1)
            rq4 = rqk[:].rearrange("p (c t h) -> p c t h", c=2, t=TB)
            pool.wait_ge(tok_free, 8 + 24)
            with pool.Fori(0, NPAIR) as p:
                pool.wait_ge(qt_done, 2 * p)
                pool.wait_ge(bias_ok, 4 * p)
                for c, buf in ((0, tC), (1, tU)):
                    pool.tensor_tensor(
                        buf[:].rearrange("p (t h d) -> p t h d", t=TB, h=2),
                        qk[:, c, :, bass.ts(p, P)].rearrange("p t (h d) -> p t h d", h=2),
                        rq4[:, c, :, bass.ts(p, 2)].unsqueeze(3).broadcast_to([P, TB, 2, HD]),
                        ALU.mult).then_inc(qn_ready, 1)
                pool.wait_ge(qn_ready, 2 * p + 2)
                for hd in range(2):
                    pool.wait_ge(bias_in[hd], 16 * p + 16)
                    pool.wait_ge(bias_ok, 4 * p + 2 * hd)
                    pool.sem_inc(bias_seen, 1)
                    pool.memset(bias[0:64, hd, BANDW - 64:BANDW], MASKED).then_inc(bias_ok, 1)
                    pool.wait_ge(bias_ok, 4 * p + (2 * hd + 1))
                    pool.sem_inc(bias_seen, 1)
                    pool.memset(bias[64:128, hd, 0:64], MASKED).then_inc(bias_ok, 1)

            def conv_out(m):
                return cv[:, (m + CB) % (CB + 1), LEFT:LEFT + S]

            pool.wait_ge(cv_done, CB)
            pool.wait_ge(bias_ok, 4 * NPAIR)
            for m in range(1, CB):
                if m > 1:
                    pool.wait_ge(ln_sum0, m - 1)
                pool.tensor_tensor(tA[:], conv_out(0) if m == 1 else tA[:], conv_out(m), ALU.add).then_inc(ln_sum0, 1)
            for m in range(1, CB):
                pool.wait_ge(ln_sq, m + 1)
                if m > 1:
                    pool.wait_ge(ln_sum, m - 1)
                pool.tensor_tensor(tA[:], tA[:], (tC, tU)[m % 2][:], ALU.add).then_inc(ln_sum, 1)
            norm_sums(1)
            norm_sums(2)
            norm_sums(3)

        @block.tensor
        def _(pe):
            def fm_block(slot, ps, ks, first=0, n=KB, kwait=None):
                for pos in range(first, first + n):
                    k = ks[pos]
                    if kwait:
                        kwait(pos)
                    for w, h in ((wh, hh), (wh, hl), (wl, hh)):
                        for s in range(2):
                            mm = pe.matmul(ps[:, s * HALF:(s + 1) * HALF], w[:, slot, k * P:(k + 1) * P],
                                           h[:, k, s * HALF:(s + 1) * HALF],
                                           start=(pos == 0 and w is wh and h is hh),
                                           stop=(pos == len(ks) - 1 and w is wl))
                return mm

            def stats(st):
                for t in range(TB):
                    mm = pe.matmul(PS[2][:, t:t + 1], tA[:, t * P:(t + 1) * P], ones[:, 0:1], start=True, stop=True)
                mm.then_inc(st_sum, 1)

            def rows(st):
                pe.wait_ge(st_diag, st + 1)
                for s in range(2):
                    mm = pe.matmul(PS[3][:, s * HALF:(s + 1) * HALF], ones[:], tG[:, 2 + s * HALF:2 + (s + 1) * HALF],
                                   start=True, stop=True)
                mm.then_inc(st_row, 1)

            def first_two(n, t, slots, free0, free1):
                st = (ST_N0, ST_N1, ST_N2, ST_N3)[n]
                ks = NORM_ORDER[n]
                pe.wait_ge(w_lo, t + 1)
                free0()
                fm_block(slots[0], PS[0], ks, kwait=lambda pos: pe.wait_ge(n_lo, 8 * n + pos + 1)).then_inc(w_used, 1)
                pe.wait_ge(n_sum, 7 * (n + 1))
                stats(st)
                pe.wait_ge(w_lo, t + 2)
                free1()
                fm_block(slots[1], PS[1], ks, 0, 4)
                rows(st)
                fm_block(slots[1], PS[1], ks, 4, 4).then_inc(w_used, 1)

            def token_tile(t, j, free):
                pe.wait_ge(w_lo, t + 1)
                for kk in range(2):
                    k = 2 * j + kk
                    for pos, tok in enumerate(SWEEP):
                        if k == 0:
                            free(pos)
                        for w, h in ((wh, hh), (wl, hh), (wh, hl)):
                            mm = pe.matmul(bank(tok), h[:, k, tok * P:(tok + 1) * P], w[:, j, kk * HALF:(kk + 1) * HALF],
                                           start=(k == 0 and w is wh and h is hh), stop=(k == KB - 1 and h is hl))
                        if k == KB - 1 and pos < TB - 1:
                            mm.then_inc(tok_done, 1)
                mm.then_inc(w_used, 1)

            pe.wait_ge(const, 5)
            pe.wait_ge(pos_masked, 1)
            for s in range(2):
                mm = pe.matmul(PS[3][:, s * HALF:(s + 1) * HALF], ones[:], swsp[:, s * HALF:(s + 1) * HALF], start=True, stop=True)
            mm.then_inc(pos_rows, 1)

            first_two(0, 0, (SA, SB), lambda: None, lambda: pe.wait_ge(pos_copied, 1))
            with pe.Fori(1, CB) as m:
                pe.wait_ge(w_lo, 2 * m + 1)
                pe.wait_ge(lin_out, m)
                fm_block(SA, PS[0], range(KB)).then_inc(w_used, 1)
                pe.wait_ge(w_lo, 2 * m + 2)
                pe.wait_ge(gate_out, m)
                fm_block(SB, PS[1], range(KB)).then_inc(w_used, 1)
            with pe.Fori(0, 3) as c:
                for j in range(4):
                    token_tile(4 * c + (T_QKV + j), j, lambda pos: pe.wait_ge(tok_free, 8 * c + (pos + 1)))

            pe.wait_ge(tok_free, 8 + 24)
            with pe.Fori(0, NPAIR) as p:
                pe.wait_ge(sc_max, 16 * p)
                for c, buf in ((0, tC), (1, tU)):
                    pe.wait_ge(qn_ready, 2 * p + (c + 1))
                    for t in range(TB):
                        mm = pe.transpose(PS[c][:, t * P:(t + 1) * P], buf[:, t * P:(t + 1) * P], ident[:])
                    mm.then_inc(qt_done, 1)

                def unit(u):
                    t = u % TB
                    return t, 64 * (u // TB), min(t + 1, 5) * P, max(0, t - 4) * P

                def scores(u):
                    t, r, w, k0 = unit(u)
                    if u == 0:
                        pe.wait_ge(qt_lo, 3 * p + 2)
                    if u >= 2:
                        pe.wait_ge(sc_max, 16 * p + (u - 1))
                    for a, b in ((0, min(w, HALF)), (HALF, w)):
                        if b > a:
                            for q, k in ((qth, kth), (qth, ktl), (qtl, kth)):
                                mm = pe.matmul(PS[u % 2][:, a:b], q[r:r + 64, t * P:(t + 1) * P], k[r:r + 64, k0 + a:k0 + b],
                                               start=(q is qth and k is kth), stop=(q is qtl))
                    mm.then_inc(sc_done, 1)

                def turn(u):
                    t, r, w, k0 = unit(u)
                    pe.wait_ge(p_diag, 16 * p + (u + 1))
                    pe.wait_ge(pt_lo, 16 * p + u)
                    for b in range(w // P):
                        mm = pe.matmul(PS[2][:, b * P:(b + 1) * P], prob[:, u % 2, b * P:(b + 1) * P], diagp[:, u % 2, :],
                                       start=True, stop=True)
                    mm.then_inc(pt_done, 1)

                def values(u):
                    t, r, w, k0 = unit(u)
                    pe.wait_ge(pt_lo, 16 * p + (u + 1))
                    if u == 0:
                        pe.wait_ge(qt_lo, 3 * p + 3)
                        pe.wait_ge(o_lo, 4 * p)
                    if u in (8, 12):
                        pe.wait_ge(o_lo, 4 * p + (u // 4 - 1))
                    c0 = u // 4 % 2 * HALF + t % 4 * P
                    for b in range(w // P):
                        for v, q in ((vh, pth), (vh, ptl), (vl, pth)):
                            mm = pe.matmul(PS[3][:, c0:c0 + P], v[:, k0 // P + b, :], q[:, u % 2, b * P:(b + 1) * P],
                                           start=(b == 0 and v is vh and q is pth), stop=(b == w // P - 1 and v is vl))
                    mm.then_inc(pv_done, 1)

                for step in range(18):
                    if step < 16:
                        scores(step)
                    if 1 <= step < 17:
                        turn(step - 1)
                    if step >= 2:
                        values(step - 2)

            pe.wait_ge(ln_sum0, CB - 1)
            pe.wait_ge(pt_lo, 64)
            for s in range(2):
                mm = pe.matmul(PS[2][:, s * HALF:(s + 1) * HALF], ones[:], tA[:, s * HALF:(s + 1) * HALF], start=True, stop=True)
            mm.then_inc(ln_mean, 1)

            def out_tile(j, k0):
                t = T_OUT + j
                pe.wait_ge(w_lo, t + 1)
                for half_ in range(2):
                    n = 2 * j + half_
                    if n >= 2:
                        pe.wait_ge(x_add, n - 1)
                    else:
                        pe.wait_ge(sc_max, 64)
                    for k in range(4):
                        for w, h in ((wh, hh), (wh, hl), (wl, hh)):
                            for s in range(2):
                                mm = pe.matmul(PS[n % 2][:, s * HALF:(s + 1) * HALF],
                                               w[:, j % 2, k * 256 + half_ * P:k * 256 + (half_ + 1) * P],
                                               h[:, k0 + k, s * HALF:(s + 1) * HALF],
                                               start=(k == 0 and w is wh and h is hh), stop=(k == 3 and w is wl))
                    mm.then_inc(w_used if half_ else m_done, 1)

            pe.wait_ge(o_lo, 16)
            out_tile(0, 4)
            pe.wait_ge(ln_sum, CB - 1)
            stats(ST_LN)
            out_tile(1, 4)
            rows(ST_LN)
            out_tile(2, 4)
            out_tile(3, 4)
            pe.wait_ge(ln_lo, CB)
            for j in range(4, 8):
                out_tile(j, 0)

            def down(slots, h0, x0):
                for m in range(KB):
                    pe.wait_ge(x_add, x0 + (m - 1))
                    for j in range(2):
                        for w, h in ((wh, hidh), (wh, hidl), (wl, hidh)):
                            for s in range(2):
                                mm = pe.matmul(PS[2 + m % 2][:, s * HALF:(s + 1) * HALF], w[:, slots[j], m * P:(m + 1) * P],
                                               h[:, h0 + j, s * HALF:(s + 1) * HALF],
                                               start=(j == 0 and w is wh and h is hidh), stop=(j == 1 and w is wl))
                    if m < KB - 1:
                        mm.then_inc(m_done, 1)
                mm.then_inc(w_used, 2)

            def ffn(f, n, t0, x0):
                b0 = FB * f
                first_two(n, t0, (SC, SD), lambda: pe.wait_ge(x_add, x0), lambda: None)
                for q, (slot, ps, done) in enumerate(((SA, PS[0], g_out), (SB, PS[1], up_out))):
                    pe.wait_ge(w_lo, t0 + 3 + q)
                    pe.wait_ge(done, b0 + 1)
                    fm_block(slot, ps, range(KB)).then_inc(w_used, 1)

                def group(i, odd):
                    t = 6 * i + (t0 - 2)
                    for q in range(4):
                        pe.wait_ge(w_lo, t + (q + 1))
                        pe.wait_ge((g_out, up_out)[q % 2], 2 * i + (b0 + q // 2))
                        fm_block(q % 2, PS[q % 2], range(KB)).then_inc(w_used, 1)
                    pe.wait_ge(w_lo, t + 6)
                    pe.wait_ge(hid_lo, 2 * i + b0)
                    down((SC, SD), 2 * (1 - odd), 8 * i + (x0 - 8))

                with pe.Fori(0, FG // 2) as ii:
                    group(2 * ii + 1, 1)
                    group(2 * ii + 2, 0)
                pe.wait_ge(w_lo, t0 + 3 * FB)
                pe.wait_ge(hid_lo, b0 + FB)
                down((SA, SB), 0, x0 + 8 * (FG - 1))

            ffn(0, 1, T_FFN0, X_OUT)

            first_two(2, T_GMLP, (SC, SD), lambda: pe.wait_ge(x_add, X_FFN0), lambda: None)
            with pe.Fori(0, 4) as c:
                for j in range(4):
                    token_tile(4 * c + (T_V + j), j, lambda pos: pe.wait_ge(tok_free, 8 * c + (32 + pos + 1)))
            pe.wait_ge(tok_free, 32 + 8 + 32)

            def positions(b, i, ps):
                pe.wait_ge(vn_lo, b + 1)
                for c in range(TB):
                    for v, w in ((vnh, wsph), (vnh, wspl), (vnl, wsph)):
                        mm = pe.matmul(ps[:, c * P:(c + 1) * P], v[:, c * P:(c + 1) * P], w[:, bass.ts(i, P)],
                                       start=(v is vnh and w is wsph), stop=(v is vnl))
                mm.then_inc(sv_done, 1)

            pe.wait_ge(wsp_lo, 1)
            positions(0, 0, PS[2])
            positions(1, 0, PS[3])

            def gmlp_group(i, odd):
                t = 4 * i + (T_GLOOP - 4)
                for j in range(2):
                    if j == 0:
                        pe.wait_ge(sv_out, 2 * i)
                        pe.wait_ge(x_add, 8 * i + (X_FFN0 - 8))
                    positions(2 * i + j, i, PS[2 + j])
                    pe.wait_ge(w_lo, t + (j + 1))
                    pe.wait_ge(u_out, 2 * i + j)
                    fm_block(j, PS[j], range(KB)).then_inc(w_used, 1)
                pe.wait_ge(w_lo, t + 4)
                pe.wait_ge(y_lo, 2 * i)
                pe.wait_ge(sv_out, 2 * i + 1)
                down_after_positions(i, odd, t)

            def down_after_positions(i, odd, t):
                x0 = 8 * i + (X_FFN0 - 8)
                for m in range(KB):
                    if m == 1:
                        pe.wait_ge(sv_out, 2 * i + 2)
                    if m >= 2:
                        pe.wait_ge(x_add, x0 + (m - 1))
                    for j in range(2):
                        for w, h in ((wh, hidh), (wh, hidl), (wl, hidh)):
                            for s in range(2):
                                mm = pe.matmul(PS[2 + m % 2][:, s * HALF:(s + 1) * HALF], w[:, (SC, SD)[j], m * P:(m + 1) * P],
                                               h[:, 2 * (1 - odd) + j, s * HALF:(s + 1) * HALF],
                                               start=(j == 0 and w is wh and h is hidh), stop=(j == 1 and w is wl))
                    if m < KB - 1:
                        mm.then_inc(m_done, 1)
                mm.then_inc(w_used, 2)

            with pe.Fori(0, (GG - 2) // 2) as ii:
                gmlp_group(2 * ii + 1, 1)
                gmlp_group(2 * ii + 2, 0)
            gmlp_group(GG - 1, 1)
            pe.wait_ge(w_lo, T_FFN1)
            pe.wait_ge(y_lo, GB)
            down((SA, SB), 2, X_FFN0 + 8 * (GG - 1))
            ffn(1, 3, T_FFN1, X_GMLP)

        def o_part(act, p, q):
            r = 64 * (q // 2)
            act.wait_ge(pv_done, 16 * p + (4 * q + 4))
            act.activation(hh[r:r + 64, bass.ds(p + 4, 1), q % 2 * HALF:(q % 2 + 1) * HALF].rearrange("p a n -> p (a n)"),
                           PS[3][r:r + 64, q % 2 * HALF:(q % 2 + 1) * HALF], ACT.Copy).then_inc(o_hi, 1)

        @block.scalar
        def _(act):
            def split(t, slot, raw_slot, freed_by):
                act.wait_ge(raw_in[raw_slot], (t // 2 + 1) * 16)
                if freed_by is not None:
                    act.wait_ge(w_used, freed_by + 1)
                act.activation(wh[:, slot, :], raw[:, raw_slot, :], ACT.Copy).then_inc(w_hi, 1)

            def split_r(t, half, slot, raw_slot, back):
                act.wait_ge(raw_in[raw_slot], half * 16 + 16)
                act.wait_ge(w_used, t + (1 - back))
                act.activation(wh[:, slot, :], raw[:, raw_slot, :], ACT.Copy).then_inc(w_hi, 1)

            def norm_hi(n, m):
                act.activation(hh[:, m, :], x[:, m, :], ACT.Copy, scale=col(NORM_G[n] + m)).then_inc(n_hi, 1)

            def norm_sq(n, m):
                if m >= 3:
                    act.wait_ge(n_sum, 7 * n + m - 2)
                act.activation((tA if m == 0 else (tC, tU)[m % 2])[:], x[:, m, :], ACT.Square).then_inc(n_sq, 1)

            def take_root(st, count):
                act.wait_ge(st_sum, st + 1)
                act.activation(root[:], PS[2][:, 0:TB], ACT.Sqrt, scale=1.0 / count, bias=epsc[:, 0:1]).then_inc(st_root, 1)

            def copy_rows(st):
                act.wait_ge(st_row, st + 1)
                act.activation(rstdB[:], PS[3][:], ACT.Copy).then_inc(st_rb, 1)

            act.wait_ge(par_in, 16)
            act.wait_ge(const, 5)
            for m in range(KB):
                act.wait_ge(x_in[m], 16)
                norm_hi(0, m)
                if m in (1, 3):
                    split(m // 2, m // 2, m // 2, None)
                norm_sq(0, m)
            act.wait_ge(pos_rows, 1)
            act.activation(rstdB[:], PS[3][:], ACT.Copy).then_inc(pos_copied, 1)
            take_root(ST_N0, D)
            act.wait_ge(pos_bias, GB)
            split(2, SA, 0, 0)
            copy_rows(ST_N0)
            act.preload_act_table(ACT.Sigmoid)

            def conv_first(m):
                if m:
                    act.wait_ge(cv_done, m)
                src = cv[:, m, :]
                act.activation(cv[:, (m + CB) % (CB + 1), LEFT:LEFT + S], src[:, 0:S], ACT.Identity,
                               scale=col(C_CONVW + m * TAPS), bias=col(C_CONVB + m)).then_inc(cv_first, 1)
                act.activation(tG[:, 2:2 + S], src[:, 1:1 + S], ACT.Copy,
                               scale=col(C_CONVW + m * TAPS + 1)).then_inc(cv_first, 1)

            for m in range(CB):
                if m:
                    split(2 * m + 2, SA, 0, 2 * m)
                if m == 3:
                    conv_first(1)
                act.wait_ge(gate_out, m + 1)
                act.activation(tU[:], tU[:], ACT.Sigmoid).then_inc(sig, 1)
                split(2 * m + 3, SB, 1, 2 * m + 1)
                if m == 0:
                    act.wait_ge(glu, 1)
                    conv_first(0)
            act.wait_ge(st_rb, 1)
            act.wait_ge(st_root, 1)
            act.sem_inc(tok_free, 4)
            act.wait_ge(lin_out, CB)
            act.wait_ge(gate_out, CB)
            act.sem_inc(tok_free, 4)

            for c in range(3):
                for q in range(4):
                    t = T_QKV + 2 + 4 * c + q
                    split(t, (t - T_QKV) % 4, t % 2, t - 4)
                if c < 2:
                    conv_first(c + 2)
                for pos, tok in enumerate(SWEEP):
                    if pos < TB - 1:
                        act.wait_ge(tok_done, 7 * c + pos + 1)
                    else:
                        act.wait_ge(w_used, T_QKV + 4 * c + 4)
                    dst = qk[:, c, tok, :] if c < 2 else vraw[:, tok, :]
                    act.activation(dst, bank(tok), ACT.Copy, scale=rcol[:, tok:tok + 1]).then_inc(tok_free, 1)
                if c < 2:
                    for j in range(4):
                        n = 4 * c + j
                        act.wait_ge(tok_free, 8 + 8 * c + 8)
                        if n >= 2:
                            act.wait_ge(qk_sum, n - 1)
                        act.activation((tC, tU)[j % 2][:], qk[:, c, 2 * j:2 * j + 2, :].rearrange("p t d -> p (t d)"),
                                       ACT.Square).then_inc(qk_sq, 1)
                if c == 1:
                    act.wait_ge(qk_sum, 8)
                    act.activation(rqk[:], ssq[:], ACT.Sqrt, scale=1.0 / HD, bias=epsc[:, 0:1]).then_inc(qk_root, 1)
            act.activation(qgs[:], col(C_QG), ACT.Copy, scale=float(HD) ** -0.5).then_inc(qg_ready, 1)
            act.preload_act_table(ACT.Exp)
            act.wait_ge(qg_ready, 1)
            act.wait_ge(tok_free, 8 + 24)
            with act.Fori(0, NPAIR) as p:
                act.wait_ge(qt_done, 2 * p + 1)
                act.activation(qth[:], PS[0][:], ACT.Copy, scale=qgs[:, 0:1]).then_inc(qt_hi, 1)
                act.wait_ge(qt_done, 2 * p + 2)
                act.activation(kth[:], PS[1][:], ACT.Copy, scale=col(C_KG)).then_inc(qt_hi, 1)
                act.activation(vh[:], vraw[:, :, bass.ts(p, P)], ACT.Copy).then_inc(qt_hi, 1)
                for step in range(17):
                    if step < 16:
                        u = step
                        w = min(u % TB + 1, 5) * P
                        act.wait_ge(sc_max, 16 * p + (u + 1))
                        act.activation(prob[:, u % 2, 0:w], prob[:, u % 2, 0:w], ACT.Exp, scale=-1.0,
                                       bias=negmax[:, u % 2:u % 2 + 1], accum_out=rsum[:, u % 2:u % 2 + 1]).then_inc(exp_done, 1)
                    if step >= 1:
                        u = step - 1
                        w = min(u % TB + 1, 5) * P
                        act.wait_ge(pt_done, 16 * p + (u + 1))
                        if u >= 2:
                            act.wait_ge(pv_done, 16 * p + (u - 1))
                        act.activation(pth[:, u % 2, 0:w], PS[2][:, 0:w], ACT.Copy).then_inc(pt_hi, 1)
                        if u >= 5 and u % 4 == 1:
                            o_part(act, p, u // 4 - 1)
                o_part(act, p, 3)


            def conv_out(m):
                return cv[:, (m + CB) % (CB + 1), LEFT:LEFT + S]

            for m in range(CB):
                act.wait_ge(ln_cent, m + 1)
                if m == 3:
                    act.wait_ge(ln_sum, 1)
                act.activation((tA if m == 0 else (tC, tU)[m % 2])[:], conv_out(m), ACT.Square).then_inc(ln_sq, 1)
            split(T_OUT + 2, SA, 0, T_OUT)
            take_root(ST_LN, CONVW)
            split(T_OUT + 3, SB, 1, T_OUT + 1)
            copy_rows(ST_LN)
            for m in range(CB):
                act.wait_ge(ln_mul, m + 1)
                act.activation(conv_out(m), conv_out(m), ACT.Silu, scale=col(C_LNG + m), bias=col(C_LNB + m)).then_inc(ln_act, 1)
                act.wait_ge(ln_act, m + 1)
                act.activation(hh[:, m, :], conv_out(m), ACT.Copy).then_inc(ln_hi, 1)
            split(T_OUT + 4, SA, 0, T_OUT + 2)
            split(T_OUT + 5, SB, 1, T_OUT + 3)
            split(T_OUT + 6, SA, 0, T_OUT + 4)
            for m in (0, 1):
                act.wait_ge(x_add, X_OUTA + m + 1)
                norm_sq(1, m)
            split(T_OUT + 7, SB, 1, T_OUT + 5)
            split(T_FFN0, SC, 0, T_OUT)
            split(T_FFN0 + 1, SD, 1, T_OUT + 1)
            for m in (2, 3):
                act.wait_ge(x_add, X_OUTA + m + 1)
                norm_sq(1, m)
            split(T_FFN0 + 2, SA, 0, T_OUT + 6)
            for m in (4, 5):
                act.wait_ge(x_add, X_OUTA + m + 1)
                norm_hi(1, m)
                norm_sq(1, m)
            act.wait_ge(w_used, T_FFN0)
            for m in range(4):
                norm_hi(1, m)
            for m in (6, 7):
                act.wait_ge(x_add, X_OUTA + m + 1)
                norm_hi(1, m)
                norm_sq(1, m)
            split(T_FFN0 + 3, SB, 1, T_OUT + 7)
            take_root(ST_N1, D)
            copy_rows(ST_N1)

            def ffn(f, t0, x0, last_n):
                b0 = FB * f
                act.preload_act_table(ACT.Silu)

                def gate(b, f0):
                    act.wait_ge(g_out, b + (b0 + 1))
                    dw = par[:, bass.ds(f0, 4)]
                    act.activation(tC[:], tG[:, 2:2 + S], ACT.Identity, scale=dw[:, 2:3], bias=dw[:, 3:4]).then_inc(g_tap2, 1)
                    act.wait_ge(g_tap0, b + (b0 + 1))
                    act.activation(tC[:], tC[:], ACT.Silu).then_inc(g_silu, 1)

                def hidden(b, slot, free):
                    act.wait_ge(hid, b + (b0 + 1))
                    if free is not None:
                        act.wait_ge(w_used, free)
                    act.activation(hidh[:, slot, :], tU[:], ACT.Copy).then_inc(hid_hi, 1)

                dw0 = C_DW + 4 * FB * f
                gate(0, dw0)
                hidden(0, 0, None)
                gate(1, dw0 + 4)
                split(t0 + 4, SA, 0, t0 + 2)
                split(t0 + 5, SB, 1, t0 + 3)
                hidden(1, 1, None)

                def group(i, ih, odd):
                    t, h = 6 * i + (t0 - 2), ih + (t0 - 2) // 2
                    split_r(t + 2, h + 1, SA, 0, 2)
                    gate(2 * i, 8 * i + dw0)
                    split_r(t + 3, h + 1, SB, 1, 2)
                    hidden(2 * i, 2 * odd, t)
                    split_r(t + 4, h + 2, SC, 0, 6)
                    split_r(t + 5, h + 2, SD, 1, 6)
                    gate(2 * i + 1, 8 * i + (dw0 + 4))
                    split_r(t + 6, h + 3, SA, 0, 4)
                    split_r(t + 7, h + 3, SB, 1, 4)
                    hidden(2 * i + 1, 2 * odd + 1, t)

                with act.Fori(0, FG // 2) as ii:
                    group(2 * ii + 1, 6 * ii + 3, 1)
                    group(2 * ii + 2, 6 * ii + 6, 0)

            def norm_after(n, x0, tail, lo):
                act.wait_ge(*lo)
                for m in range(KB):
                    act.wait_ge(x_add, x0 + m + 1)
                    norm_hi(n, m)
                    norm_sq(n, m)
                for t, slot in tail:
                    split(t, slot, t % 2, t - 4)

            ffn(0, T_FFN0, X_OUT, 2)
            split(T_GMLP, SC, 0, T_GMLP - 4)
            split(T_GMLP + 1, SD, 1, T_GMLP - 3)
            norm_after(2, X_FFN0 - KB, ((T_V, SA), (T_V + 1, SB)), (hid_lo, FB))
            take_root(ST_N2, D)
            act.wait_ge(wsp_in, 16)
            act.activation(wsph[:], wspr[:], ACT.Copy).then_inc(wsp_hi, 1)
            copy_rows(ST_N2)
            act.preload_act_table(ACT.Gelu_apprx_tanh)
            for j in range(2):
                act.wait_ge(u_out, j + 1)
                act.activation(uearly[:, j, :], uearly[:, j, :], ACT.Gelu_apprx_tanh).then_inc(u_gelu, 1)
            act.wait_ge(st_rb, ST_N2 + 1)
            act.wait_ge(st_root, ST_N2 + 1)
            act.sem_inc(tok_free, 8)

            def v_store(c, tok, q, n8):
                act.wait_ge(v_gelu, n8)
                act.dma_start(v_dram[tok * P:(tok + 1) * P, bass.ts(c, HALF)], vst[:, q, :]).then_inc(v_out[q], 16)

            with act.Fori(0, 4) as c:
                for q in range(4):
                    split_r(4 * c + (T_V + 2 + q), 2 * c + ((T_V + 2 + q) // 2), (2 + q) % 4, q % 2, 4)
                for pos, tok in enumerate(SWEEP):
                    if pos < TB - 1:
                        act.wait_ge(tok_done, 7 * c + (21 + pos + 1))
                    else:
                        act.wait_ge(w_used, 4 * c + (T_V + 4))
                    act.wait_ge(v_out[pos % 4], 32 * c + 16 * (pos // 4))
                    act.wait_ge(v_stat, 8 * c + (pos - 3) if pos >= 4 else 8 * c)
                    if pos:
                        v_store(c, SWEEP[pos - 1], (pos - 1) % 4, 8 * c + pos)
                    act.activation(vst[:, pos % 4, :], bank(tok), ACT.Gelu_apprx_tanh, scale=rcol[:, tok:tok + 1]).then_inc(v_gelu, 1)
                v_store(c, SWEEP[7], 3, 8 * c + 8)
                act.sem_inc(tok_free, 8)
            act.wait_ge(v_mv, 1)
            act.activation(root[:], mv[:].rearrange("p (t a) -> p t a", a=2)[:, :, 1:2].rearrange("p t a -> p (t a)"),
                           ACT.Sqrt, bias=epsc[:, 0:1]).then_inc(v_root, 1)
            act.preload_act_table(ACT.Gelu_apprx_tanh)

            def vn_high(b):
                act.wait_ge(vn_f, b + 1)
                act.wait_ge(sv_done, b)
                act.activation(vnh[:], tA[:], ACT.Copy).then_inc(vn_hi, 1)

            def y_high(b, slot, free):
                act.wait_ge(y_f, b + 1)
                if free is not None:
                    act.wait_ge(w_used, free)
                act.activation(hidh[:, slot, :], tC[:], ACT.Copy).then_inc(y_hi, 1)

            vn_high(0)
            vn_high(1)
            y_high(0, 0, None)
            vn_high(2)
            y_high(1, 1, None)

            def gmlp_group(i, odd, last=False):
                t, h = 4 * i + (T_GLOOP - 4), 2 * i + (T_GLOOP - 4) // 2
                split_r(t + 2, h + 1, SC, 0, 4)
                split_r(t + 3, h + 1, SD, 1, 4)
                vn_high(2 * i + 1)
                split_r(t + 4, h + 2, SA, 0, 4)
                act.wait_ge(u_out, 2 * i + 1)
                act.activation(tU[:], tU[:], ACT.Gelu_apprx_tanh).then_inc(u_gelu, 1)
                y_high(2 * i, 2 * odd, t)
                split_r(t + 5, h + 2, SB, 1, 4)
                act.wait_ge(u_out, 2 * i + 2)
                act.activation(tU[:], tU[:], ACT.Gelu_apprx_tanh).then_inc(u_gelu, 1)
                y_high(2 * i + 1, 2 * odd + 1, t)
                if not last:
                    vn_high(2 * i + 2)

            with act.Fori(0, (GG - 2) // 2) as ii:
                gmlp_group(2 * ii + 1, 1)
                gmlp_group(2 * ii + 2, 0)
            gmlp_group(GG - 1, 1, last=True)
            split(T_FFN1, SC, 0, T_FFN1 - 4)
            split(T_FFN1 + 1, SD, 1, T_FFN1 - 3)
            norm_after(3, X_GMLP - KB, ((T_FFN1 + 2, SA), (T_FFN1 + 3, SB)), (y_lo, GB))
            take_root(ST_N3, D)
            copy_rows(ST_N3)
            ffn(1, T_FFN1, X_GMLP, None)

        def o_low(dve, p, q):
            r = 64 * (q // 2)
            cols = slice(q % 2 * HALF, (q % 2 + 1) * HALF)
            dve.wait_ge(o_hi, 4 * p + (q + 1))
            dve.tensor_tensor(hl[r:r + 64, bass.ds(p + 4, 1), cols].rearrange("p a n -> p (a n)"), PS[3][r:r + 64, cols],
                              hh[r:r + 64, bass.ds(p + 4, 1), cols].rearrange("p a n -> p (a n)").bitcast(F32),
                              ALU.subtract).then_inc(o_lo, 1)

        @block.vector
        def _(dve):
            def split(t, slot, raw_slot):
                dve.wait_ge(w_hi, t + 1)
                dve.tensor_tensor(wl[:, slot, :], raw[:, raw_slot, :], wh[:, slot, :].bitcast(F32), ALU.subtract).then_inc(w_lo, 1)

            def norm_lo(n, m, pos):
                dve.wait_ge(n_hi, 8 * n + pos + 1)
                dve.scalar_tensor_tensor(out=hl[:, m, :], in0=x[:, m, :], scalar=col(NORM_G[n] + m),
                                         in1=hh[:, m, :].bitcast(F32), op0=ALU.mult, op1=ALU.subtract).then_inc(n_lo, 1)

            def inverse(st):
                dve.wait_ge(st_root, st + 1)
                dve.reciprocal(rcol[:], root[:]).then_inc(st_rcol, 1)
                dve.wait_ge(st_rcol, st + 1)
                dve.tensor_tensor(tG[:, 2:2 + S].rearrange("p (t n) -> p t n", t=TB),
                                  ident[:].unsqueeze(1).broadcast_to([P, TB, P]),
                                  rcol[:].unsqueeze(2).broadcast_to([P, TB, P]), ALU.mult).then_inc(st_diag, 1)

            dve.wait_ge(par_in, 16)
            for m in range(KB):
                norm_lo(0, m, m)
                if m in (1, 3):
                    split(m // 2, m // 2, m // 2)
            dve.wait_ge(pos_copied, 1)
            dve.wait_ge(pos_in, 32)
            for b in range(GB):
                g = b // 2
                dve.scalar_tensor_tensor(out=sBt[:, b, :], in0=rstdB[:, g * P:(g + 1) * P], scalar=col(C_GB + b),
                                         in1=sbsp[:, g * P:(g + 1) * P], op0=ALU.mult, op1=ALU.add).then_inc(pos_bias, 1)
            dve.wait_ge(const, 5)
            inverse(ST_N0)

            def taps(m, k0, k1):
                n0 = m * (TAPS - 2)
                src = cv[:, m, :]
                for k in range(k0, k1):
                    acc = cv[:, (m + CB) % (CB + 1), LEFT:LEFT + S] if k % 2 == 0 else tG[:, 2:2 + S]
                    if k < 4:
                        dve.wait_ge(cv_first, 2 * m + k - 1)
                    else:
                        dve.wait_ge(cv_tap, n0 + k - 3)
                    dve.scalar_tensor_tensor(out=acc, in0=src[:, k:k + S], scalar=col(C_CONVW + m * TAPS + k),
                                             in1=acc, op0=ALU.mult, op1=ALU.add).then_inc(cv_tap, 1)

            def join(m):
                acc = cv[:, (m + CB) % (CB + 1), LEFT:LEFT + S]
                dve.wait_ge(cv_tap, (m + 1) * (TAPS - 2))
                dve.tensor_tensor(acc, acc, tG[:, 2:2 + S], ALU.add).then_inc(cv_done, 1)

            dve.wait_ge(st_rb, 1)
            dve.wait_ge(cv_pad, 1)
            for m in range(CB):
                dve.wait_ge(w_used, 2 * m + 1)
                if m:
                    dve.wait_ge(glu, m)
                dve.tensor_tensor(tC[:], PS[0][:], rstdB[:], ALU.mult).then_inc(lin_out, 1)
                split(2 * m + 2, SA, 0)
                if m == 1:
                    taps(0, 2, 8)
                if m == 2:
                    taps(0, 14, 20)
                if m == 3:
                    taps(0, 26, 31)
                    join(0)
                dve.wait_ge(w_used, 2 * m + 2)
                dve.tensor_tensor(tU[:], PS[1][:], rstdB[:], ALU.mult).then_inc(gate_out, 1)
                split(2 * m + 3, SB, 1)
                dve.wait_ge(sig, m + 1)
                dve.wait_ge(lin_out, m + 1)
                dve.tensor_tensor(cv[:, m, LEFT:LEFT + S], tC[:], tU[:], ALU.mult).then_inc(glu, 1)
                if m == 1:
                    taps(0, 8, 14)
                if m == 2:
                    taps(0, 20, 26)
                if m == 3:
                    taps(1, 2, 5)
            plan = [[(1, 5, 14)], [(1, 14, 23)], [(1, 23, 31), (1, 0, 0)], [(2, 2, 4)],
                    [(2, 4, 12)], [(2, 12, 20)], [(2, 20, 28)], [(2, 28, 31), (2, 0, 0), (3, 2, 4)],
                    [(3, 4, 13)], [(3, 13, 22)], [(3, 22, 31), (3, 0, 0)], []]
            for q in range(12):
                t = T_QKV + 2 + q
                if q in (4, 8):
                    c = q // 4 - 1
                    for j in range(4):
                        dve.wait_ge(qk_sq, 4 * c + j + 1)
                        dve.tensor_reduce(ssq[:, (4 * c + j) * 16:(4 * c + j + 1) * 16],
                                          (tC, tU)[j % 2][:].rearrange("p (g d) -> p g d", d=HD), AX.X, ALU.add).then_inc(qk_sum, 1)
                split(t, (t - T_QKV) % 4, t % 2)
                for m, k0, k1 in plan[q]:
                    if k1:
                        taps(m, k0, k1)
                    else:
                        join(m)
            dve.wait_ge(qk_root, 1)
            dve.reciprocal(rqk[:], rqk[:]).then_inc(qk_rinv, 1)

            dve.wait_ge(tok_free, 8 + 24)
            dve.wait_ge(qg_ready, 1)
            with dve.Fori(0, NPAIR) as p:
                dve.wait_ge(qt_hi, 3 * p + 1)
                dve.scalar_tensor_tensor(out=qtl[:], in0=PS[0][:], scalar=qgs[:, 0:1], in1=qth[:].bitcast(F32),
                                         op0=ALU.mult, op1=ALU.subtract).then_inc(qt_lo, 1)
                dve.wait_ge(qt_hi, 3 * p + 2)
                dve.scalar_tensor_tensor(out=ktl[:], in0=PS[1][:], scalar=col(C_KG), in1=kth[:].bitcast(F32),
                                         op0=ALU.mult, op1=ALU.subtract).then_inc(qt_lo, 1)
                dve.wait_ge(qt_hi, 3 * p + 3)
                dve.tensor_tensor(vl[:], vraw[:, :, bass.ts(p, P)], vh[:].bitcast(F32), ALU.subtract).then_inc(qt_lo, 1)

                def inv(u):
                    dve.wait_ge(exp_done, 16 * p + (u + 1))
                    dve.wait_ge(p_diag, 16 * p + u)
                    dve.reciprocal(rinv[:, u % 2:u % 2 + 1], rsum[:, u % 2:u % 2 + 1]).then_inc(p_inv, 1)
                    dve.wait_ge(p_inv, 16 * p + (u + 1))
                    dve.tensor_scalar(diagp[:, u % 2, :], ident[:], rinv[:, u % 2:u % 2 + 1], None, ALU.mult).then_inc(p_diag, 1)

                for step in range(17):
                    if step >= 1:
                        inv(step - 1)
                    if step < 16:
                        u = step
                        w = min(u % TB + 1, 5) * P
                        dve.wait_ge(sc_done, 16 * p + (u + 1))
                        if u in (0, 8):
                            dve.wait_ge(bias_ok, 4 * p + (2 + u // 4))
                        if u >= 2:
                            dve.wait_ge(pt_done, 16 * p + (u - 1))
                        dve.sem_inc(sc_seen, 1)
                        dve.tensor_tensor_reduce(prob[:, u % 2, 0:w], PS[u % 2][:, 0:w], bias[:, u // TB, BANDW - w:BANDW],
                                                 -1.0, 3e38, ALU.add, ALU.min, negmax[:, u % 2:u % 2 + 1]).then_inc(sc_max, 1)
                    if step >= 1:
                        u = step - 1
                        w = min(u % TB + 1, 5) * P
                        dve.wait_ge(pt_hi, 16 * p + (u + 1))
                        dve.tensor_tensor(ptl[:, u % 2, 0:w], PS[2][:, 0:w], pth[:, u % 2, 0:w].bitcast(F32),
                                          ALU.subtract).then_inc(pt_lo, 1)
                        if u >= 5 and u % 4 == 1:
                            o_low(dve, p, u // 4 - 1)
                o_low(dve, p, 3)

            def conv_out(m):
                return cv[:, (m + CB) % (CB + 1), LEFT:LEFT + S]

            def add_x(n, last_used=None):
                if n % 2:
                    dve.wait_ge(w_used, T_OUT + n // 2 + 1)
                else:
                    dve.wait_ge(m_done, n // 2 + 1)
                m = n % KB
                dve.wait_ge(x_in[m], 32)
                if n >= KB:
                    dve.wait_ge(x_add, n - KB + 1)
                dve.tensor_tensor(x[:, m, :], x[:, m, :], PS[n % 2][:], ALU.add).then_inc(x_add, 1)

            dve.wait_ge(ln_mean, 1)
            for m in range(CB):
                dve.scalar_tensor_tensor(out=conv_out(m), in0=PS[2][:], scalar=-1.0 / CONVW, in1=conv_out(m),
                                         op0=ALU.mult, op1=ALU.add).then_inc(ln_cent, 1)
            add_x(0)
            add_x(1)
            split(T_OUT + 2, SA, 0)
            dve.wait_ge(cv_done, CB)
            inverse(ST_LN)
            add_x(2)
            add_x(3)
            split(T_OUT + 3, SB, 1)
            dve.wait_ge(st_rb, ST_LN + 1)
            for m in range(CB):
                dve.tensor_tensor(conv_out(m), conv_out(m), rstdB[:], ALU.mult).then_inc(ln_mul, 1)
            add_x(4)
            for m in range(CB):
                dve.wait_ge(ln_hi, m + 1)
                dve.tensor_tensor(hl[:, m, :], conv_out(m), hh[:, m, :].bitcast(F32), ALU.subtract).then_inc(ln_lo, 1)
                if m == 1:
                    add_x(5)
            split(T_OUT + 4, SA, 0)
            add_x(6)
            add_x(7)
            split(T_OUT + 5, SB, 1)
            add_x(8)
            add_x(9)
            split(T_OUT + 6, SA, 0)
            add_x(10)
            add_x(11)
            split(T_OUT + 7, SB, 1)
            split(T_FFN0, SC, 0)
            split(T_FFN0 + 1, SD, 1)
            add_x(12)
            add_x(13)
            split(T_FFN0 + 2, SA, 0)
            add_x(14)
            norm_lo(1, 4, 0)
            norm_lo(1, 5, 1)
            add_x(15)
            for pos in range(2, 8):
                norm_lo(1, NORM_ORDER[1][pos], pos)
            split(T_FFN0 + 3, SB, 1)
            inverse(ST_N1)

            def add_block(m, x0, done0, used):
                if m < KB - 1:
                    dve.wait_ge(m_done, done0 + (m + 1))
                else:
                    dve.wait_ge(w_used, used)
                dve.wait_ge(x_add, x0 + (m - 7))
                dve.tensor_tensor(x[:, m, :], x[:, m, :], PS[2 + m % 2][:], ALU.add).then_inc(x_add, 1)

            M_OUT = 8

            def ffn(f, t0, x0, done0):
                b0 = FB * f
                dve.wait_ge(st_rb, (ST_N1, ST_N3)[f] + 1)
                dw0 = C_DW + 4 * FB * f

                def gate(b, used, f0):
                    dve.wait_ge(w_used, used)
                    dve.wait_ge(g_tap0, b + b0)
                    dve.tensor_tensor(tG[:, 2:2 + S], PS[0][:], rstdB[:], ALU.mult).then_inc(g_out, 1)
                    dw = par[:, bass.ds(f0, 4)]
                    dve.wait_ge(g_tap2, b + (b0 + 1))
                    dve.scalar_tensor_tensor(out=tC[:], in0=tG[:, 1:1 + S], scalar=dw[:, 1:2], in1=tC[:],
                                             op0=ALU.mult, op1=ALU.add).then_inc(g_tap1, 1)
                    dve.wait_ge(g_tap1, b + (b0 + 1))
                    dve.scalar_tensor_tensor(out=tC[:], in0=tG[:, 0:S], scalar=dw[:, 0:1], in1=tC[:],
                                             op0=ALU.mult, op1=ALU.add).then_inc(g_tap0, 1)

                def up(b, used):
                    dve.wait_ge(w_used, used)
                    dve.wait_ge(hid_lo, b + b0)
                    dve.tensor_tensor(tU[:], PS[1][:], rstdB[:], ALU.mult).then_inc(up_out, 1)
                    dve.wait_ge(up_out, b + (b0 + 1))
                    dve.wait_ge(g_silu, b + (b0 + 1))
                    dve.tensor_tensor(tU[:], tU[:], tC[:], ALU.mult).then_inc(hid, 1)

                def low(b, slot):
                    dve.wait_ge(hid_hi, b + (b0 + 1))
                    dve.tensor_tensor(hidl[:, slot, :], tU[:], hidh[:, slot, :].bitcast(F32), ALU.subtract).then_inc(hid_lo, 1)

                gate(0, t0 + 1, dw0)
                up(0, t0 + 2)
                low(0, 0)
                gate(1, t0 + 3, dw0 + 4)
                split(t0 + 4, SA, 0)
                up(1, t0 + 4)
                split(t0 + 5, SB, 1)
                low(1, 1)

                def group(i, odd):
                    t = 6 * i + (t0 - 2)
                    xg, dg = 8 * i + (x0 - 8), 7 * i + (done0 - 7)
                    split(t + 2, SA, 0)
                    gate(2 * i, t + 1, 8 * i + dw0)
                    split(t + 3, SB, 1)
                    up(2 * i, t + 2)
                    low(2 * i, 2 * odd)
                    split(t + 4, SC, 0)
                    split(t + 5, SD, 1)
                    gate(2 * i + 1, t + 3, 8 * i + (dw0 + 4))
                    split(t + 6, SA, 0)
                    up(2 * i + 1, t + 4)
                    split(t + 7, SB, 1)
                    add_block(0, xg, dg, None)
                    low(2 * i + 1, 2 * odd + 1)
                    for m in range(1, KB):
                        add_block(m, xg, dg, t + 6)

                with dve.Fori(0, FG // 2) as ii:
                    group(2 * ii + 1, 1)
                    group(2 * ii + 2, 0)

            def last_group(n, x0, done0, used, tail):
                for m in range(KB):
                    add_block(m, x0, done0, used)
                    if n is not None and m:
                        norm_lo(n, m - 1, m - 1)
                if n is not None:
                    norm_lo(n, KB - 1, KB - 1)
                for t, slot in tail:
                    split(t, slot, t % 2)

            ffn(0, T_FFN0, X_OUT, M_OUT)
            M_FFN0 = M_OUT + 7 * FG
            split(T_GMLP, SC, 0)
            split(T_GMLP + 1, SD, 1)
            last_group(2, X_FFN0 - 8, M_FFN0 - 7, T_GMLP, ((T_V, SA), (T_V + 1, SB)))
            dve.wait_ge(g_tap0, FB)
            inverse(ST_N2)
            dve.wait_ge(wsp_hi, 1)
            dve.tensor_tensor(wspl[:], wspr[:], wsph[:].bitcast(F32), ALU.subtract).then_inc(wsp_lo, 1)
            dve.wait_ge(st_rb, ST_N2 + 1)
            for j in range(2):
                dve.wait_ge(w_used, T_GMLP + 1 + j)
                dve.tensor_tensor(uearly[:, j, :], PS[j][:], rstdB[:], ALU.mult).then_inc(u_out, 1)
            with dve.Fori(0, 4) as c:
                for q in range(4):
                    split(4 * c + (T_V + 2 + q), (2 + q) % 4, q % 2)
                for pos, tok in enumerate(SWEEP):
                    dve.wait_ge(v_gelu, 8 * c + (pos + 1))
                    dve.bn_stats(vstat[:, tok, bass.ds(c, 1), :].rearrange("p a n -> p (a n)"), vst[:, pos % 4, :]).then_inc(v_stat, 1)
            dve.wait_ge(v_stat, 32)
            for t in range(TB):
                mm = dve.bn_aggr(mv[:, 2 * t:2 * t + 2], vstat[:, t, :, :].rearrange("p a n -> p (a n)"))
            mm.then_inc(v_mv, 1)
            dve.wait_ge(v_root, 1)
            dve.reciprocal(rcol[:], root[:]).then_inc(v_rs, 1)
            dve.wait_ge(v_rs, 1)

            def vn_full(b):
                dve.wait_ge(v_in, 16 * b + 16)
                for t in range(TB):
                    ts = dve.tensor_scalar(tA[:, t * P:(t + 1) * P], tA[:, t * P:(t + 1) * P], mv[:, 2 * t:2 * t + 1],
                                           rcol[:, t:t + 1], ALU.subtract, ALU.mult)
                ts.then_inc(vn_f, 1)

            def vn_low(b):
                dve.wait_ge(vn_f, b + 1)
                dve.wait_ge(vn_hi, b + 1)
                dve.tensor_tensor(vnl[:], tA[:], vnh[:].bitcast(F32), ALU.subtract).then_inc(vn_lo, 1)

            def mixed(b, j, ih):
                dve.wait_ge(sv_done, b + 1)
                dve.wait_ge(b_in[j], ih * 16 + 16)
                dve.wait_ge(y_lo, b)
                dve.scalar_tensor_tensor(out=tC[:].rearrange("p (c t) -> p c t", c=TB),
                                         in0=PS[2 + j][:].rearrange("p (c t) -> p c t", c=TB), scalar=par[:, bass.ds(b + C_GG, 1)],
                                         in1=bblk[:, j * P:(j + 1) * P].unsqueeze(1).broadcast_to([P, TB, P]),
                                         op0=ALU.mult, op1=ALU.add).then_inc(sv_out, 1)

            def y_full(b, u):
                dve.wait_ge(sv_out, b + 1)
                dve.wait_ge(u_gelu, b + 1)
                dve.tensor_tensor(tC[:], tC[:], u, ALU.mult).then_inc(y_f, 1)

            def y_low(b, slot):
                dve.wait_ge(y_hi, b + 1)
                dve.tensor_tensor(hidl[:, slot, :], tC[:], hidh[:, slot, :].bitcast(F32), ALU.subtract).then_inc(y_lo, 1)

            for q in range(4):
                dve.wait_ge(v_out[q], 16 * 8)
            vn_full(0)
            vn_low(0)
            vn_full(1)
            vn_low(1)
            mixed(0, 0, 0)
            y_full(0, uearly[:, 0, :])
            y_low(0, 0)
            vn_full(2)
            vn_low(2)
            mixed(1, 1, 0)
            y_full(1, uearly[:, 1, :])
            y_low(1, 1)

            def gmlp_group(i, odd, last=False):
                t = 4 * i + (T_GLOOP - 4)
                xg, dg = 8 * i + (X_FFN0 - 8), 7 * i + (M_FFN0 - 7)
                split(t + 2, SC, 0)
                split(t + 3, SD, 1)
                mixed(2 * i, 0, i)
                vn_full(2 * i + 1)
                vn_low(2 * i + 1)
                split(t + 4, SA, 0)
                dve.wait_ge(w_used, t + 1)
                dve.wait_ge(y_f, 2 * i)
                dve.tensor_tensor(tU[:], PS[0][:], rstdB[:], ALU.mult).then_inc(u_out, 1)
                y_full(2 * i, tU[:])
                y_low(2 * i, 2 * odd)
                mixed(2 * i + 1, 1, i)
                split(t + 5, SB, 1)
                dve.wait_ge(w_used, t + 2)
                dve.wait_ge(y_f, 2 * i + 1)
                dve.tensor_tensor(tU[:], PS[1][:], rstdB[:], ALU.mult).then_inc(u_out, 1)
                y_full(2 * i + 1, tU[:])
                y_low(2 * i + 1, 2 * odd + 1)
                add_block(0, xg, dg, None)
                if not last:
                    vn_full(2 * i + 2)
                add_block(1, xg, dg, None)
                if not last:
                    vn_low(2 * i + 2)
                for m in range(2, KB):
                    add_block(m, xg, dg, t + 4)

            with dve.Fori(0, (GG - 2) // 2) as ii:
                gmlp_group(2 * ii + 1, 1)
                gmlp_group(2 * ii + 2, 0)
            gmlp_group(GG - 1, 1, last=True)
            M_GMLP = M_FFN0 + 7 * GG
            split(T_FFN1, SC, 0)
            split(T_FFN1 + 1, SD, 1)
            last_group(3, X_GMLP - 8, M_GMLP - 7, T_FFN1, ((T_FFN1 + 2, SA), (T_FFN1 + 3, SB)))
            inverse(ST_N3)
            ffn(1, T_FFN1, X_GMLP, M_GMLP)
            last_group(None, X_GMLP + 8 * (FG - 1), M_GMLP + 7 * (FG - 1), NT, ())


def lay_out(inputs):
    f = {k: np.asarray(v) for k, v in inputs.items()}

    def columns(a):
        return np.moveaxis(a.reshape(a.shape[:-1] + (-1, P)), -1, 0).reshape(P, -1)

    def feature_tiles(w):
        return w.reshape(KB, P, -1, P).transpose(2, 1, 0, 3).reshape(-1, P, 1024)

    def token_tiles(w):
        return w.reshape(4, 2, P, -1, HALF).transpose(3, 0, 2, 1, 4).reshape(-1, P, 1024)

    def half_tiles(w):
        return w.reshape(4, P, 4, 256).transpose(2, 1, 0, 3).reshape(4, P, 1024)

    def interleave(*tiles):
        return np.stack(tiles, 1).reshape(-1, P, 1024)

    def pipelined(ups, downs):
        parts = [ups[0]]
        for i in range(1, len(ups)):
            parts += [ups[i], downs[i - 1]]
        return parts + [downs[-1]]

    w_in = f["w_in_e"][0]
    glu = interleave(feature_tiles(w_in[:, 0:CONVW]), feature_tiles(w_in[:, CONVW:2 * CONVW]))
    stream = [glu, token_tiles(w_in[:, 2 * CONVW:]),
              half_tiles(f["w_out_e"][0][CONVW:]), half_tiles(f["w_out_e"][0][:CONVW])]

    def ffn(layer):
        gu = interleave(feature_tiles(f["w_gate"][layer]), feature_tiles(f["w_up"][layer])).reshape(FG, 4, P, 1024)
        return pipelined(gu, f["w_down"][layer].reshape(FG, 2, P, 1024))

    w_io = f["w_in_o"][0]
    u = feature_tiles(w_io[:, 0:2048]).reshape(GG, 2, P, 1024)
    gm = pipelined(u, f["w_out_o"][0].reshape(GG, 2, P, 1024))
    stream += ffn(0) + [gm[0], token_tiles(w_io[:, 2048:])] + gm[1:] + ffn(1)
    dw = np.concatenate([f["ffn_dw_w"], f["ffn_dw_b"][:, None, :]], 1).transpose(0, 2, 1)
    dw = dw.reshape(2, FB, P, 4).transpose(2, 0, 1, 3).reshape(P, -1)
    cw = f["conv_w"][0].reshape(TAPS, CB, P).transpose(2, 1, 0).reshape(P, -1)
    params = np.concatenate([
        columns(f["mix_norm_g"]), columns(f["ffn_norm_g"]), cw, columns(f["conv_b"][0]), columns(f["conv_ln_g"][0]),
        columns(f["conv_ln_b"][0]), np.tile(f["qn_g"][0], 2)[:, None], np.tile(f["kn_g"][0], 2)[:, None],
        columns(f["gate_ln_g"][0]), columns(f["gate_ln_b"][0]), dw], 1)
    c = np.ascontiguousarray
    return {
        "xT": c(f["x"][0].T),
        "wstream": np.concatenate(stream, 0),
        "params": c(params),
        "rel": c(f["rel_bias"][0][:, ::-1]),
        "wsp": c(f["w_sp"][0].transpose(2, 0, 1).reshape(P, -1)),
        "bsp": c(f["b_sp"][0].reshape(1, -1)[0]),
    }


def kernel(**inputs):
    import concourse.bacc as bacc
    from concourse.bass_utils import run_bass_kernel_spmd

    arrays = lay_out(inputs)
    nc = bacc.Bacc("TRN2", target_bir_lowering=False, num_devices=1)
    args = {k: nc.dram_tensor(k, a.shape, mybir.dt.from_np(a.dtype), kind="ExternalInput").ap() for k, a in arrays.items()}
    outT = nc.dram_tensor("outT", [D, S], F32, kind="ExternalOutput").ap()
    program(nc, **args, outT=outT)
    r = run_bass_kernel_spmd(nc, [arrays], core_ids=[0])
    return np.ascontiguousarray(r.results[0]["outT"].T)[None]
```

```python
from contextlib import ExitStack

import numpy as np

import concourse.bass as bass
from concourse import mybir

ALU = mybir.AluOpType
ACT = mybir.ActivationFunctionType
AX = mybir.AxisListType
F32 = mybir.dt.float32
F32R = mybir.dt.float32r

P = 128
D = 1024
S = 1024
HALF = 512
KB = D // P
TB = S // P
EPS = 1e-6

CONVW = 512
CB = CONVW // P
TAPS = 31
LEFT = TAPS - 1
CVW = 1056
NH, HD = 8, 64
NPAIR = NH // 2
BANDW = 640
NREL = 320
RELW = 768
MASKED = -1e30

FB = 2816 // P
FG = FB // 2
GB = 2048 // P
GG = GB // 2

T_QKV = 2 * CB
T_OUT = T_QKV + 12
T_FFN0 = T_OUT + 8
T_GMLP = T_FFN0 + 3 * FB
T_V = T_GMLP + 2
T_GLOOP = T_V + 16
T_FFN1 = T_GMLP + 3 * GB
NT = T_FFN1 + 3 * FB
SA, SB, SC, SD = range(4)

C_MIXG = 0
C_FFNG = C_MIXG + 2 * KB
C_CONVW = C_FFNG + 2 * KB
C_CONVB = C_CONVW + CB * TAPS
C_LNG = C_CONVB + CB
C_LNB = C_LNG + CB
C_QG = C_LNB + CB
C_KG = C_QG + 1
C_GG = C_KG + 1
C_GB = C_GG + GB
C_DW = C_GB + GB
NPAR = C_DW + 2 * FB * 4

ST_N0, ST_LN, ST_N1, ST_N2, ST_N3 = range(5)
NORM_G = [C_MIXG, C_FFNG, C_MIXG + KB, C_FFNG + KB]
NORM_ORDER = [list(range(8)), [4, 5, 0, 1, 2, 3, 6, 7], list(range(8)), list(range(8))]

SWEEP = [4, 5, 6, 7, 0, 1, 2, 3]


def program(nc, xT, wstream, params, rel, wsp, bsp, outT):
    with ExitStack() as ctx:
        base = nc.sbuf_base
        base = (base + 31) // 32 * 32

        def at(name, offset, shape, dt):
            return nc.alloc_sbuf_tensor_at(name, shape, dt, offset=base + offset)

        def sem(name):
            return ctx.enter_context(nc.semaphore(name))

        KiB = 1024
        o_x, o_hh, o_hl, o_hid, o_raw = 0, 32 * KiB, 64 * KiB, 96 * KiB, 128 * KiB
        o_wh, o_wl = 136 * KiB, 152 * KiB
        o_rb, o_ta, o_tc, o_tu, o_tg = 168 * KiB, 172 * KiB, 176 * KiB, 180 * KiB, 184 * KiB
        o_vn = o_tg + 4128
        o_small = o_vn + 16 * KiB

        x = at("x", o_x, [P, KB, S], F32)
        hh = at("hh", o_hh, [P, KB, S], F32R)
        hl = at("hl", o_hl, [P, KB, S], F32R)
        hidh = at("hidh", o_hid, [P, 4, S], F32R)
        hidl = at("hidl", o_hid + 16 * KiB, [P, 4, S], F32R)
        raw = at("raw", o_raw, [P, 2, 1024], F32)
        wh = at("wh", o_wh, [P, 4, 1024], F32R)
        wl = at("wl", o_wl, [P, 4, 1024], F32R)
        rstdB = at("rstdB", o_rb, [P, S], F32)
        tA = at("tA", o_ta, [P, S], F32)
        tC = at("tC", o_tc, [P, S], F32)
        tU = at("tU", o_tu, [P, S], F32)
        tG = at("tG", o_tg, [P, S + 2], F32)
        vnh = at("vnh", o_vn, [P, S], F32R)
        vnl = at("vnl", o_vn + 4 * KiB, [P, S], F32R)
        wsph = at("wsph", o_vn + 8 * KiB, [P, S], F32R)
        wspl = at("wspl", o_vn + 12 * KiB, [P, S], F32R)
        qk = at("qk", o_x, [P, 2, TB, CONVW], F32)
        vraw = at("vraw", o_vn, [P, TB, CONVW], F32)
        cv = at("cv", o_hid, [P, CB + 1, CVW], F32)
        ptl = at("ptl", o_hid + 21120, [P, 2, BANDW], F32R)
        diagp = at("diagp", o_hid + 26240, [P, 3, P], F32)
        ssq = at("ssq", o_hid + 27776, [P, 2 * TB * NH], F32)
        rqk = at("rqk", o_hid + 28288, [P, 2 * TB * NH], F32)
        qgs = at("qgs", o_hid + 28800, [P, 1], F32)
        negmax = at("negmax", o_hid + 28832, [P, 3], F32)
        rsum = at("rsum", o_hid + 28864, [P, 3], F32)
        rinv = at("rinv", o_hid + 28896, [P, 3], F32)
        qth = at("qth", o_hh, [P, S], F32R)
        qtl = at("qtl", o_hh + 4 * KiB, [P, S], F32R)
        kth = at("kth", o_hh + 8 * KiB, [P, S], F32R)
        ktl = at("ktl", o_hh + 12 * KiB, [P, S], F32R)
        vh = at("vh", o_hl, [P, TB, P], F32R)
        vl = at("vl", o_hl + 4 * KiB, [P, TB, P], F32R)
        bias = at("bias", o_hl + 8 * KiB, [P, 2, BANDW], F32)
        prob = at("prob", o_wh + 8 * KiB, [P, 3, BANDW], F32)
        pth = at("pth", o_wl + 8 * KiB, [P, 2, BANDW], F32R)
        sBt = at("sBt", o_vn, [P, GB, P], F32)
        swsp = at("swsp", o_vn + 8 * KiB, [P, S], F32)
        sbsp = at("sbsp", o_vn + 12 * KiB, [P, S], F32)
        etab = at("etab", o_hid, [NH, RELW], F32)
        uearly = at("uearly", o_hid + 8 * KiB, [P, 2, S], F32)
        vst = at("vst", o_hid + 16 * KiB, [P, TB, HALF], F32)
        wspr = at("wspr", o_hid, [P, S], F32)

        s_off = [o_small]

        def small(name, cols, dt=F32):
            t = at(name, s_off[0], [P, cols], dt)
            s_off[0] += (cols * 4 + 31) // 32 * 32
            return t

        par = small("par", NPAR)
        ident = small("ident", P)
        ones = small("ones", P)
        bblk = small("bblk", 2 * P)
        rcol = small("rcol", TB)
        root = small("root", TB)
        epsc = small("epsc", 1)
        mv = small("mv", 2 * TB)
        vstat = at("vstat", o_vn, [P, TB, 4, 6], F32)

        PS = [ctx.enter_context(nc.psum_tensor(f"ps{i}", [P, 2 * HALF], F32)) for i in range(4)]

        def bank(tok):
            return PS[tok // 2][:, tok % 2 * HALF:(tok % 2 + 1) * HALF]

        e_dram = nc.dram_tensor("rel_rows", [NH, P, RELW], F32, kind="Internal").ap()
        v_dram = nc.dram_tensor("v_gelu", [S, 2048], F32, kind="Internal").ap()
        b_dram = nc.dram_tensor("pos_bias", [P, GB * P], F32, kind="Internal").ap()
        w_dram = nc.dram_tensor("pos_masked", [P, S], F32, kind="Internal").ap()
        v_blocks = v_dram.rearrange("(c s) d -> s c d", s=P)

        raw_in = [sem(f"raw_in{i}") for i in range(2)]
        w_hi, w_lo = sem("w_hi"), sem("w_lo")
        w_used = sem("w_used")
        x_in = [sem(f"x_in{i}") for i in range(KB)]
        par_in, rel_in, pos_in = sem("par_in"), sem("rel_in"), sem("pos_in")
        const = sem("const")
        e_ready, e_out = sem("e_ready"), sem("e_out")
        pos_masked, pos_rows, pos_copied = sem("pos_masked"), sem("pos_rows"), sem("pos_copied")
        pos_bias, pos_out = sem("pos_bias"), sem("pos_out")
        n_hi, n_lo, n_sq, n_sum = sem("n_hi"), sem("n_lo"), sem("n_sq"), sem("n_sum")
        st_sum, st_root, st_rcol = sem("st_sum"), sem("st_root"), sem("st_rcol")
        st_diag, st_row, st_rb = sem("st_diag"), sem("st_row"), sem("st_rb")
        lin_out, gate_out, sig, glu = sem("lin_out"), sem("gate_out"), sem("sig"), sem("glu")
        cv_pad, cv_first, cv_tap, cv_done = sem("cv_pad"), sem("cv_first"), sem("cv_tap"), sem("cv_done")
        tok_done, tok_free = sem("tok_done"), sem("tok_free")
        qk_sq, qk_sum, qk_root, qk_rinv = sem("qk_sq"), sem("qk_sum"), sem("qk_root"), sem("qk_rinv")
        qg_ready = sem("qg_ready")
        qn_ready, qt_done, qt_hi, qt_lo = sem("qn_ready"), sem("qt_done"), sem("qt_hi"), sem("qt_lo")
        bias_in = [sem(f"bias_in{i}") for i in range(2)]
        bias_ok = sem("bias_ok")
        sc_seen, bias_seen, v_seen = sem("sc_seen"), sem("bias_seen"), sem("v_seen")
        sc_done, sc_max, exp_done = sem("sc_done"), sem("sc_max"), sem("exp_done")
        p_inv, p_diag, pt_done = sem("p_inv"), sem("p_diag"), sem("pt_done")
        pt_hi, pt_lo, pv_done = sem("pt_hi"), sem("pt_lo"), sem("pv_done")
        o_hi, o_lo = sem("o_hi"), sem("o_lo")
        ln_sum0, ln_mean, ln_cent = sem("ln_sum0"), sem("ln_mean"), sem("ln_cent")
        ln_sq, ln_sum, ln_mul = sem("ln_sq"), sem("ln_sum"), sem("ln_mul")
        ln_act, ln_hi, ln_lo = sem("ln_act"), sem("ln_hi"), sem("ln_lo")
        m_done, x_add = sem("m_done"), sem("x_add")
        g_out, g_tap2, g_tap1, g_tap0 = sem("g_out"), sem("g_tap2"), sem("g_tap1"), sem("g_tap0")
        g_silu, up_out, hid, hid_hi, hid_lo = sem("g_silu"), sem("up_out"), sem("hid"), sem("hid_hi"), sem("hid_lo")
        wsp_in, wsp_hi, wsp_lo = sem("wsp_in"), sem("wsp_hi"), sem("wsp_lo")
        v_gelu, v_stat, v_mv, v_root, v_rs = sem("v_gelu"), sem("v_stat"), sem("v_mv"), sem("v_root"), sem("v_rs")
        v_out = [sem(f"v_out{i}") for i in range(TB)]
        v_in, b_in = sem("v_in"), [sem("b_in0"), sem("b_in1")]
        vn_f, vn_hi, vn_lo = sem("vn_f"), sem("vn_hi"), sem("vn_lo")
        sv_done, sv_out, u_out, u_gelu = sem("sv_done"), sem("sv_out"), sem("u_out"), sem("u_gelu")
        y_f, y_hi, y_lo = sem("y_f"), sem("y_hi"), sem("y_lo")
        out_done = sem("out_done")

        X_OUTA, X_OUT = 8, 16
        X_FFN0 = X_OUT + FG * KB
        X_GMLP = X_FFN0 + GG * KB
        X_END = X_GMLP + FG * KB

        def unit(u):
            t = u % TB
            return t, 64 * (u // TB), min(t + 1, 5) * P, max(0, t - 4) * P

        block = ctx.enter_context(nc.Block())

        def col(c):
            return par[:, c:c + 1]

        @block.sync
        def _(sp):
            def tile(t, slot):
                sp.wait_ge(w_lo, t - 1)
                sp.dma_start(raw[:, slot, :], wstream[t]).then_inc(raw_in[slot], 16)

            sp.dma_start(par[:], params).then_inc(par_in, 16)
            for m in range(KB):
                sp.dma_start(x[:, m, :], xT[m * P:(m + 1) * P, :]).then_inc(x_in[m], 16)
                if m == 0:
                    sp.dma_start(raw[:, 0, :], wstream[0]).then_inc(raw_in[0], 16)
                if m == 2:
                    sp.dma_start(raw[:, 1, :], wstream[1]).then_inc(raw_in[1], 16)
            sp.dma_start(etab[:, 383:383 + NREL], rel).then_inc(rel_in, 16)
            sp.dma_start(swsp[:], wsp).then_inc(pos_in, 16)
            sp.dma_start(sbsp[:], bsp.partition_broadcast(P)).then_inc(pos_in, 16)
            sp.wait_ge(e_ready, 2)
            sp.dma_start(e_dram, etab[:].unsqueeze(1).broadcast_to([NH, P, RELW])).then_inc(e_out, 16)
            sp.wait_ge(pos_masked, 1)
            sp.dma_start(w_dram, swsp[:]).then_inc(pos_out, 16)
            sp.wait_ge(pos_bias, GB)
            sp.dma_start(b_dram, sBt[:].rearrange("p b t -> p (b t)")).then_inc(pos_out, 16)
            with sp.Fori(1, (T_OUT + 2) // 2) as i:
                tile(2 * i, 0)
                tile(2 * i + 1, 1)
            sp.wait_ge(e_out, 16)
            sp.wait_ge(w_used, T_OUT)
            for p in range(NPAIR):
                for hd in range(2):
                    if p:
                        sp.wait_ge(sc_max, 16 * (p - 1) + 8 * hd + 8)
                    rows = bass.AP(tensor=e_dram.tensor, offset=(2 * p + hd) * P * RELW + P - 1,
                                   ap=[[RELW - 1, P], [1, BANDW]])
                    sp.dma_start(bias[:, hd, :], rows).then_inc(bias_in[hd], 16)
            sp.wait_ge(qn_ready, 2 * NPAIR)
            for m in range(KB):
                sp.dma_start(x[:, m, :], xT[m * P:(m + 1) * P, :]).then_inc(x_in[m], 16)
            with sp.Fori((T_OUT + 2) // 2, (T_FFN0 + 4) // 2) as i:
                tile(2 * i, 0)
                tile(2 * i + 1, 1)
            with sp.Fori((T_FFN0 + 4) // 2, (T_GMLP + 2) // 2) as i:
                tile(2 * i, 0)
                tile(2 * i + 1, 1)
            sp.wait_ge(pos_out, 32)
            sp.wait_ge(x_add, X_FFN0)
            sp.dma_start(wspr[:], w_dram).then_inc(wsp_in, 16)
            tile(T_V, 0)
            tile(T_V + 1, 1)
            with sp.Fori(0, 4) as c:
                for q in range(4):
                    tile(4 * c + (T_V + 2 + q), q % 2)
                for pos, tok in enumerate(SWEEP):
                    sp.wait_ge(v_gelu, 8 * c + (pos + 1))
                    sp.sem_inc(v_seen, 1)
                    sp.dma_start(v_dram[tok * P:(tok + 1) * P, bass.ts(c, HALF)], vst[:, pos, :]).then_inc(v_out[pos], 16)
            for s in v_out:
                sp.wait_ge(s, 16 * 4)

            def vblock(b, j):
                sp.wait_ge(vn_lo, b)
                sp.dma_start(tA[:].rearrange("p (c d) -> p c d", c=TB),
                             v_blocks[:, :, bass.ts(b, P)]).then_inc(v_in, 16)
                sp.wait_ge(sv_out, b - 1)
                sp.dma_start(bblk[:, j * P:(j + 1) * P], b_dram[:, bass.ts(b, P)]).then_inc(b_in[j], 16)

            sp.wait_ge(st_row, ST_N2 + 1)
            sp.dma_start(tA[:].rearrange("p (c d) -> p c d", c=TB), v_blocks[:, :, 0:P]).then_inc(v_in, 16)
            sp.dma_start(bblk[:, 0:P], b_dram[:, 0:P]).then_inc(b_in[0], 16)
            tile(T_GLOOP + 2, 0)
            vblock(1, 1)
            tile(T_GLOOP + 3, 1)
            tile(T_GLOOP + 4, 0)
            vblock(2, 0)
            tile(T_GLOOP + 5, 1)
            vblock(3, 1)
            with sp.Fori(2, GG) as i:
                tile(4 * i + (T_GLOOP - 2), 0)
                vblock(2 * i, 0)
                tile(4 * i + (T_GLOOP - 1), 1)
                tile(4 * i + T_GLOOP, 0)
                tile(4 * i + (T_GLOOP + 1), 1)
                vblock(2 * i + 1, 1)
            with sp.Fori(T_FFN1 // 2, (T_FFN1 + 4) // 2) as i:
                tile(2 * i, 0)
                tile(2 * i + 1, 1)
            with sp.Fori((T_FFN1 + 4) // 2, NT // 2) as i:
                tile(2 * i, 0)
                tile(2 * i + 1, 1)
            for m in range(KB):
                sp.wait_ge(x_add, X_END - KB + m + 1)
                sp.dma_start(outT[m * P:(m + 1) * P, :], x[:, m, :]).then_inc(out_done, 16)
            sp.wait_ge(out_done, 16 * KB)

        @block.gpsimd
        def _(pool):
            pool.memset(ones[:], 1.0).then_inc(const, 1)
            pool.memset(epsc[:], EPS).then_inc(const, 1)
            pool.memset(ident[:], 0.0).then_inc(const, 1)
            pool.wait_ge(const, 3)
            pool.affine_select(out=ident[:], in_=ident[:], compare_op=ALU.not_equal, fill=1.0, base=0,
                               pattern=[[-1, P]], channel_multiplier=1).then_inc(const, 1)
            pool.memset(tG[:, 0:2], 0.0).then_inc(const, 1)

            def norm_sums(n):
                for m in range(1, KB):
                    pool.wait_ge(n_sq, 8 * n + m + 1)
                    if m > 1:
                        pool.wait_ge(n_sum, 7 * n + m - 1)
                    pool.tensor_tensor(tA[:], tA[:], (tC, tU)[m % 2][:], ALU.add).then_inc(n_sum, 1)

            norm_sums(0)
            pool.memset(etab[:, 383 + NREL:RELW], 0.0).then_inc(e_ready, 1)
            pool.wait_ge(rel_in, 16)
            pool.tensor_copy(etab[:, 0:383], etab[:, 383:384].broadcast_to([NH, 383])).then_inc(e_ready, 1)
            pool.wait_ge(pos_in, 32)
            w3 = swsp[:].rearrange("s (g t) -> s g t", g=GG)
            pool.affine_select(out=w3, in_=w3, compare_op=ALU.is_ge, fill=0.0, base=0,
                               pattern=[[0, GG], [1, P]], channel_multiplier=-1).then_inc(pos_masked, 1)
            pool.wait_ge(e_out, 16)
            pool.memset(cv[:, 0:CB, 0:LEFT], 0.0).then_inc(cv_pad, 1)
            pool.wait_ge(qk_rinv, 1)
            rq4 = rqk[:].rearrange("p (c t h) -> p c t h", c=2, t=TB)
            pool.wait_ge(tok_free, 8 + 24)
            with pool.Fori(0, NPAIR) as p:
                for c, buf in ((0, tC), (1, tU)):
                    pool.tensor_tensor(
                        buf[:].rearrange("p (t h d) -> p t h d", t=TB, h=2),
                        qk[:, c, :, bass.ts(p, P)].rearrange("p t (h d) -> p t h d", h=2),
                        rq4[:, c, :, bass.ts(p, 2)].unsqueeze(3).broadcast_to([P, TB, 2, HD]),
                        ALU.mult).then_inc(qn_ready, 1)
                pool.wait_ge(qn_ready, 2 * p + 2)
                for hd in range(2):
                    pool.wait_ge(bias_in[hd], 16 * p + 16)
                    if hd:
                        pool.wait_ge(bias_ok, 4 * p + 2)
                    pool.sem_inc(bias_seen, 1)
                    pool.memset(bias[0:64, hd, BANDW - 64:BANDW], MASKED).then_inc(bias_ok, 1)
                    pool.wait_ge(bias_ok, 4 * p + (2 * hd + 1))
                    pool.sem_inc(bias_seen, 1)
                    pool.memset(bias[64:128, hd, 0:64], MASKED).then_inc(bias_ok, 1)
                pool.wait_ge(qt_done, 2 * p + 2)
                pool.wait_ge(bias_ok, 4 * p + 4)

            def conv_out(m):
                return cv[:, (m + CB) % (CB + 1), LEFT:LEFT + S]

            pool.wait_ge(cv_done, CB)
            pool.wait_ge(bias_ok, 4 * NPAIR)
            for m in range(1, CB):
                if m > 1:
                    pool.wait_ge(ln_sum0, m - 1)
                pool.tensor_tensor(tA[:], conv_out(0) if m == 1 else tA[:], conv_out(m), ALU.add).then_inc(ln_sum0, 1)
            for m in range(1, CB):
                pool.wait_ge(ln_sq, m + 1)
                if m > 1:
                    pool.wait_ge(ln_sum, m - 1)
                pool.tensor_tensor(tA[:], tA[:], (tC, tU)[m % 2][:], ALU.add).then_inc(ln_sum, 1)
            norm_sums(1)
            norm_sums(2)
            norm_sums(3)

        @block.tensor
        def _(pe):
            def fm_block(slot, ps, ks, first=0, n=KB, kwait=None):
                for pos in range(first, first + n):
                    k = ks[pos]
                    if kwait:
                        kwait(pos)
                    for w, h in ((wh, hh), (wh, hl), (wl, hh)):
                        for s in range(2):
                            mm = pe.matmul(ps[:, s * HALF:(s + 1) * HALF], w[:, slot, k * P:(k + 1) * P],
                                           h[:, k, s * HALF:(s + 1) * HALF],
                                           start=(pos == 0 and w is wh and h is hh),
                                           stop=(pos == len(ks) - 1 and w is wl))
                return mm

            def stats(st):
                for t in range(TB):
                    mm = pe.matmul(PS[2][:, t:t + 1], tA[:, t * P:(t + 1) * P], ones[:, 0:1], start=True, stop=True)
                mm.then_inc(st_sum, 1)

            def rows(st):
                pe.wait_ge(st_diag, st + 1)
                for s in range(2):
                    mm = pe.matmul(PS[3][:, s * HALF:(s + 1) * HALF], ones[:], tG[:, 2 + s * HALF:2 + (s + 1) * HALF],
                                   start=True, stop=True)
                mm.then_inc(st_row, 1)

            def first_two(n, t, slots, free0, free1):
                st = (ST_N0, ST_N1, ST_N2, ST_N3)[n]
                ks = NORM_ORDER[n]
                pe.wait_ge(w_lo, t + 1)
                free0()
                fm_block(slots[0], PS[0], ks, kwait=lambda pos: pe.wait_ge(n_lo, 8 * n + pos + 1)).then_inc(w_used, 1)
                pe.wait_ge(n_sum, 7 * (n + 1))
                stats(st)
                pe.wait_ge(w_lo, t + 2)
                free1()
                fm_block(slots[1], PS[1], ks, 0, 4)
                rows(st)
                fm_block(slots[1], PS[1], ks, 4, 4).then_inc(w_used, 1)

            def token_tile(t, j, free):
                pe.wait_ge(w_lo, t + 1)
                for kk in range(2):
                    k = 2 * j + kk
                    for pos, tok in enumerate(SWEEP):
                        if k == 0:
                            free(pos)
                        for w, h in ((wh, hh), (wl, hh), (wh, hl)):
                            mm = pe.matmul(bank(tok), h[:, k, tok * P:(tok + 1) * P], w[:, j, kk * HALF:(kk + 1) * HALF],
                                           start=(k == 0 and w is wh and h is hh), stop=(k == KB - 1 and h is hl))
                        if k == KB - 1 and pos < TB - 1:
                            mm.then_inc(tok_done, 1)
                mm.then_inc(w_used, 1)

            pe.wait_ge(const, 5)
            pe.wait_ge(pos_masked, 1)
            for s in range(2):
                mm = pe.matmul(PS[3][:, s * HALF:(s + 1) * HALF], ones[:], swsp[:, s * HALF:(s + 1) * HALF], start=True, stop=True)
            mm.then_inc(pos_rows, 1)

            first_two(0, 0, (SA, SB), lambda: None, lambda: pe.wait_ge(pos_copied, 1))
            with pe.Fori(1, CB) as m:
                pe.wait_ge(w_lo, 2 * m + 1)
                pe.wait_ge(lin_out, m)
                fm_block(SA, PS[0], range(KB)).then_inc(w_used, 1)
                pe.wait_ge(w_lo, 2 * m + 2)
                pe.wait_ge(gate_out, m)
                fm_block(SB, PS[1], range(KB)).then_inc(w_used, 1)
            with pe.Fori(0, 3) as c:
                for j in range(4):
                    token_tile(4 * c + (T_QKV + j), j, lambda pos: pe.wait_ge(tok_free, 8 * c + (pos + 1)))

            def turn_qk(p, c):
                pe.wait_ge(qn_ready, 2 * p + (c + 1))
                if not isinstance(p, int) or p:
                    pe.wait_ge(sc_max, 16 * p + (c - 1))
                for t in range(TB):
                    mm = pe.transpose(PS[c][:, t * P:(t + 1) * P], (tC, tU)[c][:, t * P:(t + 1) * P], ident[:])
                mm.then_inc(qt_done, 1)

            def scores(p, u):
                t, r, w, k0 = unit(u)
                if u == 0:
                    pe.wait_ge(qt_lo, 3 * p + 2)
                if u >= 2:
                    pe.wait_ge(sc_max, 16 * p + (u - 1))
                for a, b in ((0, min(w, HALF)), (HALF, w)):
                    if b > a:
                        for q, k in ((qth, kth), (qth, ktl), (qtl, kth)):
                            mm = pe.matmul(PS[u % 2][:, a:b], q[r:r + 64, t * P:(t + 1) * P], k[r:r + 64, k0 + a:k0 + b],
                                           start=(q is qth and k is kth), stop=(q is qtl))
                mm.then_inc(sc_done, 1)

            def turn(p, u):
                t, r, w, k0 = unit(u)
                pe.wait_ge(p_diag, 16 * p + (u + 1))
                if u:
                    pe.wait_ge(pt_lo, 16 * p + u)
                for b in range(w // P):
                    mm = pe.matmul(PS[2][:, b * P:(b + 1) * P], prob[:, u % 3, b * P:(b + 1) * P], diagp[:, u % 3, :],
                                   start=True, stop=True)
                mm.then_inc(pt_done, 1)

            def values(p, u):
                t, r, w, k0 = unit(u)
                pe.wait_ge(pt_lo, 16 * p + (u + 1))
                if u == 0:
                    pe.wait_ge(qt_lo, 3 * p + 3)
                if u in (8, 12):
                    pe.wait_ge(o_lo, 4 * p + (u // 4 - 1))
                c0 = u // 4 % 2 * HALF + t % 4 * P
                for b in range(w // P):
                    for v, q in ((vh, pth), (vh, ptl), (vl, pth)):
                        mm = pe.matmul(PS[3][:, c0:c0 + P], v[:, k0 // P + b, :], q[:, u % 2, b * P:(b + 1) * P],
                                       start=(b == 0 and v is vh and q is pth), stop=(b == w // P - 1 and v is vl))
                mm.then_inc(pv_done, 1)

            def pair(p, last=False):
                for s in range(16):
                    scores(p, s)
                    if s >= 2:
                        turn(p, s - 2)
                    if s >= 3:
                        values(p, s - 3)
                if not last:
                    turn_qk(p + 1, 0)
                turn(p, 14)
                if not last:
                    turn_qk(p + 1, 1)
                values(p, 13)
                turn(p, 15)
                values(p, 14)
                values(p, 15)

            pe.wait_ge(tok_free, 8 + 24)
            turn_qk(0, 0)
            turn_qk(0, 1)
            with pe.Fori(0, NPAIR - 1) as p:
                pair(p)
            pair(NPAIR - 1, last=True)

            pe.wait_ge(ln_sum0, CB - 1)
            pe.wait_ge(pt_lo, 64)
            for s in range(2):
                mm = pe.matmul(PS[2][:, s * HALF:(s + 1) * HALF], ones[:], tA[:, s * HALF:(s + 1) * HALF], start=True, stop=True)
            mm.then_inc(ln_mean, 1)

            def out_tile(j, k0):
                t = T_OUT + j
                pe.wait_ge(w_lo, t + 1)
                for half_ in range(2):
                    n = 2 * j + half_
                    if n >= 2:
                        pe.wait_ge(x_add, n - 1)
                    else:
                        pe.wait_ge(sc_max, 64)
                    for k in range(4):
                        for w, h in ((wh, hh), (wh, hl), (wl, hh)):
                            for s in range(2):
                                mm = pe.matmul(PS[n % 2][:, s * HALF:(s + 1) * HALF],
                                               w[:, j % 2, k * 256 + half_ * P:k * 256 + (half_ + 1) * P],
                                               h[:, k0 + k, s * HALF:(s + 1) * HALF],
                                               start=(k == 0 and w is wh and h is hh), stop=(k == 3 and w is wl))
                    mm.then_inc(w_used if half_ else m_done, 1)

            pe.wait_ge(o_lo, 16)
            out_tile(0, 4)
            pe.wait_ge(ln_sum, CB - 1)
            stats(ST_LN)
            out_tile(1, 4)
            rows(ST_LN)
            out_tile(2, 4)
            out_tile(3, 4)
            pe.wait_ge(ln_lo, CB)
            for j in range(4, 8):
                out_tile(j, 0)

            def down(slots, h0, x0):
                for m in range(KB):
                    pe.wait_ge(x_add, x0 + (m - 1))
                    for j in range(2):
                        for w, h in ((wh, hidh), (wh, hidl), (wl, hidh)):
                            for s in range(2):
                                mm = pe.matmul(PS[2 + m % 2][:, s * HALF:(s + 1) * HALF], w[:, slots[j], m * P:(m + 1) * P],
                                               h[:, h0 + j, s * HALF:(s + 1) * HALF],
                                               start=(j == 0 and w is wh and h is hidh), stop=(j == 1 and w is wl))
                    if m < KB - 1:
                        mm.then_inc(m_done, 1)
                mm.then_inc(w_used, 2)

            def ffn(f, n, t0, x0):
                b0 = FB * f
                first_two(n, t0, (SC, SD), lambda: pe.wait_ge(x_add, x0), lambda: None)
                for q, (slot, ps, done) in enumerate(((SA, PS[0], g_out), (SB, PS[1], up_out))):
                    pe.wait_ge(w_lo, t0 + 3 + q)
                    pe.wait_ge(done, b0 + 1)
                    fm_block(slot, ps, range(KB)).then_inc(w_used, 1)

                def group(i, odd):
                    t = 6 * i + (t0 - 2)
                    for q in range(4):
                        pe.wait_ge(w_lo, t + (q + 1))
                        pe.wait_ge((g_out, up_out)[q % 2], 2 * i + (b0 + q // 2))
                        fm_block(q % 2, PS[q % 2], range(KB)).then_inc(w_used, 1)
                    pe.wait_ge(w_lo, t + 6)
                    pe.wait_ge(hid_lo, 2 * i + b0)
                    down((SC, SD), 2 * (1 - odd), 8 * i + (x0 - 8))

                with pe.Fori(0, FG // 2) as ii:
                    group(2 * ii + 1, 1)
                    group(2 * ii + 2, 0)
                pe.wait_ge(w_lo, t0 + 3 * FB)
                pe.wait_ge(hid_lo, b0 + FB)
                down((SA, SB), 0, x0 + 8 * (FG - 1))

            ffn(0, 1, T_FFN0, X_OUT)

            first_two(2, T_GMLP, (SC, SD), lambda: pe.wait_ge(x_add, X_FFN0), lambda: None)
            for j in range(4):
                token_tile(T_V + j, j, lambda pos: pe.wait_ge(tok_free, 32 + 8))
            with pe.Fori(1, 4) as c:
                for j in range(4):
                    token_tile(4 * c + (T_V + j), j, lambda pos: pe.wait_ge(v_gelu, 8 * c + (pos - 7)))

            def positions(b, i, ps):
                pe.wait_ge(vn_lo, b + 1)
                for c in range(TB):
                    for v, w in ((vnh, wsph), (vnh, wspl), (vnl, wsph)):
                        mm = pe.matmul(ps[:, c * P:(c + 1) * P], v[:, c * P:(c + 1) * P], w[:, bass.ts(i, P)],
                                       start=(v is vnh and w is wsph), stop=(v is vnl))
                mm.then_inc(sv_done, 1)

            def mix(i, j):
                pe.wait_ge(sv_out, 2 * i + (j - 1))
                if j == 0:
                    pe.wait_ge(x_add, 8 * i + (X_FFN0 - 8))
                positions(2 * i + j, i, PS[2 + j])

            def u_tile(i, j):
                pe.wait_ge(w_lo, 4 * i + (T_GLOOP - 3 + j))
                pe.wait_ge(u_out, 2 * i + (j - 1))
                fm_block(j, PS[j], range(KB)).then_inc(w_used, 1)

            def gmlp_down(i, odd):
                pe.wait_ge(w_lo, 4 * i + T_GLOOP)
                pe.wait_ge(y_lo, 2 * i)
                pe.wait_ge(sv_out, 2 * i + 1)
                down_after_positions(i, odd)

            def down_after_positions(i, odd):
                x0 = 8 * i + (X_FFN0 - 8)
                for m in range(KB):
                    if m == 1:
                        pe.wait_ge(sv_out, 2 * i + 2)
                    if m >= 2:
                        pe.wait_ge(x_add, x0 + (m - 1))
                    for j in range(2):
                        for w, h in ((wh, hidh), (wh, hidl), (wl, hidh)):
                            for s in range(2):
                                mm = pe.matmul(PS[2 + m % 2][:, s * HALF:(s + 1) * HALF], w[:, (SC, SD)[j], m * P:(m + 1) * P],
                                               h[:, 2 * (1 - odd) + j, s * HALF:(s + 1) * HALF],
                                               start=(j == 0 and w is wh and h is hidh), stop=(j == 1 and w is wl))
                    if m < KB - 1:
                        mm.then_inc(m_done, 1)
                mm.then_inc(w_used, 2)

            pe.wait_ge(v_gelu, 32)
            pe.wait_ge(wsp_lo, 1)
            u_tile(1, 0)
            positions(0, 0, PS[2])
            u_tile(1, 1)
            positions(1, 0, PS[3])
            mix(1, 0)
            mix(1, 1)
            gmlp_down(1, 1)

            def gmlp_group(i, odd):
                for j in range(2):
                    u_tile(i, j)
                    mix(i, j)
                gmlp_down(i, odd)

            with pe.Fori(0, (GG - 2) // 2) as ii:
                gmlp_group(2 * ii + 2, 0)
                gmlp_group(2 * ii + 3, 1)
            pe.wait_ge(w_lo, T_FFN1)
            pe.wait_ge(y_lo, GB)
            down((SA, SB), 2, X_FFN0 + 8 * (GG - 1))
            ffn(1, 3, T_FFN1, X_GMLP)

        def o_part(act, p, q):
            r = 64 * (q // 2)
            act.wait_ge(pv_done, 16 * p + (4 * q + 4))
            act.activation(hh[r:r + 64, bass.ds(p + 4, 1), q % 2 * HALF:(q % 2 + 1) * HALF].rearrange("p a n -> p (a n)"),
                           PS[3][r:r + 64, q % 2 * HALF:(q % 2 + 1) * HALF], ACT.Copy).then_inc(o_hi, 1)

        @block.scalar
        def _(act):
            def split(t, slot, raw_slot, freed_by):
                act.wait_ge(raw_in[raw_slot], (t // 2 + 1) * 16)
                if freed_by is not None:
                    act.wait_ge(w_used, freed_by + 1)
                act.activation(wh[:, slot, :], raw[:, raw_slot, :], ACT.Copy).then_inc(w_hi, 1)

            def split_r(t, half, slot, raw_slot, back):
                act.wait_ge(raw_in[raw_slot], half * 16 + 16)
                act.wait_ge(w_used, t + (1 - back))
                act.activation(wh[:, slot, :], raw[:, raw_slot, :], ACT.Copy).then_inc(w_hi, 1)

            def norm_hi(n, m):
                act.activation(hh[:, m, :], x[:, m, :], ACT.Copy, scale=col(NORM_G[n] + m)).then_inc(n_hi, 1)

            def norm_sq(n, m):
                if m >= 3:
                    act.wait_ge(n_sum, 7 * n + m - 2)
                act.activation((tA if m == 0 else (tC, tU)[m % 2])[:], x[:, m, :], ACT.Square).then_inc(n_sq, 1)

            def take_root(st, count):
                act.wait_ge(st_sum, st + 1)
                act.activation(root[:], PS[2][:, 0:TB], ACT.Sqrt, scale=1.0 / count, bias=epsc[:, 0:1]).then_inc(st_root, 1)

            def copy_rows(st):
                act.wait_ge(st_row, st + 1)
                act.activation(rstdB[:], PS[3][:], ACT.Copy).then_inc(st_rb, 1)

            act.wait_ge(par_in, 16)
            act.wait_ge(const, 5)
            for m in range(KB):
                act.wait_ge(x_in[m], 16)
                norm_hi(0, m)
                if m in (1, 3):
                    split(m // 2, m // 2, m // 2, None)
                norm_sq(0, m)
            act.wait_ge(pos_rows, 1)
            act.activation(rstdB[:], PS[3][:], ACT.Copy).then_inc(pos_copied, 1)
            take_root(ST_N0, D)
            act.wait_ge(pos_bias, GB)
            split(2, SA, 0, 0)
            copy_rows(ST_N0)
            act.preload_act_table(ACT.Sigmoid)

            def conv_first(m):
                if m:
                    act.wait_ge(cv_done, m)
                src = cv[:, m, :]
                act.activation(cv[:, (m + CB) % (CB + 1), LEFT:LEFT + S], src[:, 0:S], ACT.Identity,
                               scale=col(C_CONVW + m * TAPS), bias=col(C_CONVB + m)).then_inc(cv_first, 1)
                act.activation(tG[:, 2:2 + S], src[:, 1:1 + S], ACT.Copy,
                               scale=col(C_CONVW + m * TAPS + 1)).then_inc(cv_first, 1)

            for m in range(CB):
                if m:
                    split(2 * m + 2, SA, 0, 2 * m)
                if m == 3:
                    conv_first(1)
                act.wait_ge(gate_out, m + 1)
                act.activation(tU[:], tU[:], ACT.Sigmoid).then_inc(sig, 1)
                split(2 * m + 3, SB, 1, 2 * m + 1)
                if m == 0:
                    act.wait_ge(glu, 1)
                    conv_first(0)
            act.wait_ge(st_rb, 1)
            act.wait_ge(st_root, 1)
            act.sem_inc(tok_free, 4)
            act.wait_ge(lin_out, CB)
            act.wait_ge(gate_out, CB)
            act.sem_inc(tok_free, 4)

            for c in range(3):
                for q in range(4):
                    t = T_QKV + 2 + 4 * c + q
                    split(t, (t - T_QKV) % 4, t % 2, t - 4)
                if c < 2:
                    conv_first(c + 2)
                for pos, tok in enumerate(SWEEP):
                    if pos < TB - 1:
                        act.wait_ge(tok_done, 7 * c + pos + 1)
                    else:
                        act.wait_ge(w_used, T_QKV + 4 * c + 4)
                    dst = qk[:, c, tok, :] if c < 2 else vraw[:, tok, :]
                    act.activation(dst, bank(tok), ACT.Copy, scale=rcol[:, tok:tok + 1]).then_inc(tok_free, 1)
                if c < 2:
                    for j in range(4):
                        n = 4 * c + j
                        act.wait_ge(tok_free, 8 + 8 * c + 8)
                        if n >= 2:
                            act.wait_ge(qk_sum, n - 1)
                        act.activation((tC, tU)[j % 2][:], qk[:, c, 2 * j:2 * j + 2, :].rearrange("p t d -> p (t d)"),
                                       ACT.Square).then_inc(qk_sq, 1)
                if c == 1:
                    act.wait_ge(qk_sum, 8)
                    act.activation(rqk[:], ssq[:], ACT.Sqrt, scale=1.0 / HD, bias=epsc[:, 0:1]).then_inc(qk_root, 1)
            act.activation(qgs[:], col(C_QG), ACT.Copy, scale=float(HD) ** -0.5).then_inc(qg_ready, 1)
            act.preload_act_table(ACT.Exp)
            act.wait_ge(qg_ready, 1)
            act.wait_ge(tok_free, 8 + 24)

            def q_high(p):
                act.wait_ge(qt_done, 2 * p + 1)
                act.activation(qth[:], PS[0][:], ACT.Copy, scale=qgs[:, 0:1]).then_inc(qt_hi, 1)

            def k_high(p):
                act.wait_ge(qt_done, 2 * p + 2)
                act.activation(kth[:], PS[1][:], ACT.Copy, scale=col(C_KG)).then_inc(qt_hi, 1)

            def v_high(p):
                act.activation(vh[:], vraw[:, :, bass.ts(p, P)], ACT.Copy).then_inc(qt_hi, 1)

            def exponentials(p, u):
                w = unit(u)[2]
                act.wait_ge(sc_max, 16 * p + (u + 1))
                act.activation(prob[:, u % 3, 0:w], prob[:, u % 3, 0:w], ACT.Exp, scale=-1.0,
                               bias=negmax[:, u % 3:u % 3 + 1], accum_out=rsum[:, u % 3:u % 3 + 1]).then_inc(exp_done, 1)

            def p_high(p, u):
                w = unit(u)[2]
                act.wait_ge(pt_done, 16 * p + (u + 1))
                if u >= 2:
                    act.wait_ge(pv_done, 16 * p + (u - 1))
                act.activation(pth[:, u % 2, 0:w], PS[2][:, 0:w], ACT.Copy).then_inc(pt_hi, 1)

            def pair(p, last=False):
                for s in range(16):
                    if s >= 7 and s % 4 == 3:
                        o_part(act, p, s // 4 - 1)
                    if s >= 2:
                        p_high(p, s - 2)
                    exponentials(p, s)
                if not last:
                    q_high(p + 1)
                p_high(p, 14)
                if not last:
                    k_high(p + 1)
                p_high(p, 15)
                o_part(act, p, 3)
                if not last:
                    v_high(p + 1)

            q_high(0)
            k_high(0)
            v_high(0)
            with act.Fori(0, NPAIR - 1) as p:
                pair(p)
            pair(NPAIR - 1, last=True)

            def conv_out(m):
                return cv[:, (m + CB) % (CB + 1), LEFT:LEFT + S]

            for m in range(CB):
                act.wait_ge(ln_cent, m + 1)
                if m == 3:
                    act.wait_ge(ln_sum, 1)
                act.activation((tA if m == 0 else (tC, tU)[m % 2])[:], conv_out(m), ACT.Square).then_inc(ln_sq, 1)
            split(T_OUT + 2, SA, 0, T_OUT)
            take_root(ST_LN, CONVW)
            split(T_OUT + 3, SB, 1, T_OUT + 1)
            copy_rows(ST_LN)
            for m in range(CB):
                act.wait_ge(ln_mul, m + 1)
                act.activation(conv_out(m), conv_out(m), ACT.Silu, scale=col(C_LNG + m), bias=col(C_LNB + m)).then_inc(ln_act, 1)
                act.wait_ge(ln_act, m + 1)
                act.activation(hh[:, m, :], conv_out(m), ACT.Copy).then_inc(ln_hi, 1)
            split(T_OUT + 4, SA, 0, T_OUT + 2)
            split(T_OUT + 5, SB, 1, T_OUT + 3)
            split(T_OUT + 6, SA, 0, T_OUT + 4)
            for m in (0, 1):
                act.wait_ge(x_add, X_OUTA + m + 1)
                norm_sq(1, m)
            split(T_OUT + 7, SB, 1, T_OUT + 5)
            split(T_FFN0, SC, 0, T_OUT)
            split(T_FFN0 + 1, SD, 1, T_OUT + 1)
            for m in (2, 3):
                act.wait_ge(x_add, X_OUTA + m + 1)
                norm_sq(1, m)
            split(T_FFN0 + 2, SA, 0, T_OUT + 6)
            for m in (4, 5):
                act.wait_ge(x_add, X_OUTA + m + 1)
                norm_hi(1, m)
                norm_sq(1, m)
            act.wait_ge(w_used, T_FFN0)
            for m in range(4):
                norm_hi(1, m)
            for m in (6, 7):
                act.wait_ge(x_add, X_OUTA + m + 1)
                norm_hi(1, m)
                norm_sq(1, m)
            split(T_FFN0 + 3, SB, 1, T_OUT + 7)
            take_root(ST_N1, D)
            copy_rows(ST_N1)

            def ffn(f, t0, x0, last_n):
                b0 = FB * f
                act.preload_act_table(ACT.Silu)

                def gate(b, f0):
                    act.wait_ge(g_out, b + (b0 + 1))
                    dw = par[:, bass.ds(f0, 4)]
                    act.activation(tC[:], tG[:, 2:2 + S], ACT.Identity, scale=dw[:, 2:3], bias=dw[:, 3:4]).then_inc(g_tap2, 1)
                    act.wait_ge(g_tap0, b + (b0 + 1))
                    act.activation(tC[:], tC[:], ACT.Silu).then_inc(g_silu, 1)

                def hidden(b, slot, free):
                    act.wait_ge(hid, b + (b0 + 1))
                    if free is not None:
                        act.wait_ge(w_used, free)
                    act.activation(hidh[:, slot, :], tU[:], ACT.Copy).then_inc(hid_hi, 1)

                dw0 = C_DW + 4 * FB * f
                gate(0, dw0)
                hidden(0, 0, None)
                gate(1, dw0 + 4)
                split(t0 + 4, SA, 0, t0 + 2)
                split(t0 + 5, SB, 1, t0 + 3)
                hidden(1, 1, None)

                def group(i, ih, odd):
                    t, h = 6 * i + (t0 - 2), ih + (t0 - 2) // 2
                    split_r(t + 2, h + 1, SA, 0, 2)
                    gate(2 * i, 8 * i + dw0)
                    split_r(t + 3, h + 1, SB, 1, 2)
                    hidden(2 * i, 2 * odd, t)
                    split_r(t + 4, h + 2, SC, 0, 6)
                    split_r(t + 5, h + 2, SD, 1, 6)
                    gate(2 * i + 1, 8 * i + (dw0 + 4))
                    split_r(t + 6, h + 3, SA, 0, 4)
                    split_r(t + 7, h + 3, SB, 1, 4)
                    hidden(2 * i + 1, 2 * odd + 1, t)

                with act.Fori(0, FG // 2) as ii:
                    group(2 * ii + 1, 6 * ii + 3, 1)
                    group(2 * ii + 2, 6 * ii + 6, 0)

            def norm_after(n, x0, tail, lo):
                act.wait_ge(*lo)
                for m in range(KB):
                    act.wait_ge(x_add, x0 + m + 1)
                    norm_hi(n, m)
                    norm_sq(n, m)
                for t, slot in tail:
                    split(t, slot, t % 2, t - 4)

            ffn(0, T_FFN0, X_OUT, 2)
            split(T_GMLP, SC, 0, T_GMLP - 4)
            split(T_GMLP + 1, SD, 1, T_GMLP - 3)
            norm_after(2, X_FFN0 - KB, ((T_V, SA), (T_V + 1, SB)), (hid_lo, FB))
            take_root(ST_N2, D)
            act.wait_ge(wsp_in, 16)
            act.activation(wsph[:], wspr[:], ACT.Copy).then_inc(wsp_hi, 1)
            copy_rows(ST_N2)
            act.preload_act_table(ACT.Gelu_apprx_tanh)
            for j in range(2):
                act.wait_ge(u_out, j + 1)
                act.activation(uearly[:, j, :], uearly[:, j, :], ACT.Gelu_apprx_tanh).then_inc(u_gelu, 1)
            act.wait_ge(st_rb, ST_N2 + 1)
            act.wait_ge(st_root, ST_N2 + 1)
            act.sem_inc(tok_free, 8)

            def v_group(c, first=False):
                for q in range(4):
                    split_r(4 * c + (T_V + 2 + q), 2 * c + ((T_V + 2 + q) // 2), (2 + q) % 4, q % 2, 4)
                for pos, tok in enumerate(SWEEP):
                    if pos < TB - 1:
                        act.wait_ge(tok_done, 7 * c + (21 + pos + 1))
                    else:
                        act.wait_ge(w_used, 4 * c + (T_V + 4))
                    if not first:
                        act.wait_ge(v_out[pos], 16 * c)
                        act.wait_ge(v_stat, 8 * c + (pos - 7))
                    act.activation(vst[:, pos, :], bank(tok), ACT.Gelu_apprx_tanh, scale=rcol[:, tok:tok + 1]).then_inc(v_gelu, 1)

            v_group(0, first=True)
            with act.Fori(1, 4) as c:
                v_group(c)
            act.wait_ge(v_mv, 1)
            act.activation(root[:], mv[:].rearrange("p (t a) -> p t a", a=2)[:, :, 1:2].rearrange("p t a -> p (t a)"),
                           ACT.Sqrt, bias=epsc[:, 0:1]).then_inc(v_root, 1)
            act.preload_act_table(ACT.Gelu_apprx_tanh)

            def vn_high(b):
                act.wait_ge(vn_f, b + 1)
                act.wait_ge(sv_done, b)
                act.activation(vnh[:], tA[:], ACT.Copy).then_inc(vn_hi, 1)

            def y_high(b, slot, free):
                act.wait_ge(y_f, b + 1)
                if free is not None:
                    act.wait_ge(w_used, free)
                act.activation(hidh[:, slot, :], tC[:], ACT.Copy).then_inc(y_hi, 1)

            def u_gelu_(b):
                act.wait_ge(u_out, b + 1)
                act.activation(tU[:], tU[:], ACT.Gelu_apprx_tanh).then_inc(u_gelu, 1)

            vn_high(0)
            split(T_GLOOP + 2, SC, 0, T_GLOOP - 2)
            split(T_GLOOP + 3, SD, 1, T_GLOOP - 1)
            vn_high(1)
            y_high(0, 0, None)
            vn_high(2)
            y_high(1, 1, None)
            vn_high(3)
            u_gelu_(2)
            y_high(2, 2, None)
            split(T_GLOOP + 4, SA, 0, T_GLOOP)
            u_gelu_(3)
            y_high(3, 3, None)
            split(T_GLOOP + 5, SB, 1, T_GLOOP + 1)

            def gmlp_group(i, odd):
                t, h = 4 * i + (T_GLOOP - 4), 2 * i + (T_GLOOP - 4) // 2
                split_r(t + 2, h + 1, SC, 0, 4)
                split_r(t + 3, h + 1, SD, 1, 4)
                vn_high(2 * i)
                u_gelu_(2 * i)
                vn_high(2 * i + 1)
                y_high(2 * i, 2 * odd, t)
                split_r(t + 4, h + 2, SA, 0, 4)
                u_gelu_(2 * i + 1)
                y_high(2 * i + 1, 2 * odd + 1, t)
                split_r(t + 5, h + 2, SB, 1, 4)

            with act.Fori(0, (GG - 2) // 2) as ii:
                gmlp_group(2 * ii + 2, 0)
                gmlp_group(2 * ii + 3, 1)
            split(T_FFN1, SC, 0, T_FFN1 - 4)
            split(T_FFN1 + 1, SD, 1, T_FFN1 - 3)
            norm_after(3, X_GMLP - KB, ((T_FFN1 + 2, SA), (T_FFN1 + 3, SB)), (y_lo, GB))
            take_root(ST_N3, D)
            copy_rows(ST_N3)
            ffn(1, T_FFN1, X_GMLP, None)

        def o_low(dve, p, q):
            r = 64 * (q // 2)
            cols = slice(q % 2 * HALF, (q % 2 + 1) * HALF)
            dve.wait_ge(o_hi, 4 * p + (q + 1))
            dve.tensor_tensor(hl[r:r + 64, bass.ds(p + 4, 1), cols].rearrange("p a n -> p (a n)"), PS[3][r:r + 64, cols],
                              hh[r:r + 64, bass.ds(p + 4, 1), cols].rearrange("p a n -> p (a n)").bitcast(F32),
                              ALU.subtract).then_inc(o_lo, 1)

        @block.vector
        def _(dve):
            def split(t, slot, raw_slot):
                dve.wait_ge(w_hi, t + 1)
                dve.tensor_tensor(wl[:, slot, :], raw[:, raw_slot, :], wh[:, slot, :].bitcast(F32), ALU.subtract).then_inc(w_lo, 1)

            def norm_lo(n, m, pos):
                dve.wait_ge(n_hi, 8 * n + pos + 1)
                dve.scalar_tensor_tensor(out=hl[:, m, :], in0=x[:, m, :], scalar=col(NORM_G[n] + m),
                                         in1=hh[:, m, :].bitcast(F32), op0=ALU.mult, op1=ALU.subtract).then_inc(n_lo, 1)

            def inverse(st):
                dve.wait_ge(st_root, st + 1)
                dve.reciprocal(rcol[:], root[:]).then_inc(st_rcol, 1)
                dve.wait_ge(st_rcol, st + 1)
                dve.tensor_tensor(tG[:, 2:2 + S].rearrange("p (t n) -> p t n", t=TB),
                                  ident[:].unsqueeze(1).broadcast_to([P, TB, P]),
                                  rcol[:].unsqueeze(2).broadcast_to([P, TB, P]), ALU.mult).then_inc(st_diag, 1)

            dve.wait_ge(par_in, 16)
            for m in range(KB):
                norm_lo(0, m, m)
                if m in (1, 3):
                    split(m // 2, m // 2, m // 2)
            dve.wait_ge(pos_copied, 1)
            dve.wait_ge(pos_in, 32)
            for b in range(GB):
                g = b // 2
                dve.scalar_tensor_tensor(out=sBt[:, b, :], in0=rstdB[:, g * P:(g + 1) * P], scalar=col(C_GB + b),
                                         in1=sbsp[:, g * P:(g + 1) * P], op0=ALU.mult, op1=ALU.add).then_inc(pos_bias, 1)
            dve.wait_ge(const, 5)
            inverse(ST_N0)

            def taps(m, k0, k1):
                n0 = m * (TAPS - 2)
                src = cv[:, m, :]
                for k in range(k0, k1):
                    acc = cv[:, (m + CB) % (CB + 1), LEFT:LEFT + S] if k % 2 == 0 else tG[:, 2:2 + S]
                    if k < 4:
                        dve.wait_ge(cv_first, 2 * m + k - 1)
                    else:
                        dve.wait_ge(cv_tap, n0 + k - 3)
                    dve.scalar_tensor_tensor(out=acc, in0=src[:, k:k + S], scalar=col(C_CONVW + m * TAPS + k),
                                             in1=acc, op0=ALU.mult, op1=ALU.add).then_inc(cv_tap, 1)

            def join(m):
                acc = cv[:, (m + CB) % (CB + 1), LEFT:LEFT + S]
                dve.wait_ge(cv_tap, (m + 1) * (TAPS - 2))
                dve.tensor_tensor(acc, acc, tG[:, 2:2 + S], ALU.add).then_inc(cv_done, 1)

            dve.wait_ge(st_rb, 1)
            dve.wait_ge(cv_pad, 1)
            for m in range(CB):
                dve.wait_ge(w_used, 2 * m + 1)
                if m:
                    dve.wait_ge(glu, m)
                dve.tensor_tensor(tC[:], PS[0][:], rstdB[:], ALU.mult).then_inc(lin_out, 1)
                split(2 * m + 2, SA, 0)
                if m == 1:
                    taps(0, 2, 8)
                if m == 2:
                    taps(0, 14, 20)
                if m == 3:
                    taps(0, 26, 31)
                    join(0)
                dve.wait_ge(w_used, 2 * m + 2)
                dve.tensor_tensor(tU[:], PS[1][:], rstdB[:], ALU.mult).then_inc(gate_out, 1)
                split(2 * m + 3, SB, 1)
                dve.wait_ge(sig, m + 1)
                dve.wait_ge(lin_out, m + 1)
                dve.tensor_tensor(cv[:, m, LEFT:LEFT + S], tC[:], tU[:], ALU.mult).then_inc(glu, 1)
                if m == 1:
                    taps(0, 8, 14)
                if m == 2:
                    taps(0, 20, 26)
                if m == 3:
                    taps(1, 2, 5)
            plan = [[(1, 5, 14)], [(1, 14, 23)], [(1, 23, 31), (1, 0, 0)], [(2, 2, 4)],
                    [(2, 4, 12)], [(2, 12, 20)], [(2, 20, 28)], [(2, 28, 31), (2, 0, 0), (3, 2, 4)],
                    [(3, 4, 13)], [(3, 13, 22)], [(3, 22, 31), (3, 0, 0)], []]
            for q in range(12):
                t = T_QKV + 2 + q
                if q in (4, 8):
                    c = q // 4 - 1
                    for j in range(4):
                        dve.wait_ge(qk_sq, 4 * c + j + 1)
                        dve.tensor_reduce(ssq[:, (4 * c + j) * 16:(4 * c + j + 1) * 16],
                                          (tC, tU)[j % 2][:].rearrange("p (g d) -> p g d", d=HD), AX.X, ALU.add).then_inc(qk_sum, 1)
                split(t, (t - T_QKV) % 4, t % 2)
                for m, k0, k1 in plan[q]:
                    if k1:
                        taps(m, k0, k1)
                    else:
                        join(m)
            dve.wait_ge(qk_root, 1)
            dve.reciprocal(rqk[:], rqk[:]).then_inc(qk_rinv, 1)

            dve.wait_ge(tok_free, 8 + 24)
            dve.wait_ge(qg_ready, 1)

            def q_low(p):
                dve.wait_ge(qt_hi, 3 * p + 1)
                dve.scalar_tensor_tensor(out=qtl[:], in0=PS[0][:], scalar=qgs[:, 0:1], in1=qth[:].bitcast(F32),
                                         op0=ALU.mult, op1=ALU.subtract).then_inc(qt_lo, 1)

            def k_low(p):
                dve.wait_ge(qt_hi, 3 * p + 2)
                dve.scalar_tensor_tensor(out=ktl[:], in0=PS[1][:], scalar=col(C_KG), in1=kth[:].bitcast(F32),
                                         op0=ALU.mult, op1=ALU.subtract).then_inc(qt_lo, 1)

            def v_low(p):
                dve.wait_ge(qt_hi, 3 * p + 3)
                dve.tensor_tensor(vl[:], vraw[:, :, bass.ts(p, P)], vh[:].bitcast(F32), ALU.subtract).then_inc(qt_lo, 1)

            def maxima(p, u):
                w = unit(u)[2]
                dve.wait_ge(sc_done, 16 * p + (u + 1))
                if u in (0, 8):
                    dve.wait_ge(bias_ok, 4 * p + (2 + u // 4))
                if u >= 3:
                    dve.wait_ge(pt_done, 16 * p + (u - 2))
                dve.sem_inc(sc_seen, 1)
                dve.tensor_tensor_reduce(prob[:, u % 3, 0:w], PS[u % 2][:, 0:w], bias[:, u // TB, BANDW - w:BANDW],
                                         -1.0, 3e38, ALU.add, ALU.min, negmax[:, u % 3:u % 3 + 1]).then_inc(sc_max, 1)

            def inverse_sum(p, u):
                dve.wait_ge(exp_done, 16 * p + (u + 1))
                if u:
                    dve.wait_ge(p_diag, 16 * p + u)
                dve.reciprocal(rinv[:, u % 3:u % 3 + 1], rsum[:, u % 3:u % 3 + 1]).then_inc(p_inv, 1)
                dve.wait_ge(p_inv, 16 * p + (u + 1))
                dve.tensor_scalar(diagp[:, u % 3, :], ident[:], rinv[:, u % 3:u % 3 + 1], None, ALU.mult).then_inc(p_diag, 1)

            def p_low(p, u):
                w = unit(u)[2]
                dve.wait_ge(pt_hi, 16 * p + (u + 1))
                dve.tensor_tensor(ptl[:, u % 2, 0:w], PS[2][:, 0:w], pth[:, u % 2, 0:w].bitcast(F32),
                                  ALU.subtract).then_inc(pt_lo, 1)

            def pair(p, last=False):
                for s in range(16):
                    maxima(p, s)
                    if s >= 1:
                        inverse_sum(p, s - 1)
                    if s >= 7 and s % 4 == 3:
                        o_low(dve, p, s // 4 - 1)
                    if s >= 2:
                        p_low(p, s - 2)
                inverse_sum(p, 15)
                if not last:
                    q_low(p + 1)
                p_low(p, 14)
                if not last:
                    k_low(p + 1)
                p_low(p, 15)
                o_low(dve, p, 3)
                if not last:
                    v_low(p + 1)
                dve.wait_ge(p_diag, 16 * p + 16)

            q_low(0)
            k_low(0)
            v_low(0)
            with dve.Fori(0, NPAIR - 1) as p:
                pair(p)
            pair(NPAIR - 1, last=True)

            def conv_out(m):
                return cv[:, (m + CB) % (CB + 1), LEFT:LEFT + S]

            def add_x(n, last_used=None):
                if n % 2:
                    dve.wait_ge(w_used, T_OUT + n // 2 + 1)
                else:
                    dve.wait_ge(m_done, n // 2 + 1)
                m = n % KB
                dve.wait_ge(x_in[m], 32)
                if n >= KB:
                    dve.wait_ge(x_add, n - KB + 1)
                dve.tensor_tensor(x[:, m, :], x[:, m, :], PS[n % 2][:], ALU.add).then_inc(x_add, 1)

            dve.wait_ge(ln_mean, 1)
            for m in range(CB):
                dve.scalar_tensor_tensor(out=conv_out(m), in0=PS[2][:], scalar=-1.0 / CONVW, in1=conv_out(m),
                                         op0=ALU.mult, op1=ALU.add).then_inc(ln_cent, 1)
            add_x(0)
            add_x(1)
            split(T_OUT + 2, SA, 0)
            dve.wait_ge(cv_done, CB)
            inverse(ST_LN)
            add_x(2)
            add_x(3)
            split(T_OUT + 3, SB, 1)
            dve.wait_ge(st_rb, ST_LN + 1)
            for m in range(CB):
                dve.tensor_tensor(conv_out(m), conv_out(m), rstdB[:], ALU.mult).then_inc(ln_mul, 1)
            add_x(4)
            for m in range(CB):
                dve.wait_ge(ln_hi, m + 1)
                dve.tensor_tensor(hl[:, m, :], conv_out(m), hh[:, m, :].bitcast(F32), ALU.subtract).then_inc(ln_lo, 1)
                if m == 1:
                    add_x(5)
            split(T_OUT + 4, SA, 0)
            add_x(6)
            add_x(7)
            split(T_OUT + 5, SB, 1)
            add_x(8)
            add_x(9)
            split(T_OUT + 6, SA, 0)
            add_x(10)
            add_x(11)
            split(T_OUT + 7, SB, 1)
            split(T_FFN0, SC, 0)
            split(T_FFN0 + 1, SD, 1)
            add_x(12)
            add_x(13)
            split(T_FFN0 + 2, SA, 0)
            add_x(14)
            norm_lo(1, 4, 0)
            norm_lo(1, 5, 1)
            add_x(15)
            for pos in range(2, 8):
                norm_lo(1, NORM_ORDER[1][pos], pos)
            split(T_FFN0 + 3, SB, 1)
            inverse(ST_N1)

            def add_block(m, x0, done0, used):
                if m < KB - 1:
                    dve.wait_ge(m_done, done0 + (m + 1))
                else:
                    dve.wait_ge(w_used, used)
                dve.wait_ge(x_add, x0 + (m - 7))
                dve.tensor_tensor(x[:, m, :], x[:, m, :], PS[2 + m % 2][:], ALU.add).then_inc(x_add, 1)

            M_OUT = 8

            def ffn(f, t0, x0, done0):
                b0 = FB * f
                dve.wait_ge(st_rb, (ST_N1, ST_N3)[f] + 1)
                dw0 = C_DW + 4 * FB * f

                def gate(b, used, f0):
                    dve.wait_ge(w_used, used)
                    dve.wait_ge(g_tap0, b + b0)
                    dve.tensor_tensor(tG[:, 2:2 + S], PS[0][:], rstdB[:], ALU.mult).then_inc(g_out, 1)
                    dw = par[:, bass.ds(f0, 4)]
                    dve.wait_ge(g_tap2, b + (b0 + 1))
                    dve.scalar_tensor_tensor(out=tC[:], in0=tG[:, 1:1 + S], scalar=dw[:, 1:2], in1=tC[:],
                                             op0=ALU.mult, op1=ALU.add).then_inc(g_tap1, 1)
                    dve.wait_ge(g_tap1, b + (b0 + 1))
                    dve.scalar_tensor_tensor(out=tC[:], in0=tG[:, 0:S], scalar=dw[:, 0:1], in1=tC[:],
                                             op0=ALU.mult, op1=ALU.add).then_inc(g_tap0, 1)

                def up(b, used):
                    dve.wait_ge(w_used, used)
                    dve.wait_ge(hid_lo, b + b0)
                    dve.tensor_tensor(tU[:], PS[1][:], rstdB[:], ALU.mult).then_inc(up_out, 1)
                    dve.wait_ge(up_out, b + (b0 + 1))
                    dve.wait_ge(g_silu, b + (b0 + 1))
                    dve.tensor_tensor(tU[:], tU[:], tC[:], ALU.mult).then_inc(hid, 1)

                def low(b, slot):
                    dve.wait_ge(hid_hi, b + (b0 + 1))
                    dve.tensor_tensor(hidl[:, slot, :], tU[:], hidh[:, slot, :].bitcast(F32), ALU.subtract).then_inc(hid_lo, 1)

                gate(0, t0 + 1, dw0)
                up(0, t0 + 2)
                low(0, 0)
                gate(1, t0 + 3, dw0 + 4)
                split(t0 + 4, SA, 0)
                up(1, t0 + 4)
                split(t0 + 5, SB, 1)
                low(1, 1)

                def group(i, odd):
                    t = 6 * i + (t0 - 2)
                    xg, dg = 8 * i + (x0 - 8), 7 * i + (done0 - 7)
                    split(t + 2, SA, 0)
                    gate(2 * i, t + 1, 8 * i + dw0)
                    split(t + 3, SB, 1)
                    up(2 * i, t + 2)
                    low(2 * i, 2 * odd)
                    split(t + 4, SC, 0)
                    split(t + 5, SD, 1)
                    gate(2 * i + 1, t + 3, 8 * i + (dw0 + 4))
                    split(t + 6, SA, 0)
                    up(2 * i + 1, t + 4)
                    split(t + 7, SB, 1)
                    add_block(0, xg, dg, None)
                    low(2 * i + 1, 2 * odd + 1)
                    for m in range(1, KB):
                        add_block(m, xg, dg, t + 6)

                with dve.Fori(0, FG // 2) as ii:
                    group(2 * ii + 1, 1)
                    group(2 * ii + 2, 0)

            def last_group(n, x0, done0, used, tail):
                for m in range(KB):
                    add_block(m, x0, done0, used)
                    if n is not None and m:
                        norm_lo(n, m - 1, m - 1)
                if n is not None:
                    norm_lo(n, KB - 1, KB - 1)
                for t, slot in tail:
                    split(t, slot, t % 2)

            ffn(0, T_FFN0, X_OUT, M_OUT)
            M_FFN0 = M_OUT + 7 * FG
            split(T_GMLP, SC, 0)
            split(T_GMLP + 1, SD, 1)
            last_group(2, X_FFN0 - 8, M_FFN0 - 7, T_GMLP, ((T_V, SA), (T_V + 1, SB)))
            dve.wait_ge(g_tap0, FB)
            inverse(ST_N2)
            dve.wait_ge(wsp_hi, 1)
            dve.tensor_tensor(wspl[:], wspr[:], wsph[:].bitcast(F32), ALU.subtract).then_inc(wsp_lo, 1)
            dve.wait_ge(st_rb, ST_N2 + 1)
            for j in range(2):
                dve.wait_ge(w_used, T_GMLP + 1 + j)
                dve.tensor_tensor(uearly[:, j, :], PS[j][:], rstdB[:], ALU.mult).then_inc(u_out, 1)
            with dve.Fori(0, 4) as c:
                for q in range(4):
                    split(4 * c + (T_V + 2 + q), (2 + q) % 4, q % 2)
                for pos, tok in enumerate(SWEEP):
                    dve.wait_ge(v_gelu, 8 * c + (pos + 1))
                    dve.bn_stats(vstat[:, tok, bass.ds(c, 1), :].rearrange("p a n -> p (a n)"), vst[:, pos, :]).then_inc(v_stat, 1)
            dve.wait_ge(v_stat, 32)
            for t in range(TB):
                mm = dve.bn_aggr(mv[:, 2 * t:2 * t + 2], vstat[:, t, :, :].rearrange("p a n -> p (a n)"))
            mm.then_inc(v_mv, 1)
            dve.wait_ge(v_root, 1)
            dve.reciprocal(rcol[:], root[:]).then_inc(v_rs, 1)
            dve.wait_ge(v_rs, 1)

            def vn_full(b):
                dve.wait_ge(v_in, 16 * b + 16)
                for t in range(TB):
                    ts = dve.tensor_scalar(tA[:, t * P:(t + 1) * P], tA[:, t * P:(t + 1) * P], mv[:, 2 * t:2 * t + 1],
                                           rcol[:, t:t + 1], ALU.subtract, ALU.mult)
                ts.then_inc(vn_f, 1)

            def vn_low(b):
                dve.wait_ge(vn_f, b + 1)
                dve.wait_ge(vn_hi, b + 1)
                dve.tensor_tensor(vnl[:], tA[:], vnh[:].bitcast(F32), ALU.subtract).then_inc(vn_lo, 1)

            def mixed(b, j, ih):
                dve.wait_ge(sv_done, b + 1)
                dve.wait_ge(b_in[j], ih * 16 + 16)
                dve.wait_ge(y_lo, b)
                dve.scalar_tensor_tensor(out=tC[:].rearrange("p (c t) -> p c t", c=TB),
                                         in0=PS[2 + j][:].rearrange("p (c t) -> p c t", c=TB), scalar=par[:, bass.ds(b + C_GG, 1)],
                                         in1=bblk[:, j * P:(j + 1) * P].unsqueeze(1).broadcast_to([P, TB, P]),
                                         op0=ALU.mult, op1=ALU.add).then_inc(sv_out, 1)

            def y_full(b, u):
                dve.wait_ge(sv_out, b + 1)
                dve.wait_ge(u_gelu, b + 1)
                dve.tensor_tensor(tC[:], tC[:], u, ALU.mult).then_inc(y_f, 1)

            def y_low(b, slot):
                dve.wait_ge(y_hi, b + 1)
                dve.tensor_tensor(hidl[:, slot, :], tC[:], hidh[:, slot, :].bitcast(F32), ALU.subtract).then_inc(y_lo, 1)

            for q in range(TB):
                dve.wait_ge(v_out[q], 16 * 4)
            vn_full(0)
            vn_low(0)
            split(T_GLOOP + 2, SC, 0)
            split(T_GLOOP + 3, SD, 1)
            for b in range(2):
                vn_full(b + 1)
                mixed(b, b, 0)
                vn_low(b + 1)
                y_full(b, uearly[:, b, :])
                y_low(b, b)
            vn_full(3)

            def u_scale(b, j, t):
                dve.wait_ge(w_used, t + 1)
                dve.wait_ge(y_f, b)
                dve.tensor_tensor(tU[:], PS[j][:], rstdB[:], ALU.mult).then_inc(u_out, 1)

            def group_rest(i, odd):
                t = 4 * i + (T_GLOOP - 4)
                xg, dg = 8 * i + (X_FFN0 - 8), 7 * i + (M_FFN0 - 7)
                u_scale(2 * i, 0, t)
                mixed(2 * i, 0, i)
                vn_low(2 * i + 1)
                y_full(2 * i, tU[:])
                y_low(2 * i, 2 * odd)
                split(t + 4, SA, 0)
                u_scale(2 * i + 1, 1, t + 1)
                mixed(2 * i + 1, 1, i)
                y_full(2 * i + 1, tU[:])
                add_block(0, xg, dg, None)
                y_low(2 * i + 1, 2 * odd + 1)
                add_block(1, xg, dg, None)
                split(t + 5, SB, 1)
                for m in range(2, KB):
                    add_block(m, xg, dg, t + 4)

            def gmlp_group(i, odd):
                t = 4 * i + (T_GLOOP - 4)
                split(t + 2, SC, 0)
                split(t + 3, SD, 1)
                vn_full(2 * i)
                vn_low(2 * i)
                vn_full(2 * i + 1)
                group_rest(i, odd)

            group_rest(1, 1)
            with dve.Fori(0, (GG - 2) // 2) as ii:
                gmlp_group(2 * ii + 2, 0)
                gmlp_group(2 * ii + 3, 1)
            M_GMLP = M_FFN0 + 7 * GG
            split(T_FFN1, SC, 0)
            split(T_FFN1 + 1, SD, 1)
            last_group(3, X_GMLP - 8, M_GMLP - 7, T_FFN1, ((T_FFN1 + 2, SA), (T_FFN1 + 3, SB)))
            inverse(ST_N3)
            ffn(1, T_FFN1, X_GMLP, M_GMLP)
            last_group(None, X_GMLP + 8 * (FG - 1), M_GMLP + 7 * (FG - 1), NT, ())


def lay_out(inputs):
    f = {k: np.asarray(v) for k, v in inputs.items()}

    def columns(a):
        return np.moveaxis(a.reshape(a.shape[:-1] + (-1, P)), -1, 0).reshape(P, -1)

    def feature_tiles(w):
        return w.reshape(KB, P, -1, P).transpose(2, 1, 0, 3).reshape(-1, P, 1024)

    def token_tiles(w):
        return w.reshape(4, 2, P, -1, HALF).transpose(3, 0, 2, 1, 4).reshape(-1, P, 1024)

    def half_tiles(w):
        return w.reshape(4, P, 4, 256).transpose(2, 1, 0, 3).reshape(4, P, 1024)

    def interleave(*tiles):
        return np.stack(tiles, 1).reshape(-1, P, 1024)

    def pipelined(ups, downs):
        parts = [ups[0]]
        for i in range(1, len(ups)):
            parts += [ups[i], downs[i - 1]]
        return parts + [downs[-1]]

    w_in = f["w_in_e"][0]
    glu = interleave(feature_tiles(w_in[:, 0:CONVW]), feature_tiles(w_in[:, CONVW:2 * CONVW]))
    stream = [glu, token_tiles(w_in[:, 2 * CONVW:]),
              half_tiles(f["w_out_e"][0][CONVW:]), half_tiles(f["w_out_e"][0][:CONVW])]

    def ffn(layer):
        gu = interleave(feature_tiles(f["w_gate"][layer]), feature_tiles(f["w_up"][layer])).reshape(FG, 4, P, 1024)
        return pipelined(gu, f["w_down"][layer].reshape(FG, 2, P, 1024))

    w_io = f["w_in_o"][0]
    u = feature_tiles(w_io[:, 0:2048]).reshape(GG, 2, P, 1024)
    gm = pipelined(u, f["w_out_o"][0].reshape(GG, 2, P, 1024))
    stream += ffn(0) + [gm[0], token_tiles(w_io[:, 2048:])] + gm[1:] + ffn(1)
    dw = np.concatenate([f["ffn_dw_w"], f["ffn_dw_b"][:, None, :]], 1).transpose(0, 2, 1)
    dw = dw.reshape(2, FB, P, 4).transpose(2, 0, 1, 3).reshape(P, -1)
    cw = f["conv_w"][0].reshape(TAPS, CB, P).transpose(2, 1, 0).reshape(P, -1)
    params = np.concatenate([
        columns(f["mix_norm_g"]), columns(f["ffn_norm_g"]), cw, columns(f["conv_b"][0]), columns(f["conv_ln_g"][0]),
        columns(f["conv_ln_b"][0]), np.tile(f["qn_g"][0], 2)[:, None], np.tile(f["kn_g"][0], 2)[:, None],
        columns(f["gate_ln_g"][0]), columns(f["gate_ln_b"][0]), dw], 1)
    c = np.ascontiguousarray
    return {
        "xT": c(f["x"][0].T),
        "wstream": np.concatenate(stream, 0),
        "params": c(params),
        "rel": c(f["rel_bias"][0][:, ::-1]),
        "wsp": c(f["w_sp"][0].transpose(2, 0, 1).reshape(P, -1)),
        "bsp": c(f["b_sp"][0].reshape(1, -1)[0]),
    }


def kernel(**inputs):
    import concourse.bacc as bacc
    from concourse.bass_utils import run_bass_kernel_spmd

    arrays = lay_out(inputs)
    nc = bacc.Bacc("TRN2", target_bir_lowering=False, num_devices=1)
    args = {k: nc.dram_tensor(k, a.shape, mybir.dt.from_np(a.dtype), kind="ExternalInput").ap() for k, a in arrays.items()}
    outT = nc.dram_tensor("outT", [D, S], F32, kind="ExternalOutput").ap()
    program(nc, **args, outT=outT)
    r = run_bass_kernel_spmd(nc, [arrays], core_ids=[0])
    return np.ascontiguousarray(r.results[0]["outT"].T)[None]
```

```python
from contextlib import ExitStack

import numpy as np

import concourse.bass as bass
from concourse import mybir

ALU = mybir.AluOpType
ACT = mybir.ActivationFunctionType
AX = mybir.AxisListType
F32 = mybir.dt.float32
F32R = mybir.dt.float32r

P = 128
D = 1024
S = 1024
HALF = 512
KB = D // P
TB = S // P
EPS = 1e-6

CONVW = 512
CB = CONVW // P
TAPS = 31
LEFT = TAPS - 1
LATE = 4
CVW = 1056
NH, HD = 8, 64
NPAIR = NH // 2
BANDW = 640
NREL = 320
RELW = 768
MASKED = -1e30

FB = 2816 // P
FG = FB // 2
GB = 2048 // P
GG = GB // 2

T_QKV = 2 * CB
T_OUT = T_QKV + 12
T_FFN0 = T_OUT + 8
T_GMLP = T_FFN0 + 3 * FB
T_V = T_GMLP + 2
T_GLOOP = T_V + 16
T_FFN1 = T_GMLP + 3 * GB
NT = T_FFN1 + 3 * FB
SA, SB, SC, SD = range(4)

C_MIXG = 0
C_FFNG = C_MIXG + 2 * KB
C_CONVW = C_FFNG + 2 * KB
C_CONVB = C_CONVW + CB * TAPS
C_LNG = C_CONVB + CB
C_LNB = C_LNG + CB
C_QG = C_LNB + CB
C_KG = C_QG + 1
C_GG = C_KG + 1
C_GB = C_GG + GB
C_DW = C_GB + GB
NPAR = C_DW + 2 * FB * 4

ST_N0, ST_LN, ST_N1, ST_N2, ST_N3 = range(5)
NORM_G = [C_MIXG, C_FFNG, C_MIXG + KB, C_FFNG + KB]
NORM_ORDER = [list(range(8)), [4, 5, 0, 1, 2, 3, 6, 7], list(range(8)), list(range(8))]

SWEEP = [4, 5, 6, 7, 0, 1, 2, 3]


def program(nc, xT, wstream, params, rel, wsp, bsp, outT):
    with ExitStack() as ctx:
        base = nc.sbuf_base
        base = (base + 31) // 32 * 32

        def at(name, offset, shape, dt):
            return nc.alloc_sbuf_tensor_at(name, shape, dt, offset=base + offset)

        def sem(name):
            return ctx.enter_context(nc.semaphore(name))

        KiB = 1024
        o_x, o_hh, o_hl, o_hid, o_raw = 0, 32 * KiB, 64 * KiB, 96 * KiB, 128 * KiB
        o_wh, o_wl = 136 * KiB, 152 * KiB
        o_rb, o_ta, o_tc, o_tu, o_tg = 168 * KiB, 172 * KiB, 176 * KiB, 180 * KiB, 184 * KiB
        o_vn = o_tg + 4128
        o_small = o_vn + 16 * KiB

        x = at("x", o_x, [P, KB, S], F32)
        hh = at("hh", o_hh, [P, KB, S], F32R)
        hl = at("hl", o_hl, [P, KB, S], F32R)
        hidh = at("hidh", o_hid, [P, 4, S], F32R)
        hidl = at("hidl", o_hid + 16 * KiB, [P, 4, S], F32R)
        raw = at("raw", o_raw, [P, 2, 1024], F32)
        wh = at("wh", o_wh, [P, 4, 1024], F32R)
        wl = at("wl", o_wl, [P, 4, 1024], F32R)
        rstdB = at("rstdB", o_rb, [P, S], F32)
        tA = at("tA", o_ta, [P, S], F32)
        tC = at("tC", o_tc, [P, S], F32)
        tU = at("tU", o_tu, [P, S], F32)
        tG = at("tG", o_tg, [P, S + 2], F32)
        vnh = at("vnh", o_vn, [P, S], F32R)
        vnl = at("vnl", o_vn + 4 * KiB, [P, S], F32R)
        wsph = at("wsph", o_vn + 8 * KiB, [P, S], F32R)
        wspl = at("wspl", o_vn + 12 * KiB, [P, S], F32R)
        qk = at("qk", o_x, [P, 2, TB, CONVW], F32)
        vraw = at("vraw", o_vn, [P, TB, CONVW], F32)
        cv = at("cv", o_hid, [P, CB + 1, CVW], F32)
        ssq = at("ssq", o_hid + 27776, [P, 2 * TB * NH], F32)
        rqk = at("rqk", o_hid + 28288, [P, 2 * TB * NH], F32)
        qgs = at("qgs", o_hid + 28800, [P, 1], F32)
        negmax = at("negmax", o_hid + 28832, [P, 3], F32)
        rsum = at("rsum", o_hid + 28864, [P, 3], F32)
        rinv = at("rinv", o_hid + 28896, [P, 3], F32)
        qth = at("qth", o_hh, [P, S], F32R)
        qtl = at("qtl", o_hh + 4 * KiB, [P, S], F32R)
        kth = at("kth", o_hh + 8 * KiB, [P, S], F32R)
        ktl = at("ktl", o_hh + 12 * KiB, [P, S], F32R)
        vh = at("vh", o_hl, [P, TB, P], F32R)
        vl = at("vl", o_hl + 4 * KiB, [P, TB, P], F32R)
        bias = at("bias", o_hl + 8 * KiB, [P, 2, BANDW], F32)
        prob = at("prob", o_wh + 8 * KiB, [P, 3, BANDW], F32)
        ptr = [at(f"ptr{i}", o, [P, BANDW // P, 2, P], F32R) for i, o in enumerate((o_wl + 8 * KiB, o_hid + 21120))]
        osum = at("osum", o_rb, [P, 2, 2 * P], F32)
        sBt = at("sBt", o_vn, [P, GB, P], F32)
        swsp = at("swsp", o_vn + 8 * KiB, [P, S], F32)
        sbsp = at("sbsp", o_vn + 12 * KiB, [P, S], F32)
        etab = at("etab", o_hid, [NH, RELW], F32)
        uearly = at("uearly", o_hid + 8 * KiB, [P, 2, S], F32)
        vst = at("vst", o_hid + 16 * KiB, [P, TB, HALF], F32)
        wspr = at("wspr", o_hid, [P, S], F32)

        s_off = [o_small]

        def small(name, cols, dt=F32):
            t = at(name, s_off[0], [P, cols], dt)
            s_off[0] += (cols * 4 + 31) // 32 * 32
            return t

        par = small("par", NPAR)
        ident = small("ident", P)
        ones = small("ones", P)
        bblk = small("bblk", 2 * P)
        rcol = small("rcol", TB)
        root = small("root", TB)
        epsc = small("epsc", 1)
        mv = small("mv", 2 * TB)
        vstat = at("vstat", o_vn, [P, TB, 4, 6], F32)

        PS = [ctx.enter_context(nc.psum_tensor(f"ps{i}", [P, 2 * HALF], F32)) for i in range(4)]

        def bank(tok):
            return PS[tok // 2][:, tok % 2 * HALF:(tok % 2 + 1) * HALF]

        e_dram = nc.dram_tensor("rel_rows", [NH, P, RELW], F32, kind="Internal").ap()
        v_dram = nc.dram_tensor("v_gelu", [S, 2048], F32, kind="Internal").ap()
        b_dram = nc.dram_tensor("pos_bias", [P, GB * P], F32, kind="Internal").ap()
        w_dram = nc.dram_tensor("pos_masked", [P, S], F32, kind="Internal").ap()
        v_blocks = v_dram.rearrange("(c s) d -> s c d", s=P)

        raw_in = [sem(f"raw_in{i}") for i in range(2)]
        w_hi, w_lo = sem("w_hi"), sem("w_lo")
        w_used = sem("w_used")
        x_in = [sem(f"x_in{i}") for i in range(KB)]
        par_in, rel_in, pos_in = sem("par_in"), sem("rel_in"), sem("pos_in")
        const = sem("const")
        e_ready, e_out = sem("e_ready"), sem("e_out")
        pos_masked, pos_rows = sem("pos_masked"), sem("pos_rows")
        pos_bias, pos_out = sem("pos_bias"), sem("pos_out")
        n_hi, n_lo, n_sq, n_sum = sem("n_hi"), sem("n_lo"), sem("n_sq"), sem("n_sum")
        st_sum, st_root, st_rcol = sem("st_sum"), sem("st_root"), sem("st_rcol")
        st_diag, st_row, st_rb = sem("st_diag"), sem("st_row"), sem("st_rb")
        lin_out, gate_out, sig, glu = sem("lin_out"), sem("gate_out"), sem("sig"), sem("glu")
        cv_pad, cv_first, cv_tap = sem("cv_pad"), sem("cv_first"), sem("cv_tap")
        cv_prod, cv_late, cv_done = sem("cv_prod"), sem("cv_late"), sem("cv_done")
        tok_done, tok_free = sem("tok_done"), sem("tok_free")
        qk_sq, qk_sum, qk_root, qk_rinv = sem("qk_sq"), sem("qk_sum"), sem("qk_root"), sem("qk_rinv")
        qg_ready = sem("qg_ready")
        qn_ready, qt_done, qt_hi, qt_lo = sem("qn_ready"), sem("qt_done"), sem("qt_hi"), sem("qt_lo")
        bias_in = [sem(f"bias_in{i}") for i in range(2)]
        bias_ok = sem("bias_ok")
        sc_seen, v_seen = sem("sc_seen"), sem("v_seen")
        sc_done, sc_max, exp_done = sem("sc_done"), sem("sc_max"), sem("exp_done")
        p_inv, p_norm, pt_done = sem("p_inv"), sem("p_norm"), sem("pt_done")
        pt_hi, pt_lo, pv_done = sem("pt_hi"), sem("pt_lo"), sem("pv_done")
        o_cross, o_sum, o_hi, o_lo = sem("o_cross"), sem("o_sum"), sem("o_hi"), sem("o_lo")
        ln_sum0, ln_mean, ln_cent = sem("ln_sum0"), sem("ln_mean"), sem("ln_cent")
        ln_sq, ln_sum, ln_mul = sem("ln_sq"), sem("ln_sum"), sem("ln_mul")
        ln_act, ln_hi, ln_lo = sem("ln_act"), sem("ln_hi"), sem("ln_lo")
        m_done, x_add = sem("m_done"), sem("x_add")
        g_out, g_tap2, g_tap1, g_tap0 = sem("g_out"), sem("g_tap2"), sem("g_tap1"), sem("g_tap0")
        g_silu, up_out, hid, hid_hi, hid_lo = sem("g_silu"), sem("up_out"), sem("hid"), sem("hid_hi"), sem("hid_lo")
        wsp_in, wsp_hi, wsp_lo = sem("wsp_in"), sem("wsp_hi"), sem("wsp_lo")
        v_gelu, v_stat, v_mv, v_root, v_rs = sem("v_gelu"), sem("v_stat"), sem("v_mv"), sem("v_root"), sem("v_rs")
        v_out = [sem(f"v_out{i}") for i in range(TB)]
        v_in, b_in = [sem("v_in0"), sem("v_in1")], [sem("b_in0"), sem("b_in1")]
        vn_f, vn_hi, vn_lo = sem("vn_f"), sem("vn_hi"), sem("vn_lo")
        sv_done, sv_out, u_out, u_gelu = sem("sv_done"), sem("sv_out"), sem("u_out"), sem("u_gelu")
        y_f, y_hi, y_lo = sem("y_f"), sem("y_hi"), sem("y_lo")
        out_done = sem("out_done")

        X_OUTA, X_OUT = 8, 16
        X_FFN0 = X_OUT + FG * KB
        X_GMLP = X_FFN0 + GG * KB
        X_END = X_GMLP + FG * KB

        def unit(u):
            t = u % TB
            return t, 64 * (u // TB), min(t + 1, 5) * P, max(0, t - 4) * P

        vblk = [tA[:], tG[:, 2:2 + S]]

        block = ctx.enter_context(nc.Block())

        def col(c):
            return par[:, c:c + 1]

        @block.sync
        def _(sp):
            def tile(t, slot):
                sp.wait_ge(w_lo, t - 1)
                sp.dma_start(raw[:, slot, :], wstream[t]).then_inc(raw_in[slot], 16)

            sp.dma_start(par[:], params).then_inc(par_in, 16)
            for m in range(KB):
                sp.dma_start(x[:, m, :], xT[m * P:(m + 1) * P, :]).then_inc(x_in[m], 16)
                if m == 0:
                    sp.dma_start(raw[:, 0, :], wstream[0]).then_inc(raw_in[0], 16)
                if m == 2:
                    sp.dma_start(raw[:, 1, :], wstream[1]).then_inc(raw_in[1], 16)
            sp.dma_start(etab[:, 383:383 + NREL], rel).then_inc(rel_in, 16)
            sp.dma_start(swsp[:], wsp).then_inc(pos_in, 16)
            sp.dma_start(sbsp[:], bsp.partition_broadcast(P)).then_inc(pos_in, 16)
            sp.wait_ge(e_ready, 2)
            sp.dma_start(e_dram, etab[:].unsqueeze(1).broadcast_to([NH, P, RELW])).then_inc(e_out, 16)
            sp.wait_ge(pos_masked, 1)
            sp.dma_start(w_dram, swsp[:]).then_inc(pos_out, 16)
            with sp.Fori(1, T_QKV // 2) as i:
                tile(2 * i, 0)
                tile(2 * i + 1, 1)
            sp.wait_ge(pos_bias, GB)
            sp.dma_start(b_dram, sBt[:].rearrange("p b t -> p (b t)")).then_inc(pos_out, 16)
            with sp.Fori(T_QKV // 2, (T_OUT + 2) // 2) as i:
                tile(2 * i, 0)
                tile(2 * i + 1, 1)
            sp.wait_ge(e_out, 16)
            sp.wait_ge(w_used, T_OUT - 2)
            for p in range(NPAIR):
                for hd in range(2):
                    if p:
                        sp.wait_ge(sc_max, 16 * (p - 1) + 8 * hd + 8)
                    rows = bass.AP(tensor=e_dram.tensor, offset=(2 * p + hd) * P * RELW + P - 1,
                                   ap=[[RELW - 1, P], [1, BANDW]])
                    sp.dma_start(bias[:, hd, :], rows).then_inc(bias_in[hd], 16)
            sp.wait_ge(qn_ready, 2 * NPAIR)
            for m in range(KB):
                sp.dma_start(x[:, m, :], xT[m * P:(m + 1) * P, :]).then_inc(x_in[m], 16)
            with sp.Fori((T_OUT + 2) // 2, (T_FFN0 + 4) // 2) as i:
                tile(2 * i, 0)
                tile(2 * i + 1, 1)
            with sp.Fori((T_FFN0 + 4) // 2, (T_GMLP + 2) // 2) as i:
                tile(2 * i, 0)
                tile(2 * i + 1, 1)
            sp.wait_ge(pos_out, 32)
            sp.wait_ge(x_add, X_FFN0)
            sp.dma_start(wspr[:], w_dram).then_inc(wsp_in, 16)
            tile(T_V, 0)
            tile(T_V + 1, 1)
            with sp.Fori(0, 4) as c:
                for q in range(4):
                    tile(4 * c + (T_V + 2 + q), q % 2)
                for pos, tok in enumerate(SWEEP):
                    sp.wait_ge(v_gelu, 8 * c + (pos + 1))
                    sp.sem_inc(v_seen, 1)
                    sp.dma_start(v_dram[tok * P:(tok + 1) * P, bass.ts(c, HALF)], vst[:, pos, :]).then_inc(v_out[pos], 16)
            for s in v_out:
                sp.wait_ge(s, 16 * 4)

            def vblock(b, j):
                if not isinstance(b, int) or b >= 2:
                    sp.wait_ge(vn_lo, b - 1)
                    sp.wait_ge(sv_out, b - 1)
                sp.dma_start(vblk[j].rearrange("p (c d) -> p c d", c=TB),
                             v_blocks[:, :, bass.ts(b, P)]).then_inc(v_in[j], 16)
                sp.dma_start(bblk[:, j * P:(j + 1) * P], b_dram[:, bass.ts(b, P)]).then_inc(b_in[j], 16)

            sp.wait_ge(st_row, ST_N2 + 1)
            vblock(0, 0)
            vblock(1, 1)
            tile(T_GLOOP + 2, 0)
            tile(T_GLOOP + 3, 1)
            tile(T_GLOOP + 4, 0)
            vblock(2, 0)
            tile(T_GLOOP + 5, 1)
            vblock(3, 1)
            with sp.Fori(2, GG) as i:
                tile(4 * i + (T_GLOOP - 2), 0)
                vblock(2 * i, 0)
                tile(4 * i + (T_GLOOP - 1), 1)
                tile(4 * i + T_GLOOP, 0)
                tile(4 * i + (T_GLOOP + 1), 1)
                vblock(2 * i + 1, 1)
            with sp.Fori(T_FFN1 // 2, (T_FFN1 + 4) // 2) as i:
                tile(2 * i, 0)
                tile(2 * i + 1, 1)
            with sp.Fori((T_FFN1 + 4) // 2, NT // 2) as i:
                tile(2 * i, 0)
                tile(2 * i + 1, 1)
            for m in range(KB):
                sp.wait_ge(x_add, X_END - KB + m + 1)
                sp.dma_start(outT[m * P:(m + 1) * P, :], x[:, m, :]).then_inc(out_done, 16)
            sp.wait_ge(out_done, 16 * KB)

        @block.gpsimd
        def _(pool):
            pool.memset(ones[:], 1.0).then_inc(const, 1)
            pool.memset(epsc[:], EPS).then_inc(const, 1)
            pool.memset(ident[:], 0.0).then_inc(const, 1)
            pool.wait_ge(const, 3)
            pool.affine_select(out=ident[:], in_=ident[:], compare_op=ALU.not_equal, fill=1.0, base=0,
                               pattern=[[-1, P]], channel_multiplier=1).then_inc(const, 1)
            pool.memset(tG[:, 0:2], 0.0).then_inc(const, 1)

            def norm_sums(n):
                for m in range(1, KB):
                    pool.wait_ge(n_sq, 8 * n + m + 1)
                    if m > 1:
                        pool.wait_ge(n_sum, 7 * n + m - 1)
                    pool.tensor_tensor(tA[:], tA[:], (tC, tU)[m % 2][:], ALU.add).then_inc(n_sum, 1)

            norm_sums(0)
            pool.memset(etab[:, 383 + NREL:RELW], 0.0).then_inc(e_ready, 1)
            pool.wait_ge(rel_in, 16)
            pool.tensor_copy(etab[:, 0:383], etab[:, 383:384].broadcast_to([NH, 383])).then_inc(e_ready, 1)
            pool.wait_ge(pos_in, 32)
            w3 = swsp[:].rearrange("s (g t) -> s g t", g=GG)
            pool.affine_select(out=w3, in_=w3, compare_op=ALU.is_ge, fill=0.0, base=0,
                               pattern=[[0, GG], [1, P]], channel_multiplier=-1).then_inc(pos_masked, 1)
            pool.wait_ge(e_out, 16)
            pool.memset(cv[:, 0:CB, 0:LEFT], 0.0).then_inc(cv_pad, 1)
            pool.wait_ge(qk_rinv, 1)
            rq4 = rqk[:].rearrange("p (c t h) -> p c t h", c=2, t=TB)
            last = CB - 1
            last_acc = cv[:, (last + CB) % (CB + 1), LEFT:LEFT + S]

            def late_taps(k0, k1):
                for k in range(k0, k1):
                    n = k - (2 + LATE)
                    if n:
                        pool.wait_ge(cv_late, n)
                    pool.tensor_scalar(tA[:], cv[:, last, k:k + S], col(C_CONVW + last * TAPS + k), None, ALU.mult).then_inc(cv_prod, 1)
                    pool.wait_ge(cv_prod, n + 1)
                    pool.tensor_tensor(last_acc, last_acc, tA[:], ALU.add).then_inc(cv_late, 1)

            pool.wait_ge(cv_first, 2 * CB)
            for p in range(NPAIR):
                if p:
                    pool.wait_ge(qt_done, 2 * p)
                    pool.wait_ge(bias_ok, 4 * p)
                for c, buf in ((0, tC), (1, tU)):
                    pool.tensor_tensor(
                        buf[:].rearrange("p (t h d) -> p t h d", t=TB, h=2),
                        qk[:, c, :, p * P:(p + 1) * P].rearrange("p t (h d) -> p t h d", h=2),
                        rq4[:, c, :, 2 * p:2 * p + 2].unsqueeze(3).broadcast_to([P, TB, 2, HD]),
                        ALU.mult).then_inc(qn_ready, 1)
                for hd in range(2):
                    if p:
                        k1 = 2 + LATE + 4 * (2 * p - 1 + hd)
                        pool.wait_ge(bias_ok, 4 * p + 2 * hd)
                        late_taps(k1 - 4, k1)
                        pool.wait_ge(cv_late, k1 - 2 - LATE)
                    pool.wait_ge(qn_ready, 2 * p + 2)
                    pool.wait_ge(bias_in[hd], 16 * p + 16)
                    if hd:
                        pool.wait_ge(bias_ok, 4 * p + 2)
                    pool.memset(bias[0:64, hd, BANDW - 64:BANDW], MASKED).then_inc(bias_ok, 1)
                    pool.wait_ge(bias_ok, 4 * p + 2 * hd + 1)
                    pool.memset(bias[64:128, hd, 0:64], MASKED).then_inc(bias_ok, 1)
            pool.wait_ge(bias_ok, 4 * NPAIR)
            late_taps(2 + LATE + 8 * (NPAIR - 1), TAPS)
            pool.wait_ge(cv_late, TAPS - 2 - LATE)

            def conv_out(m):
                return cv[:, (m + CB) % (CB + 1), LEFT:LEFT + S]

            for m in range(1, CB):
                if m > 1:
                    pool.wait_ge(ln_sum0, m - 1)
                if m == last:
                    pool.wait_ge(cv_tap, last * (TAPS - 2) + LATE)
                    pool.tensor_tensor(last_acc, last_acc, tG[:, 2:2 + S], ALU.add).then_inc(cv_done, 1)
                    pool.wait_ge(cv_done, CB)
                pool.tensor_tensor(tA[:], conv_out(0) if m == 1 else tA[:], conv_out(m), ALU.add).then_inc(ln_sum0, 1)
            for m in range(1, CB):
                pool.wait_ge(ln_sq, m + 1)
                if m > 1:
                    pool.wait_ge(ln_sum, m - 1)
                pool.tensor_tensor(tA[:], tA[:], (tC, tU)[m % 2][:], ALU.add).then_inc(ln_sum, 1)
            norm_sums(1)
            norm_sums(2)
            norm_sums(3)

        @block.tensor
        def _(pe):
            def fm_block(slot, ps, ks, first=0, n=KB, kwait=None):
                for pos in range(first, first + n):
                    k = ks[pos]
                    if kwait:
                        kwait(pos)
                    for w, h in ((wh, hh), (wh, hl), (wl, hh)):
                        for s in range(2):
                            mm = pe.matmul(ps[:, s * HALF:(s + 1) * HALF], w[:, slot, k * P:(k + 1) * P],
                                           h[:, k, s * HALF:(s + 1) * HALF],
                                           start=(pos == 0 and w is wh and h is hh),
                                           stop=(pos == len(ks) - 1 and w is wl))
                return mm

            def stats(st):
                for t in range(TB):
                    mm = pe.matmul(PS[2][:, t:t + 1], tA[:, t * P:(t + 1) * P], ones[:, 0:1], start=True, stop=True)
                mm.then_inc(st_sum, 1)

            def rows(st):
                pe.wait_ge(st_diag, st + 1)
                for s in range(2):
                    mm = pe.matmul(PS[3][:, s * HALF:(s + 1) * HALF], ones[:], tG[:, 2 + s * HALF:2 + (s + 1) * HALF],
                                   start=True, stop=True)
                mm.then_inc(st_row, 1)

            def first_two(n, t, slots, free0, free1):
                st = (ST_N0, ST_N1, ST_N2, ST_N3)[n]
                ks = NORM_ORDER[n]
                pe.wait_ge(w_lo, t + 1)
                free0()
                fm_block(slots[0], PS[0], ks, kwait=lambda pos: pe.wait_ge(n_lo, 8 * n + pos + 1)).then_inc(w_used, 1)
                pe.wait_ge(n_sum, 7 * (n + 1))
                stats(st)
                pe.wait_ge(w_lo, t + 2)
                free1()
                fm_block(slots[1], PS[1], ks, 0, 4)
                rows(st)
                fm_block(slots[1], PS[1], ks, 4, 4).then_inc(w_used, 1)

            def token_tile(t, j, free):
                pe.wait_ge(w_lo, t + 1)
                for kk in range(2):
                    k = 2 * j + kk
                    for pos, tok in enumerate(SWEEP):
                        if k == 0:
                            free(pos)
                        for w, h in ((wh, hh), (wl, hh), (wh, hl)):
                            mm = pe.matmul(bank(tok), h[:, k, tok * P:(tok + 1) * P], w[:, j, kk * HALF:(kk + 1) * HALF],
                                           start=(k == 0 and w is wh and h is hh), stop=(k == KB - 1 and h is hl))
                        if k == KB - 1 and pos < TB - 1:
                            mm.then_inc(tok_done, 1)
                mm.then_inc(w_used, 1)

            pe.wait_ge(const, 5)
            first_two(0, 0, (SA, SB), lambda: None, lambda: None)
            pe.wait_ge(pos_masked, 1)
            pe.wait_ge(st_rb, 1)
            for s in range(2):
                mm = pe.matmul(PS[3][:, s * HALF:(s + 1) * HALF], ones[:], swsp[:, s * HALF:(s + 1) * HALF], start=True, stop=True)
            mm.then_inc(pos_rows, 1)
            with pe.Fori(1, CB) as m:
                pe.wait_ge(w_lo, 2 * m + 1)
                pe.wait_ge(lin_out, m)
                fm_block(SA, PS[0], range(KB)).then_inc(w_used, 1)
                pe.wait_ge(w_lo, 2 * m + 2)
                pe.wait_ge(gate_out, m)
                fm_block(SB, PS[1], range(KB)).then_inc(w_used, 1)
            with pe.Fori(0, 3) as c:
                for j in range(4):
                    token_tile(4 * c + (T_QKV + j), j, lambda pos: pe.wait_ge(tok_free, 8 * c + (pos + 1)))

            def turn_qk(p, c):
                pe.wait_ge(qn_ready, 2 * p + (c + 1))
                if not isinstance(p, int) or p:
                    pe.wait_ge(sc_max, 16 * p + (c - 1))
                for t in range(TB):
                    mm = pe.transpose(PS[c][:, t * P:(t + 1) * P], (tC, tU)[c][:, t * P:(t + 1) * P], ident[:])
                mm.then_inc(qt_done, 1)

            def scores(p, u):
                t, r, w, k0 = unit(u)
                if u == 0:
                    pe.wait_ge(qt_lo, 3 * p + 2)
                if u >= 2:
                    pe.wait_ge(sc_max, 16 * p + (u - 1))
                n = w if w <= HALF else w // 2
                for a in range(w // n):
                    for q, k in ((qth, kth), (qth, ktl), (qtl, kth)):
                        mm = pe.matmul(PS[u % 2][:, a * HALF:a * HALF + n], q[r:r + 64, t * P:(t + 1) * P],
                                       k[r:r + 64, k0 + a * n:k0 + (a + 1) * n],
                                       start=(q is qth and k is kth), stop=(q is qtl))
                mm.then_inc(sc_done, 1)

            def turn(p, u):
                t, r, w, k0 = unit(u)
                pe.wait_ge(p_norm, 16 * p + (u + 1))
                if u:
                    pe.wait_ge(pt_lo, 16 * p + u)
                for b in range(w // P):
                    mm = pe.transpose(PS[2][:, b * P:(b + 1) * P], prob[:, u % 3, b * P:(b + 1) * P], ident[:])
                mm.then_inc(pt_done, 1)

            def values(p, u):
                t, r, w, k0 = unit(u)
                pe.wait_ge(pt_lo, 16 * p + (u + 1))
                if u == 0:
                    pe.wait_ge(qt_lo, 3 * p + 3)
                if u % 2 == 0 and u >= 4:
                    pe.wait_ge(o_sum, 8 * p + (u // 2 - 1))
                c0 = u // 2 % 2 * HALF + u % 2 * 2 * P
                for b in range(w // P):
                    for v in (vh, vl):
                        mm = pe.matmul(PS[3][:, c0:c0 + 2 * P], v[:, k0 // P + b, :],
                                       ptr[u % 2][:, b, :, :].rearrange("p a n -> p (a n)"),
                                       start=(b == 0 and v is vh), stop=(b == w // P - 1 and v is vl))
                mm.then_inc(pv_done, 1)

            def pair(p, last=False):
                for s in range(16):
                    scores(p, s)
                    if s >= 2:
                        turn(p, s - 2)
                    if s >= 3:
                        values(p, s - 3)
                if not last:
                    turn_qk(p + 1, 0)
                turn(p, 14)
                if not last:
                    turn_qk(p + 1, 1)
                values(p, 13)
                turn(p, 15)
                values(p, 14)
                values(p, 15)

            pe.wait_ge(tok_free, 8 + 24)
            turn_qk(0, 0)
            turn_qk(0, 1)
            with pe.Fori(0, NPAIR - 1) as p:
                pair(p)
            pair(NPAIR - 1, last=True)

            pe.wait_ge(ln_sum0, CB - 1)
            pe.wait_ge(pt_lo, 16 * NPAIR)
            for s in range(2):
                mm = pe.matmul(PS[2][:, s * HALF:(s + 1) * HALF], ones[:], tA[:, s * HALF:(s + 1) * HALF], start=True, stop=True)
            mm.then_inc(ln_mean, 1)

            def out_tile(j, k0):
                t = T_OUT + j
                pe.wait_ge(w_lo, t + 1)
                for odd in range(2):
                    n = 2 * j + odd
                    if n >= 2:
                        pe.wait_ge(x_add, n - 1)
                    else:
                        pe.wait_ge(sc_max, 16 * NPAIR)
                    for k in range(4):
                        for w, h in ((wh, hh), (wh, hl), (wl, hh)):
                            for s in range(2):
                                mm = pe.matmul(PS[n % 2][:, s * HALF:(s + 1) * HALF],
                                               w[:, j % 2, k * 256 + odd * P:k * 256 + (odd + 1) * P],
                                               h[:, k0 + k, s * HALF:(s + 1) * HALF],
                                               start=(k == 0 and w is wh and h is hh), stop=(k == 3 and w is wl))
                    mm.then_inc(w_used if odd else m_done, 1)

            pe.wait_ge(o_lo, 8 * NPAIR)
            out_tile(0, 4)
            pe.wait_ge(ln_sum, CB - 1)
            stats(ST_LN)
            out_tile(1, 4)
            rows(ST_LN)
            out_tile(2, 4)
            out_tile(3, 4)
            pe.wait_ge(ln_lo, CB)
            for j in range(4, 8):
                out_tile(j, 0)

            def down(slots, h0, x0):
                for m in range(KB):
                    pe.wait_ge(x_add, x0 + (m - 1))
                    for j in range(2):
                        for w, h in ((wh, hidh), (wh, hidl), (wl, hidh)):
                            for s in range(2):
                                mm = pe.matmul(PS[2 + m % 2][:, s * HALF:(s + 1) * HALF], w[:, slots[j], m * P:(m + 1) * P],
                                               h[:, h0 + j, s * HALF:(s + 1) * HALF],
                                               start=(j == 0 and w is wh and h is hidh), stop=(j == 1 and w is wl))
                    if m < KB - 1:
                        mm.then_inc(m_done, 1)
                mm.then_inc(w_used, 2)

            def ffn(f, n, t0, x0):
                b0 = FB * f
                first_two(n, t0, (SC, SD), lambda: pe.wait_ge(x_add, x0), lambda: None)
                for q, (slot, ps, done) in enumerate(((SA, PS[0], g_out), (SB, PS[1], up_out))):
                    pe.wait_ge(w_lo, t0 + 3 + q)
                    pe.wait_ge(done, b0 + 1)
                    fm_block(slot, ps, range(KB)).then_inc(w_used, 1)

                def group(i, odd):
                    t = 6 * i + (t0 - 2)
                    for q in range(4):
                        pe.wait_ge(w_lo, t + (q + 1))
                        pe.wait_ge((g_out, up_out)[q % 2], 2 * i + (b0 + q // 2))
                        fm_block(q % 2, PS[q % 2], range(KB)).then_inc(w_used, 1)
                    pe.wait_ge(w_lo, t + 6)
                    pe.wait_ge(hid_lo, 2 * i + b0)
                    down((SC, SD), 2 * (1 - odd), 8 * i + (x0 - 8))

                with pe.Fori(0, FG // 2) as ii:
                    group(2 * ii + 1, 1)
                    group(2 * ii + 2, 0)
                pe.wait_ge(w_lo, t0 + 3 * FB)
                pe.wait_ge(hid_lo, b0 + FB)
                down((SA, SB), 0, x0 + 8 * (FG - 1))

            ffn(0, 1, T_FFN0, X_OUT)

            first_two(2, T_GMLP, (SC, SD), lambda: pe.wait_ge(x_add, X_FFN0), lambda: None)
            for j in range(4):
                token_tile(T_V + j, j, lambda pos: pe.wait_ge(tok_free, 32 + 8))
            with pe.Fori(1, 4) as c:
                for j in range(4):
                    token_tile(4 * c + (T_V + j), j, lambda pos: pe.wait_ge(v_gelu, 8 * c + (pos - 7)))

            def positions(b, i, ps):
                pe.wait_ge(vn_lo, b + 1)
                for c in range(TB):
                    for v, w in ((vnh, wsph), (vnh, wspl), (vnl, wsph)):
                        mm = pe.matmul(ps[:, c * P:(c + 1) * P], v[:, c * P:(c + 1) * P], w[:, bass.ts(i, P)],
                                       start=(v is vnh and w is wsph), stop=(v is vnl))
                mm.then_inc(sv_done, 1)

            def mix(i, j):
                pe.wait_ge(sv_out, 2 * i + (j - 1))
                if j == 0:
                    pe.wait_ge(x_add, 8 * i + (X_FFN0 - 8))
                positions(2 * i + j, i, PS[2 + j])

            def u_tile(i, j):
                pe.wait_ge(w_lo, 4 * i + (T_GLOOP - 3 + j))
                pe.wait_ge(u_out, 2 * i + (j - 1))
                fm_block(j, PS[j], range(KB)).then_inc(w_used, 1)

            def gmlp_down(i, odd):
                pe.wait_ge(w_lo, 4 * i + T_GLOOP)
                pe.wait_ge(y_lo, 2 * i)
                pe.wait_ge(sv_out, 2 * i + 1)
                down_after_positions(i, odd)

            def down_after_positions(i, odd):
                x0 = 8 * i + (X_FFN0 - 8)
                for m in range(KB):
                    if m == 1:
                        pe.wait_ge(sv_out, 2 * i + 2)
                    if m >= 2:
                        pe.wait_ge(x_add, x0 + (m - 1))
                    for j in range(2):
                        for w, h in ((wh, hidh), (wh, hidl), (wl, hidh)):
                            for s in range(2):
                                mm = pe.matmul(PS[2 + m % 2][:, s * HALF:(s + 1) * HALF], w[:, (SC, SD)[j], m * P:(m + 1) * P],
                                               h[:, 2 * (1 - odd) + j, s * HALF:(s + 1) * HALF],
                                               start=(j == 0 and w is wh and h is hidh), stop=(j == 1 and w is wl))
                    if m < KB - 1:
                        mm.then_inc(m_done, 1)
                mm.then_inc(w_used, 2)

            pe.wait_ge(v_gelu, 32)
            pe.wait_ge(wsp_lo, 1)
            u_tile(1, 0)
            positions(0, 0, PS[2])
            u_tile(1, 1)
            positions(1, 0, PS[3])
            mix(1, 0)
            mix(1, 1)
            gmlp_down(1, 1)

            def gmlp_group(i, odd):
                for j in range(2):
                    u_tile(i, j)
                    mix(i, j)
                gmlp_down(i, odd)

            with pe.Fori(0, (GG - 2) // 2) as ii:
                gmlp_group(2 * ii + 2, 0)
                gmlp_group(2 * ii + 3, 1)
            pe.wait_ge(w_lo, T_FFN1)
            pe.wait_ge(y_lo, GB)
            down((SA, SB), 2, X_FFN0 + 8 * (GG - 1))
            ffn(1, 3, T_FFN1, X_GMLP)

        def outputs(j):
            r, c0 = 64 * (j // 4), j % 4 * 2 * P
            cols = PS[3][r:r + 64, j % 2 * HALF:(j % 2 + 1) * HALF].rearrange("p (u x n) -> p x u n", u=2, x=2)
            return slice(r, r + 64), slice(c0, c0 + 2 * P), cols

        @block.scalar
        def _(act):
            def split(t, slot, raw_slot, freed_by):
                act.wait_ge(raw_in[raw_slot], (t // 2 + 1) * 16)
                if freed_by is not None:
                    act.wait_ge(w_used, freed_by + 1)
                act.activation(wh[:, slot, :], raw[:, raw_slot, :], ACT.Copy).then_inc(w_hi, 1)

            def split_r(t, half, slot, raw_slot, back):
                act.wait_ge(raw_in[raw_slot], half * 16 + 16)
                act.wait_ge(w_used, t + (1 - back))
                act.activation(wh[:, slot, :], raw[:, raw_slot, :], ACT.Copy).then_inc(w_hi, 1)

            def norm_hi(n, m):
                act.activation(hh[:, m, :], x[:, m, :], ACT.Copy, scale=col(NORM_G[n] + m)).then_inc(n_hi, 1)

            def norm_sq(n, m):
                if m >= 3:
                    act.wait_ge(n_sum, 7 * n + m - 2)
                act.activation((tA if m == 0 else (tC, tU)[m % 2])[:], x[:, m, :], ACT.Square).then_inc(n_sq, 1)

            def take_root(st, count):
                act.wait_ge(st_sum, st + 1)
                act.activation(root[:], PS[2][:, 0:TB], ACT.Sqrt, scale=1.0 / count, bias=epsc[:, 0:1]).then_inc(st_root, 1)

            def copy_rows(st):
                act.wait_ge(st_row, st + 1)
                act.activation(rstdB[:], PS[3][:], ACT.Copy).then_inc(st_rb, 1)

            act.wait_ge(par_in, 16)
            act.wait_ge(const, 5)
            for m in range(KB):
                act.wait_ge(x_in[m], 16)
                norm_hi(0, m)
                if m in (1, 3):
                    split(m // 2, m // 2, m // 2, None)
                norm_sq(0, m)
            take_root(ST_N0, D)
            split(2, SA, 0, 0)
            copy_rows(ST_N0)
            act.preload_act_table(ACT.Sigmoid)

            def conv_first(m):
                if m:
                    act.wait_ge(cv_done, m)
                src = cv[:, m, :]
                act.activation(cv[:, (m + CB) % (CB + 1), LEFT:LEFT + S], src[:, 0:S], ACT.Identity,
                               scale=col(C_CONVW + m * TAPS), bias=col(C_CONVB + m)).then_inc(cv_first, 1)
                act.activation(tG[:, 2:2 + S], src[:, 1:1 + S], ACT.Copy,
                               scale=col(C_CONVW + m * TAPS + 1)).then_inc(cv_first, 1)

            for m in range(CB):
                if m:
                    split(2 * m + 2, SA, 0, 2 * m)
                act.wait_ge(gate_out, m + 1)
                act.activation(tU[:], tU[:], ACT.Sigmoid).then_inc(sig, 1)
                split(2 * m + 3, SB, 1, 2 * m + 1)
                if m == 0:
                    act.wait_ge(glu, 1)
                    conv_first(0)
            act.wait_ge(st_rb, 1)
            act.wait_ge(st_root, 1)
            act.wait_ge(pos_bias, GB)
            act.sem_inc(tok_free, 4)
            act.wait_ge(lin_out, CB)
            act.wait_ge(gate_out, CB)
            act.sem_inc(tok_free, 4)
            conv_first(1)

            for c in range(3):
                for q in range(4):
                    t = T_QKV + 2 + 4 * c + q
                    split(t, (t - T_QKV) % 4, t % 2, t - 4)
                    if 4 * c + q == 5:
                        conv_first(2)
                if c == 2:
                    conv_first(3)
                    act.wait_ge(pos_out, 32)
                for pos, tok in enumerate(SWEEP):
                    if pos < TB - 1:
                        act.wait_ge(tok_done, 7 * c + pos + 1)
                    else:
                        act.wait_ge(w_used, T_QKV + 4 * c + 4)
                    dst = qk[:, c, tok, :] if c < 2 else vraw[:, tok, :]
                    act.activation(dst, bank(tok), ACT.Copy, scale=rcol[:, tok:tok + 1]).then_inc(tok_free, 1)
                if c < 2:
                    for j in range(4):
                        n = 4 * c + j
                        act.wait_ge(tok_free, 8 + 8 * c + 8)
                        if n >= 2:
                            act.wait_ge(qk_sum, n - 1)
                        act.activation((tC, tU)[j % 2][:], qk[:, c, 2 * j:2 * j + 2, :].rearrange("p t d -> p (t d)"),
                                       ACT.Square).then_inc(qk_sq, 1)
                if c == 1:
                    act.wait_ge(qk_sum, 8)
                    act.activation(rqk[:], ssq[:], ACT.Sqrt, scale=1.0 / HD, bias=epsc[:, 0:1]).then_inc(qk_root, 1)
            act.activation(qgs[:], col(C_QG), ACT.Copy, scale=float(HD) ** -0.5).then_inc(qg_ready, 1)
            act.preload_act_table(ACT.Exp)
            act.wait_ge(qg_ready, 1)
            act.wait_ge(tok_free, 8 + 24)

            def q_high(p):
                act.wait_ge(qt_done, 2 * p + 1)
                act.activation(qth[:], PS[0][:], ACT.Copy, scale=qgs[:, 0:1]).then_inc(qt_hi, 1)

            def k_high(p):
                act.wait_ge(qt_done, 2 * p + 2)
                act.activation(kth[:], PS[1][:], ACT.Copy, scale=col(C_KG)).then_inc(qt_hi, 1)

            def v_high(p):
                act.activation(vh[:], vraw[:, :, bass.ts(p, P)], ACT.Copy).then_inc(qt_hi, 1)

            def exponentials(p, u):
                w = unit(u)[2]
                act.wait_ge(sc_max, 16 * p + (u + 1))
                act.activation(prob[:, u % 3, 0:w], prob[:, u % 3, 0:w], ACT.Exp, scale=-1.0,
                               bias=negmax[:, u % 3:u % 3 + 1], accum_out=rsum[:, u % 3:u % 3 + 1]).then_inc(exp_done, 1)

            def p_high(p, u):
                w = unit(u)[2]
                act.wait_ge(pt_done, 16 * p + (u + 1))
                if u >= 2:
                    act.wait_ge(pv_done, 16 * p + (u - 1))
                act.activation(ptr[u % 2][:, 0:w // P, 0, :], PS[2][:, 0:w].rearrange("p (b n) -> p b n", n=P),
                               ACT.Copy).then_inc(pt_hi, 1)

            def o_copy(p, j):
                rows, toks, cols = outputs(j)
                act.wait_ge(pv_done, 16 * p + (2 * j + 2))
                if j >= 2:
                    act.wait_ge(o_lo, 8 * p + (j - 1))
                act.activation(osum[rows, j % 2, :].rearrange("p (u n) -> p u n", u=2), cols[:, 1], ACT.Copy).then_inc(o_cross, 1)

            def o_high(p, j):
                rows, toks, cols = outputs(j)
                act.wait_ge(o_sum, 8 * p + (j + 1))
                act.activation(hh[rows, bass.ds(p + 4, 1), toks].rearrange("p a n -> p (a n)"), osum[rows, j % 2, :],
                               ACT.Copy).then_inc(o_hi, 1)

            def pair(p, last=False):
                v_high(p)
                for s in range(16):
                    if s >= 2:
                        p_high(p, s - 2)
                    exponentials(p, s)
                    if s >= 6 and s % 2 == 0:
                        o_high(p, s // 2 - 3)
                    if s >= 5 and s % 2 == 1:
                        o_copy(p, s // 2 - 2)
                if not last:
                    q_high(p + 1)
                p_high(p, 14)
                o_high(p, 5)
                if not last:
                    k_high(p + 1)
                o_copy(p, 6)
                p_high(p, 15)
                o_high(p, 6)
                o_copy(p, 7)
                o_high(p, 7)
                act.wait_ge(pv_done, 16 * p + 16)

            q_high(0)
            k_high(0)
            with act.Fori(0, NPAIR - 1) as p:
                pair(p)
            pair(NPAIR - 1, last=True)

            def conv_out(m):
                return cv[:, (m + CB) % (CB + 1), LEFT:LEFT + S]

            for m in range(CB):
                act.wait_ge(ln_cent, m + 1)
                if m == 3:
                    act.wait_ge(ln_sum, 1)
                act.activation((tA if m == 0 else (tC, tU)[m % 2])[:], conv_out(m), ACT.Square).then_inc(ln_sq, 1)
            split(T_OUT + 2, SA, 0, T_OUT)
            take_root(ST_LN, CONVW)
            split(T_OUT + 3, SB, 1, T_OUT + 1)
            copy_rows(ST_LN)
            for m in range(CB):
                act.wait_ge(ln_mul, m + 1)
                act.activation(conv_out(m), conv_out(m), ACT.Silu, scale=col(C_LNG + m), bias=col(C_LNB + m)).then_inc(ln_act, 1)
                act.wait_ge(ln_act, m + 1)
                act.activation(hh[:, m, :], conv_out(m), ACT.Copy).then_inc(ln_hi, 1)
            split(T_OUT + 4, SA, 0, T_OUT + 2)
            split(T_OUT + 5, SB, 1, T_OUT + 3)
            split(T_OUT + 6, SA, 0, T_OUT + 4)
            for m in (0, 1):
                act.wait_ge(x_add, X_OUTA + m + 1)
                norm_sq(1, m)
            split(T_OUT + 7, SB, 1, T_OUT + 5)
            split(T_FFN0, SC, 0, T_OUT)
            split(T_FFN0 + 1, SD, 1, T_OUT + 1)
            for m in (2, 3):
                act.wait_ge(x_add, X_OUTA + m + 1)
                norm_sq(1, m)
            split(T_FFN0 + 2, SA, 0, T_OUT + 6)
            for m in (4, 5):
                act.wait_ge(x_add, X_OUTA + m + 1)
                norm_hi(1, m)
                norm_sq(1, m)
            act.wait_ge(w_used, T_FFN0)
            for m in range(4):
                norm_hi(1, m)
            for m in (6, 7):
                act.wait_ge(x_add, X_OUTA + m + 1)
                norm_hi(1, m)
                norm_sq(1, m)
            split(T_FFN0 + 3, SB, 1, T_OUT + 7)
            take_root(ST_N1, D)
            copy_rows(ST_N1)

            def ffn(f, t0, x0, last_n):
                b0 = FB * f
                act.preload_act_table(ACT.Silu)

                def gate(b, f0):
                    act.wait_ge(g_out, b + (b0 + 1))
                    dw = par[:, bass.ds(f0, 4)]
                    act.activation(tC[:], tG[:, 2:2 + S], ACT.Identity, scale=dw[:, 2:3], bias=dw[:, 3:4]).then_inc(g_tap2, 1)
                    act.wait_ge(g_tap0, b + (b0 + 1))
                    act.activation(tC[:], tC[:], ACT.Silu).then_inc(g_silu, 1)

                def hidden(b, slot, free):
                    act.wait_ge(hid, b + (b0 + 1))
                    if free is not None:
                        act.wait_ge(w_used, free)
                    act.activation(hidh[:, slot, :], tU[:], ACT.Copy).then_inc(hid_hi, 1)

                dw0 = C_DW + 4 * FB * f
                gate(0, dw0)
                hidden(0, 0, None)
                gate(1, dw0 + 4)
                split(t0 + 4, SA, 0, t0 + 2)
                split(t0 + 5, SB, 1, t0 + 3)
                hidden(1, 1, None)

                def group(i, ih, odd):
                    t, h = 6 * i + (t0 - 2), ih + (t0 - 2) // 2
                    split_r(t + 2, h + 1, SA, 0, 2)
                    gate(2 * i, 8 * i + dw0)
                    split_r(t + 3, h + 1, SB, 1, 2)
                    hidden(2 * i, 2 * odd, t)
                    split_r(t + 4, h + 2, SC, 0, 6)
                    split_r(t + 5, h + 2, SD, 1, 6)
                    gate(2 * i + 1, 8 * i + (dw0 + 4))
                    split_r(t + 6, h + 3, SA, 0, 4)
                    split_r(t + 7, h + 3, SB, 1, 4)
                    hidden(2 * i + 1, 2 * odd + 1, t)

                with act.Fori(0, FG // 2) as ii:
                    group(2 * ii + 1, 6 * ii + 3, 1)
                    group(2 * ii + 2, 6 * ii + 6, 0)

            def norm_after(n, x0, tail, lo):
                act.wait_ge(*lo)
                for m in range(KB):
                    act.wait_ge(x_add, x0 + m + 1)
                    norm_hi(n, m)
                    norm_sq(n, m)
                for t, slot in tail:
                    split(t, slot, t % 2, t - 4)

            ffn(0, T_FFN0, X_OUT, 2)
            split(T_GMLP, SC, 0, T_GMLP - 4)
            split(T_GMLP + 1, SD, 1, T_GMLP - 3)
            norm_after(2, X_FFN0 - KB, ((T_V, SA), (T_V + 1, SB)), (hid_lo, FB))
            take_root(ST_N2, D)
            act.wait_ge(wsp_in, 16)
            act.activation(wsph[:], wspr[:], ACT.Copy).then_inc(wsp_hi, 1)
            copy_rows(ST_N2)
            act.preload_act_table(ACT.Gelu_apprx_tanh)
            for j in range(2):
                act.wait_ge(u_out, j + 1)
                act.activation(uearly[:, j, :], uearly[:, j, :], ACT.Gelu_apprx_tanh).then_inc(u_gelu, 1)
            act.wait_ge(st_rb, ST_N2 + 1)
            act.wait_ge(st_root, ST_N2 + 1)
            act.sem_inc(tok_free, 8)

            def v_group(c, first=False):
                for q in range(4):
                    split_r(4 * c + (T_V + 2 + q), 2 * c + ((T_V + 2 + q) // 2), (2 + q) % 4, q % 2, 4)
                for pos, tok in enumerate(SWEEP):
                    if pos < TB - 1:
                        act.wait_ge(tok_done, 7 * c + (21 + pos + 1))
                    else:
                        act.wait_ge(w_used, 4 * c + (T_V + 4))
                    if not first:
                        act.wait_ge(v_out[pos], 16 * c)
                        act.wait_ge(v_stat, 8 * c + (pos - 7))
                    act.activation(vst[:, pos, :], bank(tok), ACT.Gelu_apprx_tanh, scale=rcol[:, tok:tok + 1]).then_inc(v_gelu, 1)

            v_group(0, first=True)
            with act.Fori(1, 4) as c:
                v_group(c)
            act.wait_ge(v_mv, 1)
            act.activation(root[:], mv[:].rearrange("p (t a) -> p t a", a=2)[:, :, 1:2].rearrange("p t a -> p (t a)"),
                           ACT.Sqrt, bias=epsc[:, 0:1]).then_inc(v_root, 1)
            act.preload_act_table(ACT.Gelu_apprx_tanh)

            def vn_high(b, j):
                act.wait_ge(vn_f, b + 1)
                act.wait_ge(sv_done, b)
                act.activation(vnh[:], vblk[j], ACT.Copy).then_inc(vn_hi, 1)

            def y_high(b, slot, free):
                act.wait_ge(y_f, b + 1)
                if free is not None:
                    act.wait_ge(w_used, free)
                act.activation(hidh[:, slot, :], tC[:], ACT.Copy).then_inc(y_hi, 1)

            def gelu_u(b):
                act.wait_ge(u_out, b + 1)
                act.activation(tU[:], tU[:], ACT.Gelu_apprx_tanh).then_inc(u_gelu, 1)

            vn_high(0, 0)
            split(T_GLOOP + 2, SC, 0, T_GLOOP - 2)
            split(T_GLOOP + 3, SD, 1, T_GLOOP - 1)
            vn_high(1, 1)
            y_high(0, 0, None)
            vn_high(2, 0)
            y_high(1, 1, None)
            vn_high(3, 1)
            gelu_u(2)
            y_high(2, 2, None)
            split(T_GLOOP + 4, SA, 0, T_GLOOP)
            gelu_u(3)
            y_high(3, 3, None)
            split(T_GLOOP + 5, SB, 1, T_GLOOP + 1)

            def gmlp_group(i, odd):
                t, h = 4 * i + (T_GLOOP - 4), 2 * i + (T_GLOOP - 4) // 2
                split_r(t + 2, h + 1, SC, 0, 4)
                split_r(t + 3, h + 1, SD, 1, 4)
                vn_high(2 * i, 0)
                gelu_u(2 * i)
                vn_high(2 * i + 1, 1)
                y_high(2 * i, 2 * odd, t)
                split_r(t + 4, h + 2, SA, 0, 4)
                gelu_u(2 * i + 1)
                y_high(2 * i + 1, 2 * odd + 1, t)
                split_r(t + 5, h + 2, SB, 1, 4)

            with act.Fori(0, (GG - 2) // 2) as ii:
                gmlp_group(2 * ii + 2, 0)
                gmlp_group(2 * ii + 3, 1)
            split(T_FFN1, SC, 0, T_FFN1 - 4)
            split(T_FFN1 + 1, SD, 1, T_FFN1 - 3)
            norm_after(3, X_GMLP - KB, ((T_FFN1 + 2, SA), (T_FFN1 + 3, SB)), (y_lo, GB))
            take_root(ST_N3, D)
            copy_rows(ST_N3)
            ffn(1, T_FFN1, X_GMLP, None)

        @block.vector
        def _(dve):
            def split(t, slot, raw_slot):
                dve.wait_ge(w_hi, t + 1)
                dve.tensor_tensor(wl[:, slot, :], raw[:, raw_slot, :], wh[:, slot, :].bitcast(F32), ALU.subtract).then_inc(w_lo, 1)

            def norm_lo(n, m, pos):
                dve.wait_ge(n_hi, 8 * n + pos + 1)
                dve.scalar_tensor_tensor(out=hl[:, m, :], in0=x[:, m, :], scalar=col(NORM_G[n] + m),
                                         in1=hh[:, m, :].bitcast(F32), op0=ALU.mult, op1=ALU.subtract).then_inc(n_lo, 1)

            def inverse(st):
                dve.wait_ge(st_root, st + 1)
                dve.reciprocal(rcol[:], root[:]).then_inc(st_rcol, 1)
                dve.wait_ge(st_rcol, st + 1)
                dve.tensor_tensor(tG[:, 2:2 + S].rearrange("p (t n) -> p t n", t=TB),
                                  ident[:].unsqueeze(1).broadcast_to([P, TB, P]),
                                  rcol[:].unsqueeze(2).broadcast_to([P, TB, P]), ALU.mult).then_inc(st_diag, 1)

            dve.wait_ge(par_in, 16)
            for m in range(KB):
                norm_lo(0, m, m)
                if m in (1, 3):
                    split(m // 2, m // 2, m // 2)
            dve.wait_ge(const, 5)
            inverse(ST_N0)

            def taps(m, k0, k1):
                n0 = m * (TAPS - 2)
                src = cv[:, m, :]
                for k in range(k0, k1):
                    acc = cv[:, (m + CB) % (CB + 1), LEFT:LEFT + S] if k % 2 == 0 else tG[:, 2:2 + S]
                    if k < 4:
                        dve.wait_ge(cv_first, 2 * m + k - 1)
                    else:
                        dve.wait_ge(cv_tap, n0 + k - 3)
                    dve.scalar_tensor_tensor(out=acc, in0=src[:, k:k + S], scalar=col(C_CONVW + m * TAPS + k),
                                             in1=acc, op0=ALU.mult, op1=ALU.add).then_inc(cv_tap, 1)

            def join(m):
                acc = cv[:, (m + CB) % (CB + 1), LEFT:LEFT + S]
                dve.wait_ge(cv_tap, (m + 1) * (TAPS - 2))
                dve.tensor_tensor(acc, acc, tG[:, 2:2 + S], ALU.add).then_inc(cv_done, 1)

            dve.wait_ge(st_rb, 1)
            dve.wait_ge(cv_pad, 1)
            for m in range(CB):
                dve.wait_ge(w_used, 2 * m + 1)
                if m:
                    dve.wait_ge(glu, m)
                dve.tensor_tensor(tC[:], PS[0][:], rstdB[:], ALU.mult).then_inc(lin_out, 1)
                split(2 * m + 2, SA, 0)
                if m == 1:
                    taps(0, 2, 8)
                if m == 2:
                    taps(0, 14, 20)
                if m == 3:
                    taps(0, 26, 29)
                dve.wait_ge(w_used, 2 * m + 2)
                dve.tensor_tensor(tU[:], PS[1][:], rstdB[:], ALU.mult).then_inc(gate_out, 1)
                split(2 * m + 3, SB, 1)
                dve.wait_ge(sig, m + 1)
                dve.wait_ge(lin_out, m + 1)
                dve.tensor_tensor(cv[:, m, LEFT:LEFT + S], tC[:], tU[:], ALU.mult).then_inc(glu, 1)
                if m == 0:
                    dve.wait_ge(pos_rows, 1)
                    dve.wait_ge(pos_in, 32)
                    for b in range(GB):
                        g = b // 2
                        dve.scalar_tensor_tensor(out=sBt[:, b, :], in0=PS[3][:, g * P:(g + 1) * P], scalar=col(C_GB + b),
                                                 in1=sbsp[:, g * P:(g + 1) * P], op0=ALU.mult, op1=ALU.add).then_inc(pos_bias, 1)
                if m == 1:
                    taps(0, 8, 14)
                if m == 2:
                    taps(0, 20, 26)
                if m == 3:
                    taps(0, 29, 31)
                    join(0)
            plan = [[(1, 2, 8)], [(1, 8, 14)], [(1, 14, 20)], [(1, 20, 26)], [(1, 26, 31), (1, 0, 0)],
                    [(2, 2, 6)], [(2, 6, 11)], [(2, 11, 16)], [(2, 16, 21)], [(2, 21, 26)], [(2, 26, 31), (2, 0, 0)], []]
            for q in range(12):
                t = T_QKV + 2 + q
                if q in (4, 8):
                    c = q // 4 - 1
                    for j in range(4):
                        dve.wait_ge(qk_sq, 4 * c + j + 1)
                        dve.tensor_reduce(ssq[:, (4 * c + j) * 16:(4 * c + j + 1) * 16],
                                          (tC, tU)[j % 2][:].rearrange("p (g d) -> p g d", d=HD), AX.X, ALU.add).then_inc(qk_sum, 1)
                split(t, (t - T_QKV) % 4, t % 2)
                for m, k0, k1 in plan[q]:
                    if k1:
                        taps(m, k0, k1)
                    else:
                        join(m)
            dve.wait_ge(qk_root, 1)
            dve.reciprocal(rqk[:], rqk[:]).then_inc(qk_rinv, 1)

            dve.wait_ge(tok_free, 8 + 24)
            dve.wait_ge(qg_ready, 1)

            def q_low(p):
                dve.wait_ge(qt_hi, 3 * p + 1)
                dve.scalar_tensor_tensor(out=qtl[:], in0=PS[0][:], scalar=qgs[:, 0:1], in1=qth[:].bitcast(F32),
                                         op0=ALU.mult, op1=ALU.subtract).then_inc(qt_lo, 1)

            def k_low(p):
                dve.wait_ge(qt_hi, 3 * p + 2)
                dve.scalar_tensor_tensor(out=ktl[:], in0=PS[1][:], scalar=col(C_KG), in1=kth[:].bitcast(F32),
                                         op0=ALU.mult, op1=ALU.subtract).then_inc(qt_lo, 1)

            def v_low(p):
                dve.wait_ge(qt_hi, 3 * p + 3)
                dve.tensor_tensor(vl[:], vraw[:, :, bass.ts(p, P)], vh[:].bitcast(F32), ALU.subtract).then_inc(qt_lo, 1)

            def maxima(p, u):
                w = unit(u)[2]
                dve.wait_ge(sc_done, 16 * p + (u + 1))
                if u in (0, 8):
                    dve.wait_ge(bias_ok, 4 * p + (2 + u // 4))
                if u >= 3:
                    dve.wait_ge(pt_done, 16 * p + (u - 2))
                dve.sem_inc(sc_seen, 1)
                n = w if w <= HALF else w // 2
                dve.tensor_tensor_reduce(prob[:, u % 3, 0:w].rearrange("p (a n) -> p a n", n=n),
                                         PS[u % 2][:].rearrange("p (a n) -> p a n", a=2)[:, 0:w // n, 0:n],
                                         bias[:, u // TB, BANDW - w:BANDW].rearrange("p (a n) -> p a n", n=n), -1.0, 3e38, ALU.add, ALU.min, negmax[:, u % 3:u % 3 + 1]).then_inc(sc_max, 1)

            def divide(p, u):
                dve.wait_ge(exp_done, 16 * p + (u + 1))
                if u:
                    dve.wait_ge(p_norm, 16 * p + u)
                dve.reciprocal(rinv[:, u % 3:u % 3 + 1], rsum[:, u % 3:u % 3 + 1]).then_inc(p_inv, 1)
                w = unit(u)[2]
                dve.wait_ge(p_inv, 16 * p + (u + 1))
                dve.tensor_scalar(prob[:, u % 3, 0:w], prob[:, u % 3, 0:w], rinv[:, u % 3:u % 3 + 1], None, ALU.mult).then_inc(p_norm, 1)

            def p_low(p, u):
                w = unit(u)[2]
                dve.wait_ge(pt_hi, 16 * p + (u + 1))
                dve.tensor_tensor(ptr[u % 2][:, 0:w // P, 1, :], PS[2][:, 0:w].rearrange("p (b n) -> p b n", n=P),
                                  ptr[u % 2][:, 0:w // P, 0, :].bitcast(F32), ALU.subtract).then_inc(pt_lo, 1)

            def o_add(p, j):
                rows, toks, cols = outputs(j)
                dve.wait_ge(o_cross, 8 * p + (j + 1))
                both = osum[rows, j % 2, :].rearrange("p (u n) -> p u n", u=2)
                dve.tensor_tensor(both, cols[:, 0], both, ALU.add).then_inc(o_sum, 1)

            def o_low(p, j):
                rows, toks, cols = outputs(j)
                dve.wait_ge(o_hi, 8 * p + (j + 1))
                dve.tensor_tensor(hl[rows, bass.ds(p + 4, 1), toks].rearrange("p a n -> p (a n)"), osum[rows, j % 2, :],
                                  hh[rows, bass.ds(p + 4, 1), toks].rearrange("p a n -> p (a n)").bitcast(F32),
                                  ALU.subtract).then_inc(o_lo, 1)

            dve.wait_ge(cv_first, 2 * CB)

            def late_tap(n):
                dve.wait_ge(cv_tap, n + (CB - 1) * (TAPS - 2))
                dve.scalar_tensor_tensor(out=tG[:, 2:2 + S], in0=cv[:, CB - 1, 2 + n:2 + n + S],
                                         scalar=col(C_CONVW + (CB - 1) * TAPS + 2 + n),
                                         in1=tG[:, 2:2 + S], op0=ALU.mult, op1=ALU.add).then_inc(cv_tap, 1)

            def pair(p, last=False):
                for s in range(16):
                    if s:
                        maxima(p, s)
                    if s >= 1:
                        divide(p, s - 1)
                    if s >= 2:
                        p_low(p, s - 2)
                    if s == 2:
                        v_low(p)
                    if s >= 6 and s % 2 == 0:
                        o_low(p, s // 2 - 3)
                    if s >= 5 and s % 2 == 1:
                        o_add(p, s // 2 - 2)
                    if last and s in (5, 7, 9, 11):
                        late_tap((s - 5) // 2)
                divide(p, 15)
                if not last:
                    q_low(p + 1)
                p_low(p, 14)
                o_low(p, 5)
                if not last:
                    k_low(p + 1)
                o_add(p, 6)
                p_low(p, 15)
                o_low(p, 6)
                if not last:
                    maxima(p + 1, 0)
                o_add(p, 7)
                o_low(p, 7)

            q_low(0)
            k_low(0)
            maxima(0, 0)
            with dve.Fori(0, NPAIR - 1) as p:
                pair(p)
            pair(NPAIR - 1, last=True)

            def conv_out(m):
                return cv[:, (m + CB) % (CB + 1), LEFT:LEFT + S]

            def add_x(n, last_used=None):
                if n % 2:
                    dve.wait_ge(w_used, T_OUT + n // 2 + 1)
                else:
                    dve.wait_ge(m_done, n // 2 + 1)
                m = n % KB
                dve.wait_ge(x_in[m], 32)
                if n >= KB:
                    dve.wait_ge(x_add, n - KB + 1)
                dve.tensor_tensor(x[:, m, :], x[:, m, :], PS[n % 2][:], ALU.add).then_inc(x_add, 1)

            dve.wait_ge(ln_mean, 1)
            for m in range(CB):
                dve.scalar_tensor_tensor(out=conv_out(m), in0=PS[2][:], scalar=-1.0 / CONVW, in1=conv_out(m),
                                         op0=ALU.mult, op1=ALU.add).then_inc(ln_cent, 1)
            add_x(0)
            add_x(1)
            split(T_OUT + 2, SA, 0)
            dve.wait_ge(cv_done, CB)
            inverse(ST_LN)
            add_x(2)
            add_x(3)
            split(T_OUT + 3, SB, 1)
            dve.wait_ge(st_rb, ST_LN + 1)
            for m in range(CB):
                dve.tensor_tensor(conv_out(m), conv_out(m), rstdB[:], ALU.mult).then_inc(ln_mul, 1)
            add_x(4)
            for m in range(CB):
                dve.wait_ge(ln_hi, m + 1)
                dve.tensor_tensor(hl[:, m, :], conv_out(m), hh[:, m, :].bitcast(F32), ALU.subtract).then_inc(ln_lo, 1)
                if m == 1:
                    add_x(5)
            split(T_OUT + 4, SA, 0)
            add_x(6)
            add_x(7)
            split(T_OUT + 5, SB, 1)
            add_x(8)
            add_x(9)
            split(T_OUT + 6, SA, 0)
            add_x(10)
            add_x(11)
            split(T_OUT + 7, SB, 1)
            split(T_FFN0, SC, 0)
            split(T_FFN0 + 1, SD, 1)
            add_x(12)
            add_x(13)
            split(T_FFN0 + 2, SA, 0)
            add_x(14)
            norm_lo(1, 4, 0)
            norm_lo(1, 5, 1)
            add_x(15)
            for pos in range(2, 8):
                norm_lo(1, NORM_ORDER[1][pos], pos)
            split(T_FFN0 + 3, SB, 1)
            inverse(ST_N1)

            def add_block(m, x0, done0, used):
                if m < KB - 1:
                    dve.wait_ge(m_done, done0 + (m + 1))
                else:
                    dve.wait_ge(w_used, used)
                dve.wait_ge(x_add, x0 + (m - 7))
                dve.tensor_tensor(x[:, m, :], x[:, m, :], PS[2 + m % 2][:], ALU.add).then_inc(x_add, 1)

            M_OUT = 8

            def ffn(f, t0, x0, done0):
                b0 = FB * f
                dve.wait_ge(st_rb, (ST_N1, ST_N3)[f] + 1)
                dw0 = C_DW + 4 * FB * f

                def gate(b, used, f0):
                    dve.wait_ge(w_used, used)
                    dve.wait_ge(g_tap0, b + b0)
                    dve.tensor_tensor(tG[:, 2:2 + S], PS[0][:], rstdB[:], ALU.mult).then_inc(g_out, 1)
                    dw = par[:, bass.ds(f0, 4)]
                    dve.wait_ge(g_tap2, b + (b0 + 1))
                    dve.scalar_tensor_tensor(out=tC[:], in0=tG[:, 1:1 + S], scalar=dw[:, 1:2], in1=tC[:],
                                             op0=ALU.mult, op1=ALU.add).then_inc(g_tap1, 1)
                    dve.wait_ge(g_tap1, b + (b0 + 1))
                    dve.scalar_tensor_tensor(out=tC[:], in0=tG[:, 0:S], scalar=dw[:, 0:1], in1=tC[:],
                                             op0=ALU.mult, op1=ALU.add).then_inc(g_tap0, 1)

                def up(b, used):
                    dve.wait_ge(w_used, used)
                    dve.wait_ge(hid_lo, b + b0)
                    dve.tensor_tensor(tU[:], PS[1][:], rstdB[:], ALU.mult).then_inc(up_out, 1)
                    dve.wait_ge(up_out, b + (b0 + 1))
                    dve.wait_ge(g_silu, b + (b0 + 1))
                    dve.tensor_tensor(tU[:], tU[:], tC[:], ALU.mult).then_inc(hid, 1)

                def low(b, slot):
                    dve.wait_ge(hid_hi, b + (b0 + 1))
                    dve.tensor_tensor(hidl[:, slot, :], tU[:], hidh[:, slot, :].bitcast(F32), ALU.subtract).then_inc(hid_lo, 1)

                gate(0, t0 + 1, dw0)
                up(0, t0 + 2)
                low(0, 0)
                gate(1, t0 + 3, dw0 + 4)
                split(t0 + 4, SA, 0)
                up(1, t0 + 4)
                split(t0 + 5, SB, 1)
                low(1, 1)

                def group(i, odd):
                    t = 6 * i + (t0 - 2)
                    xg, dg = 8 * i + (x0 - 8), 7 * i + (done0 - 7)
                    split(t + 2, SA, 0)
                    gate(2 * i, t + 1, 8 * i + dw0)
                    split(t + 3, SB, 1)
                    up(2 * i, t + 2)
                    low(2 * i, 2 * odd)
                    split(t + 4, SC, 0)
                    split(t + 5, SD, 1)
                    gate(2 * i + 1, t + 3, 8 * i + (dw0 + 4))
                    split(t + 6, SA, 0)
                    up(2 * i + 1, t + 4)
                    split(t + 7, SB, 1)
                    add_block(0, xg, dg, None)
                    low(2 * i + 1, 2 * odd + 1)
                    for m in range(1, KB):
                        add_block(m, xg, dg, t + 6)

                with dve.Fori(0, FG // 2) as ii:
                    group(2 * ii + 1, 1)
                    group(2 * ii + 2, 0)

            def last_group(n, x0, done0, used, tail):
                for m in range(KB):
                    add_block(m, x0, done0, used)
                    if n is not None and m:
                        norm_lo(n, m - 1, m - 1)
                if n is not None:
                    norm_lo(n, KB - 1, KB - 1)
                for t, slot in tail:
                    split(t, slot, t % 2)

            ffn(0, T_FFN0, X_OUT, M_OUT)
            M_FFN0 = M_OUT + 7 * FG
            split(T_GMLP, SC, 0)
            split(T_GMLP + 1, SD, 1)
            last_group(2, X_FFN0 - 8, M_FFN0 - 7, T_GMLP, ((T_V, SA), (T_V + 1, SB)))
            dve.wait_ge(g_tap0, FB)
            inverse(ST_N2)
            dve.wait_ge(wsp_hi, 1)
            dve.tensor_tensor(wspl[:], wspr[:], wsph[:].bitcast(F32), ALU.subtract).then_inc(wsp_lo, 1)
            dve.wait_ge(st_rb, ST_N2 + 1)
            for j in range(2):
                dve.wait_ge(w_used, T_GMLP + 1 + j)
                dve.tensor_tensor(uearly[:, j, :], PS[j][:], rstdB[:], ALU.mult).then_inc(u_out, 1)
            with dve.Fori(0, 4) as c:
                for q in range(4):
                    split(4 * c + (T_V + 2 + q), (2 + q) % 4, q % 2)
                for pos, tok in enumerate(SWEEP):
                    dve.wait_ge(v_gelu, 8 * c + (pos + 1))
                    dve.bn_stats(vstat[:, tok, bass.ds(c, 1), :].rearrange("p a n -> p (a n)"), vst[:, pos, :]).then_inc(v_stat, 1)
            dve.wait_ge(v_stat, 32)
            for t in range(TB):
                mm = dve.bn_aggr(mv[:, 2 * t:2 * t + 2], vstat[:, t, :, :].rearrange("p a n -> p (a n)"))
            mm.then_inc(v_mv, 1)
            dve.wait_ge(v_root, 1)
            dve.reciprocal(rcol[:], root[:]).then_inc(v_rs, 1)
            dve.wait_ge(v_rs, 1)

            def vn_full(b, j, ih):
                dve.wait_ge(v_in[j], ih * 16 + 16)
                for t in range(TB):
                    part = vblk[j][:, t * P:(t + 1) * P]
                    ts = dve.tensor_scalar(part, part, mv[:, 2 * t:2 * t + 1],
                                           rcol[:, t:t + 1], ALU.subtract, ALU.mult)
                ts.then_inc(vn_f, 1)

            def vn_low(b, j):
                dve.wait_ge(vn_f, b + 1)
                dve.wait_ge(vn_hi, b + 1)
                dve.tensor_tensor(vnl[:], vblk[j], vnh[:].bitcast(F32), ALU.subtract).then_inc(vn_lo, 1)

            def mixed(b, j, ih):
                dve.wait_ge(sv_done, b + 1)
                dve.wait_ge(b_in[j], ih * 16 + 16)
                dve.wait_ge(y_lo, b)
                dve.scalar_tensor_tensor(out=tC[:].rearrange("p (c t) -> p c t", c=TB),
                                         in0=PS[2 + j][:].rearrange("p (c t) -> p c t", c=TB), scalar=par[:, bass.ds(b + C_GG, 1)],
                                         in1=bblk[:, j * P:(j + 1) * P].unsqueeze(1).broadcast_to([P, TB, P]),
                                         op0=ALU.mult, op1=ALU.add).then_inc(sv_out, 1)

            def y_full(b, u):
                dve.wait_ge(sv_out, b + 1)
                dve.wait_ge(u_gelu, b + 1)
                dve.tensor_tensor(tC[:], tC[:], u, ALU.mult).then_inc(y_f, 1)

            def y_low(b, slot):
                dve.wait_ge(y_hi, b + 1)
                dve.tensor_tensor(hidl[:, slot, :], tC[:], hidh[:, slot, :].bitcast(F32), ALU.subtract).then_inc(y_lo, 1)

            for q in range(TB):
                dve.wait_ge(v_out[q], 16 * 4)
            vn_full(0, 0, 0)
            vn_low(0, 0)
            split(T_GLOOP + 2, SC, 0)
            split(T_GLOOP + 3, SD, 1)
            for b in range(2):
                vn_full(b + 1, (b + 1) % 2, (b + 1) // 2)
                mixed(b, b, 0)
                vn_low(b + 1, (b + 1) % 2)
                y_full(b, uearly[:, b, :])
                y_low(b, b)
            vn_full(3, 1, 1)

            def u_scale(b, j, t):
                dve.wait_ge(w_used, t + 1)
                dve.wait_ge(y_f, b)
                dve.tensor_tensor(tU[:], PS[j][:], rstdB[:], ALU.mult).then_inc(u_out, 1)

            def group_rest(i, odd):
                t = 4 * i + (T_GLOOP - 4)
                xg, dg = 8 * i + (X_FFN0 - 8), 7 * i + (M_FFN0 - 7)
                u_scale(2 * i, 0, t)
                mixed(2 * i, 0, i)
                vn_low(2 * i + 1, 1)
                y_full(2 * i, tU[:])
                y_low(2 * i, 2 * odd)
                split(t + 4, SA, 0)
                u_scale(2 * i + 1, 1, t + 1)
                mixed(2 * i + 1, 1, i)
                y_full(2 * i + 1, tU[:])
                add_block(0, xg, dg, None)
                y_low(2 * i + 1, 2 * odd + 1)
                add_block(1, xg, dg, None)
                split(t + 5, SB, 1)
                for m in range(2, KB):
                    add_block(m, xg, dg, t + 4)

            def gmlp_group(i, odd):
                t = 4 * i + (T_GLOOP - 4)
                split(t + 2, SC, 0)
                split(t + 3, SD, 1)
                vn_full(2 * i, 0, i)
                vn_low(2 * i, 0)
                vn_full(2 * i + 1, 1, i)
                group_rest(i, odd)

            group_rest(1, 1)
            with dve.Fori(0, (GG - 2) // 2) as ii:
                gmlp_group(2 * ii + 2, 0)
                gmlp_group(2 * ii + 3, 1)
            M_GMLP = M_FFN0 + 7 * GG
            split(T_FFN1, SC, 0)
            split(T_FFN1 + 1, SD, 1)
            last_group(3, X_GMLP - 8, M_GMLP - 7, T_FFN1, ((T_FFN1 + 2, SA), (T_FFN1 + 3, SB)))
            inverse(ST_N3)
            ffn(1, T_FFN1, X_GMLP, M_GMLP)
            last_group(None, X_GMLP + 8 * (FG - 1), M_GMLP + 7 * (FG - 1), NT, ())


def lay_out(inputs):
    f = {k: np.asarray(v) for k, v in inputs.items()}

    def columns(a):
        return np.moveaxis(a.reshape(a.shape[:-1] + (-1, P)), -1, 0).reshape(P, -1)

    def feature_tiles(w):
        return w.reshape(KB, P, -1, P).transpose(2, 1, 0, 3).reshape(-1, P, 1024)

    def token_tiles(w):
        return w.reshape(4, 2, P, -1, HALF).transpose(3, 0, 2, 1, 4).reshape(-1, P, 1024)

    def half_tiles(w):
        return w.reshape(4, P, 4, 256).transpose(2, 1, 0, 3).reshape(4, P, 1024)

    def interleave(*tiles):
        return np.stack(tiles, 1).reshape(-1, P, 1024)

    def pipelined(ups, downs):
        parts = [ups[0]]
        for i in range(1, len(ups)):
            parts += [ups[i], downs[i - 1]]
        return parts + [downs[-1]]

    w_in = f["w_in_e"][0]
    glu = interleave(feature_tiles(w_in[:, 0:CONVW]), feature_tiles(w_in[:, CONVW:2 * CONVW]))
    stream = [glu, token_tiles(w_in[:, 2 * CONVW:]),
              half_tiles(f["w_out_e"][0][CONVW:]), half_tiles(f["w_out_e"][0][:CONVW])]

    def ffn(layer):
        gu = interleave(feature_tiles(f["w_gate"][layer]), feature_tiles(f["w_up"][layer])).reshape(FG, 4, P, 1024)
        return pipelined(gu, f["w_down"][layer].reshape(FG, 2, P, 1024))

    w_io = f["w_in_o"][0]
    u = feature_tiles(w_io[:, 0:2048]).reshape(GG, 2, P, 1024)
    gm = pipelined(u, f["w_out_o"][0].reshape(GG, 2, P, 1024))
    stream += ffn(0) + [gm[0], token_tiles(w_io[:, 2048:])] + gm[1:] + ffn(1)
    dw = np.concatenate([f["ffn_dw_w"], f["ffn_dw_b"][:, None, :]], 1).transpose(0, 2, 1)
    dw = dw.reshape(2, FB, P, 4).transpose(2, 0, 1, 3).reshape(P, -1)
    cw = f["conv_w"][0].reshape(TAPS, CB, P).transpose(2, 1, 0).reshape(P, -1)
    params = np.concatenate([
        columns(f["mix_norm_g"]), columns(f["ffn_norm_g"]), cw, columns(f["conv_b"][0]), columns(f["conv_ln_g"][0]),
        columns(f["conv_ln_b"][0]), np.tile(f["qn_g"][0], 2)[:, None], np.tile(f["kn_g"][0], 2)[:, None],
        columns(f["gate_ln_g"][0]), columns(f["gate_ln_b"][0]), dw], 1)
    c = np.ascontiguousarray
    return {
        "xT": c(f["x"][0].T),
        "wstream": np.concatenate(stream, 0),
        "params": c(params),
        "rel": c(f["rel_bias"][0][:, ::-1]),
        "wsp": c(f["w_sp"][0].transpose(2, 0, 1).reshape(P, -1)),
        "bsp": c(f["b_sp"][0].reshape(1, -1)[0]),
    }


def kernel(**inputs):
    import concourse.bacc as bacc
    from concourse.bass_utils import run_bass_kernel_spmd

    arrays = lay_out(inputs)
    nc = bacc.Bacc("TRN2", target_bir_lowering=False, num_devices=1)
    args = {k: nc.dram_tensor(k, a.shape, mybir.dt.from_np(a.dtype), kind="ExternalInput").ap() for k, a in arrays.items()}
    outT = nc.dram_tensor("outT", [D, S], F32, kind="ExternalOutput").ap()
    program(nc, **args, outT=outT)
    r = run_bass_kernel_spmd(nc, [arrays], core_ids=[0])
    return np.ascontiguousarray(r.results[0]["outT"].T)[None]
```
